# Optimizing a Trainium2 kernel written in Bass

```python
import math
import jax, jax.numpy as jnp
from jax import lax
import numpy as np

D_MODEL = 1024
BATCH = 1
SEQ = 1024
DEPTH = 2
DEC_BATCH = 8
DEC_SEQ = 16
PAST_LEN = 512

CHUNK = 64
EPS = 1e-6
N_AB = (DEPTH + 1) // 2
N_C = DEPTH // 2
DN_HEADS = 8
DN_DK = 64
DN_DV = 64
CONV_W = 4
DN_QKV = DN_HEADS * (2 * DN_DK + DN_DV)
GLA_HEADS = 8
GLA_DK = 32
GLA_DV = 64
GLA_RANK = 16
GLA_NORMALIZER = 16.0
AB_SIZES = (DN_HEADS * DN_DK, DN_HEADS * DN_DK, DN_HEADS * DN_DV,
            DN_HEADS, DN_HEADS, DN_HEADS * DN_DV,
            GLA_HEADS * GLA_DK, GLA_HEADS * GLA_DK, GLA_HEADS * GLA_DV,
            GLA_RANK, GLA_HEADS * GLA_DV)
AB_IN = sum(AB_SIZES)
AB_MIX = DN_HEADS * DN_DV + GLA_HEADS * GLA_DV
C_HEADS = 16
C_HD = 64
C_BAND_CHUNKS = 8
C_PAST = C_BAND_CHUNKS * CHUNK
C_BAND = C_PAST + CHUNK
MAX_REL = 128
D_FF = ((8 * D_MODEL // 3 + 255) // 256) * 256

kernel_name = 'hybrid_streaming_gdn_gla_chunkattn_step'

def _rmsnorm(x, g):
    xf = x.astype(jnp.float32)
    y = xf * lax.rsqrt(jnp.mean(xf * xf, axis=-1, keepdims=True) + EPS)
    return (y * g.astype(jnp.float32)).astype(x.dtype)

def _l2norm(x):
    return x * lax.rsqrt(jnp.sum(x * x, axis=-1, keepdims=True) + EPS)

def _split(x, sizes):
    return jnp.split(x, [int(s) for s in np.cumsum(sizes)[:-1]], axis=-1)

def _causal_conv(x, buf, w):
    L = x.shape[1]
    xp = jnp.concatenate([buf.astype(x.dtype), x], axis=1)
    y = xp[:, 0:L] * w[0]
    for i in range(1, CONV_W):
        y = y + xp[:, i:i + L] * w[i]
    return jax.nn.silu(y), xp[:, L:]

def _chunks(x, c):
    b, l, h = x.shape[:3]
    x = x.reshape((b, l // c, c, h) + tuple(x.shape[3:]))
    return jnp.moveaxis(x, (1, 3), (0, 2))

def _unchunks(o):
    n, b, h, c, d = o.shape
    return jnp.moveaxis(o, (0, 2), (1, 3)).reshape(b, n * c, h, d)

def _gated_delta(q, k, v, g, beta, s0):
    L = q.shape[1]
    c = min(CHUNK, L)
    causal = jnp.tril(jnp.ones((c, c), dtype=bool))
    strict = jnp.tril(jnp.ones((c, c), dtype=bool), -1)
    eye = jnp.eye(c, dtype=jnp.float32)

    def step(s, inp):
        qc, kc, vc, gc, bc = inp
        gcum = jnp.cumsum(gc, axis=-1)
        decay = jnp.exp(jnp.where(causal, gcum[..., :, None] - gcum[..., None, :], -jnp.inf))
        kb = kc * bc[..., None]
        a = jnp.where(strict, jnp.einsum('bhid,bhjd->bhij', kb, kc) * decay, 0.0)
        rhs = jnp.concatenate([vc * bc[..., None], kb * jnp.exp(gcum)[..., None]], axis=-1)
        sol = lax.linalg.triangular_solve(eye + a, rhs, left_side=True, lower=True)
        dv = vc.shape[-1]
        u, wk = sol[..., :dv], sol[..., dv:]
        v_new = u - jnp.einsum('bhcd,bhde->bhce', wk, s)
        o = (jnp.einsum('bhcd,bhde->bhce', qc * jnp.exp(gcum)[..., None], s)
             + jnp.einsum('bhij,bhje->bhie', jnp.einsum('bhid,bhjd->bhij', qc, kc) * decay, v_new))
        glast = gcum[..., -1:]
        s = (s * jnp.exp(glast)[..., None]
             + jnp.einsum('bhcd,bhce->bhde', kc * jnp.exp(glast - gcum)[..., None], v_new))
        return s, o

    xs = (_chunks(q, c), _chunks(k, c), _chunks(v, c), _chunks(g, c), _chunks(beta, c))
    s, o = lax.scan(step, s0.astype(jnp.float32), xs)
    return _unchunks(o), s

def _gla(q, k, v, gk, s0):
    L = q.shape[1]
    c = min(CHUNK, L)
    causal = jnp.tril(jnp.ones((c, c), dtype=bool))

    def step(s, inp):
        qc, kc, vc, gc = inp
        b = jnp.cumsum(gc, axis=2)
        o_inter = jnp.einsum('bhcd,bhde->bhce', qc * jnp.exp(b), s)
        diff = b[:, :, :, None, :] - b[:, :, None, :, :]
        decay = jnp.exp(jnp.where(causal[:, :, None], diff, -jnp.inf))
        a = jnp.einsum('bhid,bhjd,bhijd->bhij', qc, kc, decay)
        o = o_inter + jnp.einsum('bhij,bhje->bhie', a, vc)
        blast = b[:, :, -1:, :]
        s = (s * jnp.exp(blast[:, :, 0, :])[..., None]
             + jnp.einsum('bhcd,bhce->bhde', kc * jnp.exp(blast - b), vc))
        return s, o

    xs = (_chunks(q, c), _chunks(k, c), _chunks(v, c), _chunks(gk, c))
    s, o = lax.scan(step, s0.astype(jnp.float32), xs)
    return _unchunks(o), s

def _ab_mixer(h, conv_buf, dn_s0, gla_s0, w_in, conv_w, a_log, dt_bias, dn_onorm,
              gk_w2, gk_b, gla_onorm, w_out):
    B, L, _ = h.shape
    f32 = jnp.float32
    proj = h @ w_in
    qkv_raw, dn_a, dn_b, dn_gate, gla_q, gla_k, gla_v, gla_lr, gla_gate = _split(
        proj, (DN_QKV,) + AB_SIZES[3:])
    qkv, conv_new = _causal_conv(qkv_raw, conv_buf, conv_w)
    dq, dk, dv = _split(qkv, (DN_HEADS * DN_DK, DN_HEADS * DN_DK, DN_HEADS * DN_DV))
    q = _l2norm(dq.reshape(B, L, DN_HEADS, DN_DK).astype(f32)) * (DN_DK ** -0.5)
    k = _l2norm(dk.reshape(B, L, DN_HEADS, DN_DK).astype(f32))
    v = dv.reshape(B, L, DN_HEADS, DN_DV).astype(f32)
    beta = jax.nn.sigmoid(dn_b.astype(f32))
    g = -jnp.exp(a_log.astype(f32)) * jax.nn.softplus(dn_a.astype(f32) + dt_bias.astype(f32))
    o_dn, dn_s = _gated_delta(q, k, v, g, beta, dn_s0)
    o_dn = _rmsnorm(o_dn, dn_onorm) * jax.nn.silu(dn_gate.reshape(B, L, DN_HEADS, DN_DV).astype(f32))
    q2 = gla_q.reshape(B, L, GLA_HEADS, GLA_DK).astype(f32) * (GLA_DK ** -0.5)
    k2 = gla_k.reshape(B, L, GLA_HEADS, GLA_DK).astype(f32)
    v2 = gla_v.reshape(B, L, GLA_HEADS, GLA_DV).astype(f32)
    glog = jax.nn.log_sigmoid((gla_lr @ gk_w2 + gk_b).astype(f32)) / GLA_NORMALIZER
    glog = glog.reshape(B, L, GLA_HEADS, GLA_DK)
    o_gla, gla_s = _gla(q2, k2, v2, glog, gla_s0)
    o_gla = _rmsnorm(o_gla, gla_onorm) * jax.nn.silu(gla_gate.reshape(B, L, GLA_HEADS, GLA_DV).astype(f32))
    o = jnp.concatenate([o_dn.reshape(B, L, -1), o_gla.reshape(B, L, -1)], axis=-1).astype(h.dtype)
    return o @ w_out, conv_new, dn_s, gla_s

def _rel_bias(table, rel):
    return table[:, jnp.clip(rel, -MAX_REL, MAX_REL) + MAX_REL].astype(jnp.float32)

def _band_attn_prompt(q, k, v, table):
    B, L, H, hd = q.shape
    n = L // CHUNK
    zpad = jnp.zeros((B, C_PAST, H, hd), k.dtype)
    kp = jnp.concatenate([zpad, k], axis=1)
    vp = jnp.concatenate([zpad, v], axis=1)
    qi = jnp.arange(CHUNK)
    kj = jnp.arange(C_BAND)
    bias = _rel_bias(table, qi[:, None] + C_PAST - kj[None, :])
    qc = jnp.moveaxis(q.reshape(B, n, CHUNK, H, hd), 1, 0)

    def one(args):
        c, qb = args
        kb = lax.dynamic_slice_in_dim(kp, c * CHUNK, C_BAND, axis=1)
        vb = lax.dynamic_slice_in_dim(vp, c * CHUNK, C_BAND, axis=1)
        valid = (c * CHUNK - C_PAST + kj) >= 0
        s = jnp.einsum('bqhd,bkhd->bhqk', qb, kb).astype(jnp.float32) * (hd ** -0.5) + bias
        p = jax.nn.softmax(jnp.where(valid, s, -jnp.inf), axis=-1).astype(vb.dtype)
        return jnp.einsum('bhqk,bkhd->bqhd', p, vb)

    o = lax.map(one, (jnp.arange(n), qc))
    return jnp.moveaxis(o, 0, 1).reshape(B, L, H * hd)

def _band_attn_sample(q, k, v, k_cache, v_cache, table):
    B, L, H, hd = q.shape
    nc = k_cache.shape[1]
    kk = jnp.concatenate([k_cache.astype(k.dtype), k], axis=1)
    vv = jnp.concatenate([v_cache.astype(v.dtype), v], axis=1)
    qpos = PAST_LEN + jnp.arange(L)
    kpos = jnp.concatenate([PAST_LEN - nc + jnp.arange(nc), PAST_LEN + jnp.arange(L)])
    bias = _rel_bias(table, qpos[:, None] - kpos[None, :])
    qch = qpos // CHUNK
    kch = kpos // CHUNK
    valid = (kch[None, :] <= qch[:, None]) & (kch[None, :] >= qch[:, None] - C_BAND_CHUNKS)
    s = jnp.einsum('bqhd,bkhd->bhqk', q, kk).astype(jnp.float32) * (hd ** -0.5) + bias
    p = jax.nn.softmax(jnp.where(valid, s, -jnp.inf), axis=-1).astype(vv.dtype)
    return jnp.einsum('bhqk,bkhd->bqhd', p, vv).reshape(B, L, H * hd)

def _swiglu(h, w_gu, w_down):
    gate, up = jnp.split(h @ w_gu, 2, axis=-1)
    return (jax.nn.silu(gate) * up) @ w_down

def _trunk(x, conv0, dn0, gla0, ck, cv, w, prompt):
    B, L, _ = x.shape
    convs, dns, glas, ks, vs = [], [], [], [], []
    for layer in range(DEPTH):
        i = layer // 2
        if layer % 2 == 0:
            h = _rmsnorm(x, w['ab_norm'][i])
            y, cb, sd, sg = _ab_mixer(h, conv0[i], dn0[i], gla0[i], w['ab_w_in'][i], w['dn_conv_w'][i],
                                      w['dn_a_log'][i], w['dn_dt_bias'][i], w['dn_out_norm'][i],
                                      w['gla_gk_w2'][i], w['gla_gk_b'][i], w['gla_out_norm'][i],
                                      w['ab_w_out'][i])
            convs.append(cb)
            dns.append(sd)
            glas.append(sg)
        else:
            h = _rmsnorm(x, w['c_norm'][i])
            q, k, v = jnp.split(h @ w['c_w_qkv'][i], 3, axis=-1)
            q = q.reshape(B, L, C_HEADS, C_HD)
            k = k.reshape(B, L, C_HEADS, C_HD)
            v = v.reshape(B, L, C_HEADS, C_HD)
            if prompt:
                o = _band_attn_prompt(q, k, v, w['c_rel_bias'][i])
                rows = min(C_PAST, L)
                ks.append(k[:, L - rows:])
                vs.append(v[:, L - rows:])
            else:
                o = _band_attn_sample(q, k, v, ck[i], cv[i], w['c_rel_bias'][i])
                ks.append(k)
                vs.append(v)
            y = o.astype(x.dtype) @ w['c_w_out'][i]
        x = x + y.astype(x.dtype)
        x = x + _swiglu(_rmsnorm(x, w['ffn_norm'][layer]), w['ffn_w_gu'][layer],
                        w['ffn_w_down'][layer]).astype(x.dtype)
    y_out = _rmsnorm(x, w['final_norm'])
    dt = x.dtype
    return (y_out, jnp.stack(convs).astype(dt), jnp.stack(dns).astype(dt), jnp.stack(glas).astype(dt),
            jnp.stack(ks).astype(dt), jnp.stack(vs).astype(dt))

def setup_inputs(seed: int = 0) -> dict:
    key = jax.random.key(seed)
    ks = jax.random.split(key, 32)
    f32 = jnp.float32

    def nrm(k, shape, scale):
        return scale * jax.random.normal(k, shape, f32)

    c_rows = min(C_PAST, PAST_LEN)
    dt = jnp.exp(jax.random.uniform(ks[10], (N_AB, DN_HEADS), f32, math.log(1e-3), math.log(1e-1)))
    return {
        'x_prompt': nrm(ks[0], (BATCH, SEQ, D_MODEL), 1.0),
        'x_sample': nrm(ks[1], (DEC_BATCH, DEC_SEQ, D_MODEL), 1.0),
        'state_dn_conv': nrm(ks[2], (N_AB, DEC_BATCH, CONV_W - 1, DN_QKV), 1.0),
        'state_dn': nrm(ks[3], (N_AB, DEC_BATCH, DN_HEADS, DN_DK, DN_DV), 0.5),
        'state_gla': nrm(ks[4], (N_AB, DEC_BATCH, GLA_HEADS, GLA_DK, GLA_DV), 1.0),
        'cache_c_k': nrm(ks[5], (N_C, DEC_BATCH, c_rows, C_HEADS, C_HD), 1.0),
        'cache_c_v': nrm(ks[6], (N_C, DEC_BATCH, c_rows, C_HEADS, C_HD), 1.0),
        'ab_norm': 1.0 + nrm(ks[7], (N_AB, D_MODEL), 0.01),
        'ab_w_in': nrm(ks[8], (N_AB, D_MODEL, AB_IN), D_MODEL ** -0.5),
        'dn_conv_w': nrm(ks[9], (N_AB, CONV_W, DN_QKV), CONV_W ** -0.5),
        'dn_a_log': jnp.log(jax.random.uniform(ks[11], (N_AB, DN_HEADS), f32, 1.0, 16.0)),
        'dn_dt_bias': dt + jnp.log(-jnp.expm1(-dt)),
        'dn_out_norm': 1.0 + nrm(ks[12], (N_AB, DN_DV), 0.01),
        'gla_gk_w2': nrm(ks[13], (N_AB, GLA_RANK, GLA_HEADS * GLA_DK), GLA_RANK ** -0.5),
        'gla_gk_b': nrm(ks[14], (N_AB, GLA_HEADS * GLA_DK), 0.1),
        'gla_out_norm': 1.0 + nrm(ks[15], (N_AB, GLA_DV), 0.01),
        'ab_w_out': nrm(ks[16], (N_AB, AB_MIX, D_MODEL), AB_MIX ** -0.5),
        'c_norm': 1.0 + nrm(ks[17], (N_C, D_MODEL), 0.01),
        'c_w_qkv': nrm(ks[18], (N_C, D_MODEL, 3 * C_HEADS * C_HD), D_MODEL ** -0.5),
        'c_rel_bias': nrm(ks[19], (N_C, C_HEADS, 2 * MAX_REL + 1), 0.5),
        'c_w_out': nrm(ks[20], (N_C, C_HEADS * C_HD, D_MODEL), (C_HEADS * C_HD) ** -0.5),
        'ffn_norm': 1.0 + nrm(ks[21], (DEPTH, D_MODEL), 0.01),
        'ffn_w_gu': nrm(ks[22], (DEPTH, D_MODEL, 2 * D_FF), D_MODEL ** -0.5),
        'ffn_w_down': nrm(ks[23], (DEPTH, D_FF, D_MODEL), D_FF ** -0.5),
        'final_norm': 1.0 + nrm(ks[24], (D_MODEL,), 0.01),
    }

def reference(x_prompt, x_sample, state_dn_conv, state_dn, state_gla, cache_c_k, cache_c_v,
              ab_norm, ab_w_in, dn_conv_w, dn_a_log, dn_dt_bias, dn_out_norm, gla_gk_w2, gla_gk_b,
              gla_out_norm, ab_w_out, c_norm, c_w_qkv, c_rel_bias, c_w_out, ffn_norm, ffn_w_gu,
              ffn_w_down, final_norm):
    w = {'ab_norm': ab_norm, 'ab_w_in': ab_w_in, 'dn_conv_w': dn_conv_w, 'dn_a_log': dn_a_log,
         'dn_dt_bias': dn_dt_bias, 'dn_out_norm': dn_out_norm, 'gla_gk_w2': gla_gk_w2,
         'gla_gk_b': gla_gk_b, 'gla_out_norm': gla_out_norm, 'ab_w_out': ab_w_out, 'c_norm': c_norm,
         'c_w_qkv': c_w_qkv, 'c_rel_bias': c_rel_bias, 'c_w_out': c_w_out, 'ffn_norm': ffn_norm,
         'ffn_w_gu': ffn_w_gu, 'ffn_w_down': ffn_w_down, 'final_norm': final_norm}
    B = x_prompt.shape[0]
    conv0 = jnp.zeros((N_AB, B, CONV_W - 1, DN_QKV), x_prompt.dtype)
    dn0 = jnp.zeros((N_AB, B, DN_HEADS, DN_DK, DN_DV), jnp.float32)
    gla0 = jnp.zeros((N_AB, B, GLA_HEADS, GLA_DK, GLA_DV), jnp.float32)
    y_prompt, conv_p, dn_p, gla_p, ck_p, cv_p = _trunk(x_prompt, conv0, dn0, gla0, None, None, w, True)
    y_sample, conv_s, dn_s, gla_s, ck_s, cv_s = _trunk(x_sample, state_dn_conv, state_dn, state_gla,
                                                       cache_c_k, cache_c_v, w, False)
    return (y_prompt, y_sample, conv_p, conv_s, dn_p, dn_s, gla_p, gla_s, ck_p, ck_s, cv_p, cv_s)


_drawn_inputs = setup_inputs


def setup_inputs(seed=0):
    import zlib

    import numpy as np

    out = dict(_drawn_inputs(seed))
    spreads = {}
    factors = {'ab_norm': 3.577,
     'dn_out_norm': 29.398,
     'gla_out_norm': 27.485,
     'c_norm': 20.82,
     'ffn_norm': 5.905,
     'final_norm': 185.173,
     'cache_c_k': 8.0,
     'cache_c_v': 8.0,
     'c_rel_bias': 14.229}
    for name, (base, spread) in spreads.items():
        noise = np.random.default_rng([zlib.crc32(name.encode()), seed]).standard_normal(out[name].shape)
        drawn = base * np.exp(spread * noise) if base else spread * noise
        out[name] = __import__('jax').numpy.asarray(drawn.astype(out[name].dtype))
    for name, factor in factors.items():
        out[name] = (out[name] * factor).astype(out[name].dtype)
    return out
```

```python
from contextlib import ExitStack, contextmanager

import numpy as np

import concourse.bass as bass
from concourse import mybir

F32 = mybir.dt.float32
U8 = mybir.dt.uint8
ALU = mybir.AluOpType
ACT = mybir.ActivationFunctionType
AX_X = mybir.AxisListType.X
ds = bass.ds

P = 128
D = 1024
KT = D // P
LP, BS, LS = 1024, 8, 16
T = LP + BS * LS
NT = T // P
NPT = LP // P
G, GN = 3, T // 3
H, DK = 8, 64
GK = 32
QKV = 3 * H * DK
NCB = QKV // P
AB_IN = 3616
COL_AB = QKV
COL_GATE = COL_AB + 2 * H
COL_GQK = COL_GATE + H * DK
COL_LR = COL_GQK + 2 * H * GK + H * DK
RANK = 16
CH, HD = 16, 64
PAST = 512
FF = 2816
FC = FF // 256
EPS = 1e-6
NEG = -1e30
LEVELS = [1, 2, 4, 8, 16, 32, 64]
RL = 384
NMISC = 48


def shape_constants():
    a = np.arange(P)
    row, col = a[:, None], a[None, :]
    same = row // LS == col // LS
    f = {"ident": np.eye(P), "ones": np.ones((P, P)),
         "upto_p": row <= col, "upto_s": (row <= col) & same,
         "after_p": row > col, "after_s": (row > col) & same}
    spans = []
    for s in LEVELS:
        mid = col // (2 * s) * (2 * s) + s
        spans.append(np.where(col >= mid, (row >= mid) & (row <= col), (row > col) & (row < mid)))
    f["spans"] = np.concatenate(spans, 1)
    f["streams"] = row // LS == np.arange(BS)[None, :]
    f["stream_cols"] = np.broadcast_to((a[None, :] // LS == np.arange(BS)[:, None]).reshape(1, -1), (P, BS * P))
    f["far_mask"] = np.where((row >= 64) & (col < 64), NEG, 0.0)
    f["own_mask"] = np.where((row < 64) & (col >= 64), NEG, 0.0)
    f["new_mask"] = np.concatenate([np.where(4 * g + row // 32 == col // LS, 0.0, NEG) for g in range(2)], 1)
    u = {}
    up = [(row // (2 * s) == col // (2 * s)) & (row % (2 * s) < s) & (col % (2 * s) >= s) for s in LEVELS]
    u["up"] = np.concatenate(up + [np.eye(P) > 0], 1)
    u["low"] = np.concatenate([m.T for m in up], 1)
    where, n = {}, 0
    for k, v in f.items():
        where[k] = (n, n + v.shape[1])
        n += v.shape[1]
    m = 0
    for k, v in u.items():
        where[k] = (m, m + v.shape[1])
        m += v.shape[1]
    return (np.concatenate([v.astype(np.float32) for v in f.values()], 1),
            np.concatenate([v.astype(np.float32) for v in u.values()], 1), where)


def bc(ap, shape):
    return ap.broadcast_to(shape)


class Env:

    def __init__(self, nc, dram):
        self.nc, self.d = nc, dram
        self.top = ExitStack()
        self.scr = {}
        self.times = {}

    def apart(self, eng):
        eng.sem_inc(self.passed, 1)

    @contextmanager
    def stage(self):
        before = self.nc.snapshot_sems()
        with ExitStack() as ctx:
            yield ctx
        self.nc.clear_and_free_semaphores(self.nc.allocated_since(before))
        self.nc.all_engine_barrier()

    def own(self, name):
        n = self.times[name] = self.times.get(name, 0) + 1
        return name if n == 1 else f"{name}_{n}"

    def sb(self, ctx, name, shape, dt=F32):
        return ctx.enter_context(self.nc.sbuf_tensor(self.own(name), shape, dt))

    def sem(self, ctx, *names):
        out = [self.nc.alloc_semaphore(name=self.own(x)) for x in names]
        return out if len(out) > 1 else out[0]

    def dram(self, name, shape, kind="Internal"):
        self.scr[name] = self.nc.dram_tensor(f"{name}_dram", shape, F32, kind=kind).ap()
        return self.scr[name]



def load_x(e):
    nc, d, PS, xT, ident = e.nc, e.d, e.PS, e.xT, e.ident
    xp = d["x_prompt"].rearrange("a s d -> (a s) d")
    xs = d["x_sample"].rearrange("b s d -> (b s) d")
    with e.stage() as ctx:
        tok = e.sb(ctx, "x_tok", [P, 2, D])
        masks = e.sb(ctx, "mask_floats", [P, e.cu.shape[1]])
        gain_rows = e.sb(ctx, "gain_rows", [len(e.gain_of) * KT, P])
        gains_in, gains_turned, gains_kept, masks_kept = e.sem(ctx, "gains_in", "gains_turned", "gains_kept", "masks_kept")
        consts, in0, in1, turned, saved = e.sem(ctx, "consts_in", "x_in0", "x_in1", "x_turned", "xT_saved")
        low_out, high_out = e.sem(ctx, "x_low_out", "x_high_out")
        x_in = [in0, in1]
        block = ctx.enter_context(nc.Block())

        @block.sync
        def _(sp):
            sp.dma_start(e.cf[:], d["const_f"]).then_inc(consts, 16)
            sp.dma_start(masks[:], d["const_u"]).then_inc(consts, 16)
            for n, gain in enumerate(e.gain_of.values()):
                sp.dma_start(gain_rows[n * KT:(n + 1) * KT], gain.rearrange("(k p) -> k p", p=P)).then_inc(gains_in, 16)
            for s in range(2):
                sp.dma_start(tok[:, s], xp[s * P:(s + 1) * P]).then_inc(x_in[s], 16)
            with sp.Fori(1, NPT // 2) as i:
                for s in range(2):
                    sp.wait_ge(turned, i * 4 - 2 + 2 * s)
                    sp.dma_start(tok[:, s], xp[ds(i * 256 + s * P, P)]).then_inc(x_in[s], 16)
            sp.wait_ge(turned, 2 * NPT - 2)
            sp.dma_start(tok[:, 0], xs).then_inc(x_in[0], 16)
            sp.wait_ge(low_out, NT + 2)
            sp.wait_ge(high_out, NT + 2)
            sp.dma_start(e.scr["xT"].rearrange("(k p) t -> p k t", p=P), xT[:]).then_inc(saved, 16)
            sp.wait_ge(saved, 16)

        @block.tensor
        def _(pe):
            pe.wait_ge(consts, 32)
            pe.wait_ge(gains_in, 16 * len(e.gain_of))
            r = len(e.gain_of) * KT
            pe.transpose(PS[:, 7, 0:r], gain_rows[:], ident[0:r, 0:r]).then_inc(gains_turned, 1)

            def tile(i, s):
                t = i * 2 + s
                pe.wait_ge(x_in[s], (i + 1) * 16)
                for h, out in enumerate((low_out, high_out)):
                    pe.wait_ge(out, t + 1)
                    for k in range(4):
                        m = pe.transpose(PS[:, 2 * s + h, k * P:(k + 1) * P],
                                         tok[:, s, (h * 4 + k) * P:(h * 4 + k + 1) * P], ident)
                    m.then_inc(turned, 1)
            with pe.Fori(0, NPT // 2) as i:
                tile(i, 0)
                tile(i, 1)
            tile(NPT // 2, 0)

        def copies(eng, copy, h, out):
            eng.sem_inc(out, 2)

            def tile(i, s):
                t = i * 2 + s
                eng.wait_ge(turned, t * 2 + h + 1)
                copy(xT[:, 4 * h:4 * h + 4, ds(t * P, P)],
                     PS[:, 2 * s + h, :].rearrange("p (k t) -> p k t", k=4)).then_inc(out, 1)
            with eng.Fori(0, NPT // 2) as i:
                tile(i, 0)
                tile(i, 1)
            tile(NPT // 2, 0)

        @block.scalar
        def _(act):
            copies(act, nc.scalar.copy, 0, low_out)

        @block.vector
        def _(dve):
            dve.wait_ge(consts, 32)
            nc.vector.tensor_copy(e.cu[:], masks[:]).then_inc(masks_kept, 1)
            dve.wait_ge(gains_turned, 1)
            nc.vector.tensor_copy(e.gains[:], PS[:, 7, 0:len(e.gain_of) * KT]).then_inc(gains_kept, 1)
            copies(dve, nc.vector.tensor_copy, 1, high_out)


def rmsnorm(e, gain, dst):
    nc, PS, xT = e.nc, e.PS, e.xT
    with e.stage() as ctx:
        at = list(e.gain_of).index(gain) * KT
        g = e.gains[:, at:at + KT]
        sq = e.sb(ctx, "norm_sq", [P, 2, T])
        acc = e.sb(ctx, "norm_acc", [P, T])
        rstd = e.sb(ctx, "norm_rstd", [P, T])
        eps = e.sb(ctx, "norm_eps", [P, 1])
        eps_set, squared, added, summed, rooted, inverted, done = e.sem(
            ctx, "eps_set", "squared", "added", "summed", "rooted", "inverted", "normed")
        block = ctx.enter_context(nc.Block())
        ps = PS[:, 0:G, 0:GN]

        @block.scalar
        def _(act):
            for k in range(KT):
                if k >= 2:
                    act.wait_ge(added, k - 1)
                nc.scalar.activation(sq[:, k % 2], xT[:, k], ACT.Square).then_inc(squared, 1)
            act.wait_ge(summed, 1)
            act.wait_ge(eps_set, 1)
            nc.scalar.activation(rstd[:].rearrange("p (g n) -> p g n", g=G), ps, ACT.Sqrt,
                                 scale=1.0 / D, bias=eps[:, 0:1]).then_inc(rooted, 1)

        @block.tensor
        def _(pe):
            pe.wait_ge(added, KT)
            for j in range(G):
                m = nc.tensor.matmul(PS[:, j, 0:GN], e.ones, acc[:, j * GN:(j + 1) * GN], start=True, stop=True)
            m.then_inc(summed, 1)

        @block.vector
        def _(dve):
            nc.vector.memset(eps[:], EPS).then_inc(eps_set, 1)
            for k in range(KT):
                dve.wait_ge(squared, k + 1)
                if k == 0:
                    nc.vector.tensor_copy(acc[:], sq[:, 0]).then_inc(added, 1)
                else:
                    dve.wait_ge(added, k)
                    nc.vector.tensor_tensor(acc[:], acc[:], sq[:, k % 2], ALU.add).then_inc(added, 1)
            dve.wait_ge(rooted, 1)
            nc.vector.reciprocal(rstd[:], rstd[:]).then_inc(inverted, 1)
            dve.wait_ge(inverted, 1)
            for k in range(KT):
                nc.vector.scalar_tensor_tensor(out=dst[:, k], in0=xT[:, k], scalar=g[:, k:k + 1], in1=rstd[:],
                                               op0=ALU.mult, op1=ALU.mult).then_inc(done, 1)


def reload_x(e):
    with e.stage() as ctx:
        loaded = e.sem(ctx, "xT_loaded")
        block = ctx.enter_context(e.nc.Block())

        @block.sync
        def _(sp):
            sp.dma_start(e.xT[:], e.scr["xT"].rearrange("(k p) t -> p k t", p=P)).then_inc(loaded, 16)
            sp.wait_ge(loaded, 16)


def save_x(e):
    with e.stage() as ctx:
        saved = e.sem(ctx, "xT_saved")
        block = ctx.enter_context(e.nc.Block())

        @block.sync
        def _(sp):
            sp.dma_start(e.scr["xT"].rearrange("(k p) t -> p k t", p=P), e.xT[:]).then_inc(saved, 16)
            sp.wait_ge(saved, 16)


def product(nc, PS, banks, w, src, kts):
    last = len(kts) - 1
    for n, k in enumerate(kts):
        for j in range(G):
            m = nc.tensor.matmul(PS[:, banks + j, 0:GN], w(k), src(k, j), start=(n == 0), stop=(n == last))
    return m


def groups(ap):
    return ap.rearrange("p (g n) -> p g n", g=G)



def ffn(e, w_gu, w_down, hT):
    nc, PS, xT = e.nc, e.PS, e.xT
    wv = w_gu.rearrange("(k p) n -> p k n", p=P)
    with e.stage() as ctx:
        wg = e.sb(ctx, "w_gate", [P, KT, 256])
        wu = e.sb(ctx, "w_up", [P, KT, 256])
        wd = e.sb(ctx, "w_down", [P, 2, D])
        sg = e.sb(ctx, "silu_gate", [P, T])
        act_t = e.sb(ctx, "ffn_act", [P, 2, T])
        wg_in, wu_in, wd_in, gate_mm, up_mm, down_mm, silu_done, act_done, x_added = e.sem(
            ctx, "wg_in", "wu_in", "wd_in", "gate_mm", "up_mm", "down_mm", "silu_done", "act_done", "x_added")
        block = ctx.enter_context(nc.Block())
        A, B = 0, 3

        @block.sync
        def _(sp):
            def load(i):
                sp.dma_start(wg[:], wv[:, :, ds(i * 256, 256)]).then_inc(wg_in, 16)
                sp.dma_start(wu[:], wv[:, :, ds(i * 256 + FF, 256)]).then_inc(wu_in, 16)
                sp.dma_start(wd[:], w_down[ds(i * 256, 256)].rearrange("(k p) n -> p k n", p=P)).then_inc(wd_in, 16)
            load(0)
            with sp.Fori(1, FC) as i:
                sp.wait_ge(gate_mm, i * 2)
                sp.dma_start(wg[:], wv[:, :, ds(i * 256, 256)]).then_inc(wg_in, 16)
                sp.wait_ge(up_mm, i * 2)
                sp.dma_start(wu[:], wv[:, :, ds(i * 256 + FF, 256)]).then_inc(wu_in, 16)
                sp.wait_ge(down_mm, i * KT)
                sp.dma_start(wd[:], w_down[ds(i * 256, 256)].rearrange("(k p) n -> p k n", p=P)).then_inc(wd_in, 16)

        @block.tensor
        def _(pe):
            with pe.Fori(0, FC) as i:
                pe.wait_ge(wg_in, (i + 1) * 16)
                for f in range(2):
                    if f == 0:
                        pe.wait_ge(x_added, i * KT + 7)
                    else:
                        pe.wait_ge(silu_done, i * 2 + 1)
                    product(nc, PS, A, lambda k: wg[:, k, f * P:(f + 1) * P],
                            lambda k, j: hT[:, k, j * GN:(j + 1) * GN], range(KT)).then_inc(gate_mm, 1)
                    if f == 0:
                        pe.wait_ge(wu_in, (i + 1) * 16)
                        pe.wait_ge(x_added, i * KT + 8)
                    else:
                        pe.wait_ge(act_done, i * 2 + 1)
                    product(nc, PS, B, lambda k: wu[:, k, f * P:(f + 1) * P],
                            lambda k, j: hT[:, k, j * GN:(j + 1) * GN], range(KT)).then_inc(up_mm, 1)
                pe.wait_ge(wd_in, (i + 1) * 16)
                for n in range(KT):
                    if n == 0:
                        pe.wait_ge(act_done, i * 2 + 2)
                    elif n > 1:
                        pe.wait_ge(x_added, i * KT + 8 + n - 1)
                    product(nc, PS, (A, B)[n % 2], lambda k: wd[:, k, n * P:(n + 1) * P],
                            lambda k, j: act_t[:, k, j * GN:(j + 1) * GN], range(2)).then_inc(down_mm, 1)

        @block.scalar
        def _(act):
            with act.Fori(0, FC) as i:
                for f in range(2):
                    act.wait_ge(gate_mm, i * 2 + f + 1)
                    act.wait_ge(act_done, i * 2 + f) if f else act.wait_ge(x_added, i * KT + 8)
                    nc.scalar.activation(groups(sg[:]), PS[:, A:A + G, 0:GN], ACT.Silu).then_inc(silu_done, 1)

        @block.vector
        def _(dve):
            dve.sem_inc(x_added, 8)
            with dve.Fori(0, FC) as i:
                for f in range(2):
                    dve.wait_ge(up_mm, i * 2 + f + 1)
                    dve.wait_ge(silu_done, i * 2 + f + 1)
                    nc.vector.tensor_tensor(groups(act_t[:, f]), groups(sg[:]), PS[:, B:B + G, 0:GN],
                                            ALU.mult).then_inc(act_done, 1)
                dve.wait_ge(x_added, i * KT + 8)
                for n in range(KT):
                    dve.wait_ge(down_mm, i * KT + n + 1)
                    b = (A, B)[n % 2]
                    nc.vector.tensor_tensor(groups(xT[:, n]), groups(xT[:, n]), PS[:, b:b + G, 0:GN],
                                            ALU.add).then_inc(x_added, 1)


def project_add(e, w, src):
    nc, PS, xT = e.nc, e.PS, e.xT
    wv = w.rearrange("(k p) n -> p k n", p=P)
    with e.stage() as ctx:
        ws = e.sb(ctx, "w_slots", [P, 2, KT, P])
        in0, in1, mm, added = e.sem(ctx, "w_in0", "w_in1", "out_mm", "out_added")
        w_in = [in0, in1]
        block = ctx.enter_context(nc.Block())

        @block.sync
        def _(sp):
            for s in range(2):
                sp.dma_start(ws[:, s], wv[:, :, s * P:(s + 1) * P]).then_inc(w_in[s], 16)
            with sp.Fori(1, KT // 2) as i:
                for s in range(2):
                    sp.wait_ge(mm, i * 2 - 1 + s)
                    sp.dma_start(ws[:, s], wv[:, :, ds(i * 256 + s * P, P)]).then_inc(w_in[s], 16)

        @block.tensor
        def _(pe):
            with pe.Fori(0, KT // 2) as i:
                for s in range(2):
                    pe.wait_ge(w_in[s], (i + 1) * 16)
                    pe.wait_ge(added, i * 2 + s + 1)
                    product(nc, PS, 3 * s, lambda k: ws[:, s, k], lambda k, j: src[:, k, j * GN:(j + 1) * GN],
                            range(KT)).then_inc(mm, 1)

        @block.vector
        def _(dve):
            dve.sem_inc(added, 2)
            with dve.Fori(0, KT // 2) as i:
                for s in range(2):
                    dve.wait_ge(mm, i * 2 + s + 1)
                    x = xT[:, ds(i * 2 + s, 1)].rearrange("p o (g n) -> p (o g) n", g=G)
                    nc.vector.tensor_tensor(x, x, PS[:, 3 * s:3 * s + G, 0:GN], ALU.add).then_inc(added, 1)


def write_y(e, yT):
    nc, d, PS, ident = e.nc, e.d, e.PS, e.ident
    yp = d["y_prompt"].rearrange("a s d -> (a s) d")
    ys = d["y_sample"].rearrange("b s d -> (b s) d")
    with e.stage() as ctx:
        stage = e.sb(ctx, "y_stage", [P, 2, P * KT])
        tok = e.sb(ctx, "y_tok", [P, 2, D])
        staged, turned, low, high, o0, o1 = e.sem(ctx, "y_staged", "y_turned", "y_low", "y_high", "y_out0", "y_out1")
        outs = [o0, o1]
        block = ctx.enter_context(nc.Block())

        def each(eng, body):
            with eng.Fori(0, NPT // 2) as i:
                body(i, 0)
                body(i, 1)
            body(NPT // 2, 0)

        @block.gpsimd
        def _(pool):
            def tile(i, s):
                t = i * 2 + s
                pool.wait_ge(turned, t * 2 + 2)
                e.apart(pool)
                nc.gpsimd.tensor_copy(stage[:, s].rearrange("p (k t) -> p k t", k=KT),
                                      yT[:, :, ds(t * P, P)]).then_inc(staged, 1)
            each(pool, tile)

        @block.tensor
        def _(pe):
            pe.sem_inc(turned, 4)

            def tile(i, s):
                t = i * 2 + s
                pe.wait_ge(staged, t + 1)
                for h, out in enumerate((low, high)):
                    pe.wait_ge(out, t + 1)
                    for k in range(4):
                        m = pe.transpose(PS[:, 2 * s + h, k * P:(k + 1) * P],
                                         stage[:, s, (h * 4 + k) * P:(h * 4 + k + 1) * P], ident)
                    m.then_inc(turned, 1)
            each(pe, tile)

        def copies(eng, copy, h, out):
            eng.sem_inc(out, 2)

            def tile(i, s):
                t = i * 2 + s
                eng.wait_ge(turned, t * 2 + h + 5)
                eng.wait_ge(outs[s], (i + 1) * 16)
                copy(tok[:, s, h * 512:(h + 1) * 512], PS[:, 2 * s + h, :]).then_inc(out, 1)
            each(eng, tile)

        @block.scalar
        def _(act):
            copies(act, nc.scalar.copy, 0, low)

        @block.vector
        def _(dve):
            copies(dve, nc.vector.tensor_copy, 1, high)

        @block.sync
        def _(sp):
            for s in range(2):
                sp.sem_inc(outs[s], 16)

            def tile(i, s):
                t = i * 2 + s
                sp.wait_ge(low, t + 3)
                sp.wait_ge(high, t + 3)
            with sp.Fori(0, NPT // 2) as i:
                for s in range(2):
                    tile(i, s)
                    sp.dma_start(yp[ds(i * 256 + s * P, P)], tok[:, s]).then_inc(outs[s], 16)
            tile(NPT // 2, 0)
            sp.dma_start(ys, tok[:, 0]).then_inc(outs[0], 16)
            sp.wait_ge(outs[0], 16 * (NPT // 2 + 2))
            sp.wait_ge(outs[1], 16 * (NPT // 2 + 1))

def conv_projection(e, hT):
    nc, d, PS, ident = e.nc, e.d, e.PS, e.ident
    wv = d["ab_w_in"][0].rearrange("(k p) n -> p k n", p=P)
    rows = e.scr["qkv"].rearrange("(t p) c -> p t c", p=P)
    W = 4
    NS = BS * (W - 1)
    with e.stage() as ctx:
        ws = e.sb(ctx, "w_conv_in", [P, 2, KT, P])
        srow = e.sb(ctx, "state_rows", [NS + W, QKV])
        taps = e.sb(ctx, "state_taps", [P, NCB, NS + W])
        raw = e.sb(ctx, "conv_raw", [P, 2, LP + W - 1])
        raws = e.sb(ctx, "conv_raw_s", [P, 2, BS, LS + W - 1])
        acc = e.sb(ctx, "conv_acc", [P, 2, T])
        sil = e.sb(ctx, "conv_silu", [P, 2, T])
        tok = e.sb(ctx, "conv_tok", [P, 2, NT, P])
        sq = e.sb(ctx, "conv_sq", [P, 2, NT * P])
        newest = e.sb(ctx, "conv_newest", [P, 2, NS + W - 1])
        newrows = e.sb(ctx, "newest_rows", [NS + W - 1, QKV])
        (state_in, state_turned, state_kept, w0, w1, mm, raw_ready, state_put, conv_step, conv_done, gathered, silu_done,
         turned, tok_ready, squared, ss_done, stored0, stored1, rows_out, new_turned, new_kept, pad) = e.sem(
            ctx, "state_in", "state_turned", "state_kept", "w_in0", "w_in1", "conv_mm", "raw_ready", "state_put",
            "conv_step", "conv_done", "gathered", "silu_done", "tok_turned", "tok_ready", "squared", "ss_done",
            "tok_stored0", "tok_stored1", "newest_out", "new_turned", "new_kept", "pad_set")
        w_in, stored = [w0, w1], [stored0, stored1]
        NP2 = NCB // 2
        block = ctx.enter_context(nc.Block())

        @block.sync
        def _(sp):
            sp.dma_start(srow[0:NS], d["state_dn_conv"][0].rearrange("b w c -> (b w) c")).then_inc(state_in, 16)
            sp.dma_start(srow[NS:NS + W], d["dn_conv_w"][0]).then_inc(state_in, 16)
            for s in range(2):
                sp.sem_inc(stored[s], 16)
            with sp.Fori(0, NP2) as i:
                for s in range(2):
                    sp.wait_ge(tok_ready, i * 6 + s * 3 + 5)
                    sp.dma_start(rows[:, :, ds(i * 256 + s * P, P)], tok[:, s]).then_inc(stored[s], 16)
            sp.wait_ge(stored[0], 16 * (NP2 + 1))
            sp.wait_ge(stored[1], 16 * (NP2 + 1))
            sp.wait_ge(new_kept, NCB)
            nw = newrows[:]
            sp.dma_start(d["conv_p"].rearrange("n b w c -> (n b w) c"), nw[0:W - 1]).then_inc(rows_out, 16)
            sp.dma_start(d["conv_s"].rearrange("n b w c -> (n b w) c"), nw[W - 1:NS + W - 1]).then_inc(rows_out, 16)
            sp.wait_ge(rows_out, 32)

        @block.gpsimd
        def _(pool):
            pool.sem_inc(squared, 2)

            def square(i, s):
                pool.wait_ge(tok_ready, i * 6 + s * 3 + 5)
                pool.wait_ge(ss_done, i * 2 + s + 1)
                e.apart(pool)
                nc.gpsimd.tensor_tensor(sq[:, s], tok[:, s].rearrange("p t c -> p (t c)"),
                                        tok[:, s].rearrange("p t c -> p (t c)"), ALU.mult).then_inc(squared, 1)
            for s in range(2):
                pool.dma_start(ws[:, s], wv[:, :, s * P:(s + 1) * P]).then_inc(w_in[s], 16)
            with pool.Fori(0, NP2 - 1) as i:
                for s in range(2):
                    pool.wait_ge(mm, i * 2 + 1 + s)
                    e.apart(pool)
                    pool.dma_start(ws[:, s], wv[:, :, ds(i * 256 + 256 + s * P, P)]).then_inc(w_in[s], 16)
                    square(i, s)
            square(NP2 - 1, 0)
            square(NP2 - 1, 1)

        @block.tensor
        def _(pe):
            pe.sem_inc(new_turned, 2)
            pe.wait_ge(state_in, 32)
            for n in range(NCB):
                m = pe.transpose(PS[:, 6, n * (NS + W):(n + 1) * (NS + W)], srow[:, n * P:(n + 1) * P],
                                 ident[0:NS + W, 0:NS + W])
            m.then_inc(state_turned, 1)

            def multiply(i, s):
                pe.wait_ge(w_in[s], (i + 1) * 16)
                pe.wait_ge(raw_ready, i * 2 + s + 1)
                product(nc, PS, 3 * s, lambda k: ws[:, s, k], lambda k, j: hT[:, k, j * GN:(j + 1) * GN],
                        range(KT)).then_inc(mm, 1)

            def turn(i, s):
                pe.wait_ge(silu_done, i * 2 + s + 3)
                for c in range(3):
                    bank = 6 + (s * 3 + c) % 2
                    pe.wait_ge(tok_ready, i * 6 + s * 3 + c + 1)
                    if c == 2:
                        pe.wait_ge(gathered, i * 2 + s + 1)
                        pe.transpose(PS[0:NS + W - 1, bank, 384:512], newest[:, s], ident).then_inc(new_turned, 1)
                    for t in range(3):
                        m = pe.transpose(PS[:, bank, t * P:(t + 1) * P], sil[:, s, (3 * c + t) * P:(3 * c + t + 1) * P],
                                         ident)
                    m.then_inc(turned, 1)

            pe.wait_ge(state_kept, 1)
            multiply(0, 0)
            with pe.Fori(0, NP2 - 1) as i:
                multiply(i, 1)
                turn(i, 0)
                multiply(i + 1, 0)
                turn(i, 1)
            multiply(NP2 - 1, 1)
            turn(NP2 - 1, 0)
            turn(NP2 - 1, 1)

        @block.scalar
        def _(act):
            act.sem_inc(raw_ready, 2)
            act.sem_inc(tok_ready, 2)
            act.sem_inc(silu_done, 2)
            act.wait_ge(state_turned, 1)
            nc.scalar.copy(taps[:], PS[:, 6, 0:NCB * (NS + W)].rearrange("p (n r) -> p n r", n=NCB)).then_inc(state_kept, 1)
            act.wait_ge(pad, 1)

            def copy_raw(i, s):
                act.wait_ge(mm, i * 2 + s + 1)
                act.wait_ge(conv_done, i * 2 + s + 1)
                b = 3 * s
                o = W - 1
                nc.scalar.copy(raw[:, s, o:o + 2 * GN].rearrange("p (g n) -> p g n", g=2), PS[:, b:b + 2, 0:GN])
                nc.scalar.copy(raw[:, s, o + 2 * GN:o + LP], PS[:, b + 2, 0:LP - 2 * GN])
                nc.scalar.copy(raws[:, s, :, o:], PS[:, b + 2, LP - 2 * GN:GN].rearrange("p (b l) -> p b l", b=BS)
                               ).then_inc(raw_ready, 1)

            def silu(i, s):
                act.wait_ge(conv_step, (i * 2 + s) * 8 + 8)
                nc.scalar.activation(sil[:, s], acc[:, s], ACT.Silu).then_inc(silu_done, 1)

            def copy_tok(i, s):
                act.wait_ge(stored[s], (i + 1) * 16)
                act.wait_ge(squared, i * 2 + s + 1)
                for c in range(3):
                    bank = 6 + (s * 3 + c) % 2
                    act.wait_ge(turned, i * 6 + s * 3 + c + 1)
                    if c == 2:
                        nc.scalar.copy(newrows[:, ds(i * 256 + s * P, P)],
                                       PS[0:NS + W - 1, bank, 384:512]).then_inc(new_kept, 1)
                    nc.scalar.copy(tok[:, s, 3 * c:3 * c + 3], PS[:, bank, 0:384].rearrange("p (t c) -> p t c", t=3)
                                   ).then_inc(tok_ready, 1)

            copy_raw(0, 0)
            with act.Fori(0, NP2 - 1) as i:
                silu(i, 0)
                copy_raw(i, 1)
                copy_tok(i, 0)
                silu(i, 1)
                copy_raw(i + 1, 0)
                copy_tok(i, 1)
            silu(NP2 - 1, 0)
            copy_raw(NP2 - 1, 1)
            copy_tok(NP2 - 1, 0)
            silu(NP2 - 1, 1)
            copy_tok(NP2 - 1, 1)

        @block.vector
        def _(dve):
            dve.sem_inc(conv_done, 2)
            dve.sem_inc(ss_done, 2)
            nc.vector.memset(raw[:, :, 0:W - 1], 0.0).then_inc(pad, 1)
            dve.wait_ge(state_kept, 1)
            dve.wait_ge(pad, 1)

            def conv(i, s):
                n = i * 2 + s
                dve.wait_ge(conv_done, n + 1)
                nc.vector.tensor_copy(raws[:, s, :, 0:W - 1],
                                      taps[:, ds(n, 1), 0:NS].rearrange("p o (b w) -> p (o b) w", b=BS)).then_inc(state_put, 1)
                dve.wait_ge(raw_ready, n + 3)
                dve.wait_ge(state_put, n + 1)
                dve.wait_ge(silu_done, n + 1)
                ap, as_ = acc[:, s, 0:LP], acc[:, s, LP:T].rearrange("p (b l) -> p b l", b=BS)
                for w in range(W):
                    c = taps[:, ds(n, 1), NS + w:NS + w + 1].rearrange("p o w -> p (o w)")
                    if w == 0:
                        nc.vector.tensor_scalar(ap, raw[:, s, 0:LP], c, None, ALU.mult).then_inc(conv_step, 1)
                        nc.vector.tensor_scalar(as_, raws[:, s, :, 0:LS], c, None, ALU.mult).then_inc(conv_step, 1)
                    else:
                        dve.wait_ge(conv_step, n * 8 + 2 * w - 1)
                        nc.vector.scalar_tensor_tensor(out=ap, in0=raw[:, s, w:w + LP], scalar=c, in1=ap,
                                                       op0=ALU.mult, op1=ALU.add).then_inc(conv_step, 1)
                        dve.wait_ge(conv_step, n * 8 + 2 * w)
                        nc.vector.scalar_tensor_tensor(out=as_, in0=raws[:, s, :, w:w + LS], scalar=c, in1=as_,
                                                       op0=ALU.mult, op1=ALU.add).then_inc(conv_step, 1)
                dve.wait_ge(new_turned, n + 1)
                nc.vector.tensor_copy(newest[:, s, 0:W - 1], raw[:, s, LP:LP + W - 1])
                nc.vector.tensor_copy(newest[:, s, W - 1:].rearrange("p (b w) -> p b w", b=BS),
                                      raws[:, s, :, LS:]).then_inc(gathered, 1)
                dve.wait_ge(gathered, n + 1)
                dve.sem_inc(conv_done, 1)

            def sums(i, s):
                n = i * 2 + s
                dve.wait_ge(squared, n + 3)
                nc.vector.reduce_sum(e.ss[:, :, ds(n * 2, 2)], sq[:, s].rearrange("p (t h c) -> p t h c", t=NT, h=2),
                                     AX_X).then_inc(ss_done, 1)

            conv(0, 0)
            with dve.Fori(0, NP2 - 1) as i:
                conv(i, 1)
                sums(i, 0)
                conv(i + 1, 0)
                sums(i, 1)
            conv(NP2 - 1, 1)
            sums(NP2 - 1, 0)
            sums(NP2 - 1, 1)


def rest_projection(e, hT):
    nc, d, PS = e.nc, e.d, e.PS
    wv = d["ab_w_in"][0].rearrange("(k p) n -> p k n", p=P)
    rows = e.scr["rest"]
    with e.stage() as ctx:
        wgt = e.sb(ctx, "w_gates", [P, KT, 512])
        wqv = e.sb(ctx, "w_gla", [P, KT, 512])
        wm = e.sb(ctx, "w_misc", [P, KT, NMISC])
        out = e.sb(ctx, "rest_rows", [P, 4, 512])
        gate_in, gla_in, misc_in, wm_zero, misc_mm, misc_kept, mm, copied, s0, s1, s2, s3 = e.sem(
            ctx, "gate_in", "gla_in", "misc_in", "misc_zero", "misc_mm", "misc_kept", "rest_mm", "rest_copied",
            "rest_out0", "rest_out1", "rest_out2", "rest_out3")
        stored = [s0, s1, s2, s3]
        block = ctx.enter_context(nc.Block())
        N = 2 * NT

        @block.gpsimd
        def _(pool):
            nc.gpsimd.memset(wm[:], 0.0).then_inc(wm_zero, 1)
            pool.wait_ge(wm_zero, 1)
            pool.dma_start(wm[:, :, 0:RANK], wv[:, :, COL_LR:COL_LR + RANK]).then_inc(misc_in, 16)
            pool.dma_start(wm[:, :, 32:48], wv[:, :, COL_AB:COL_AB + 2 * H]).then_inc(misc_in, 16)
            pool.dma_start(wgt[:], wv[:, :, COL_GATE:COL_GATE + 512]).then_inc(gate_in, 16)
            pool.dma_start(wqv[:], wv[:, :, COL_GQK:COL_GQK + 512]).then_inc(gla_in, 16)
            pool.wait_ge(mm, NT)
            pool.dma_start(wgt[:], wv[:, :, 2 * COL_GATE:2 * COL_GATE + 512]).then_inc(gate_in, 16)
            pool.wait_ge(mm, 2 * NT)
            pool.dma_start(wqv[:], wv[:, :, COL_GQK + 512:COL_GQK + 1024]).then_inc(gla_in, 16)

        @block.sync
        def _(sp):
            for s in range(4):
                sp.sem_inc(stored[s], 16)
            with sp.Fori(0, 2) as i:
                for q in range(2):
                    for t in range(NT):
                        n = q * NT + t
                        sp.wait_ge(copied, i * N + n + 4)
                        sp.dma_start(rows[t * P:(t + 1) * P, ds(i + 2 * q, 1)].rearrange("t o c -> t (o c)"),
                                       out[:, n % 2 + 2 * q]).then_inc(stored[n % 2 + 2 * q], 16)
            for s, per in enumerate((5, 4, 4, 5)):
                sp.wait_ge(stored[s], 16 * (2 * per + 1))

        @block.tensor
        def _(pe):
            pe.wait_ge(misc_in, 32)
            for k in range(KT):
                for j in range(G):
                    m = nc.tensor.matmul(PS[0:NMISC, j, 0:GN], wm[:, k], hT[:, k, j * GN:(j + 1) * GN],
                                         start=(k == 0), stop=(k == KT - 1))
            m.then_inc(misc_mm, 1)
            with pe.Fori(0, 2) as i:
                for q, (w, w_in) in enumerate(((wgt, gate_in), (wqv, gla_in))):
                    pe.wait_ge(w_in, (i + 1) * 16)
                    for t in range(NT):
                        n = q * NT + t
                        pe.wait_ge(copied, i * N + n + 1)
                        for k in range(KT):
                            m = nc.tensor.matmul(PS[:, 4 + n % 3, :], hT[:, k, t * P:(t + 1) * P], w[:, k],
                                                 start=(k == 0), stop=(k == KT - 1))
                        m.then_inc(mm, 1)

        @block.scalar
        def _(act):
            act.sem_inc(copied, 3)
            act.wait_ge(misc_mm, 1)
            nc.scalar.copy(groups(e.misc[:]), PS[0:NMISC, 0:G, 0:GN]).then_inc(misc_kept, 1)
            with act.Fori(0, 2) as i:
                for q, f in enumerate((ACT.Silu, ACT.Copy)):
                    for t in range(NT):
                        n = q * NT + t
                        act.wait_ge(mm, i * N + n + 1)
                        slot = n % 2 + 2 * q
                        per = len([m for m in range(q * NT, q * NT + NT) if m % 2 == n % 2])
                        act.wait_ge(stored[slot], i * (16 * per) + 16 * ((n - q * NT) // 2 + 1))
                        nc.scalar.activation(out[:, slot], PS[:, 4 + n % 3, :], f).then_inc(copied, 1)



def token_scalars(e):
    nc, d, PS, ident, misc = e.nc, e.d, e.PS, e.ident, e.misc
    NH, NZ = NT * H, NT * H * GK
    with e.stage() as ctx:
        w2 = e.sb(ctx, "gk_w2", [RANK, H * GK])
        gkb = e.sb(ctx, "gk_b", [1, H * GK])
        alog = e.sb(ctx, "a_log", [P, H])
        dtb = e.sb(ctx, "dt_bias", [P, H])
        eps = e.sb(ctx, "l2_eps", [P, 1])
        zt = e.sb(ctx, "z_tail", [P, NZ])
        at = e.sb(ctx, "a_tail", [P, NT, H])
        ax = e.sb(ctx, "a_biased", [P, NT, H])
        ab = e.sb(ctx, "ab_tok", [P, NT, 2 * H])
        w_in, z_mm, ab_turned, ab_kept, eps_set, rooted, z_tail, z_done, biased, a_tail, a_exp, decay, b_exp, b_one, \
            inverted, scaled, beta_done, a_soft, a_neg = e.sem(
                ctx, "gk_in", "z_mm", "ab_turned", "ab_kept", "l2_eps_set", "norm_rooted", "z_tail_step", "z_done",
                "a_is_biased", "a_tail_step", "a_log_exp", "decay_done", "b_exp", "b_plus_one", "norm_inverted",
                "norm_scaled", "beta_done", "a_softplus", "a_negated")
        block = ctx.enter_context(nc.Block())
        Z = PS[:, 0:5, :].rearrange("p b n -> p (b n)")[:, 0:NZ]

        @block.sync
        def _(sp):
            sp.dma_start(w2[:], d["gla_gk_w2"][0]).then_inc(w_in, 16)
            sp.dma_start(gkb[:], d["gla_gk_b"]).then_inc(w_in, 16)
            sp.dma_start(alog[:], d["dn_a_log"].broadcast_to((P, H))).then_inc(w_in, 16)
            sp.dma_start(dtb[:], d["dn_dt_bias"].broadcast_to((P, H))).then_inc(w_in, 16)

        @block.tensor
        def _(pe):
            for t in range(NT):
                m = pe.transpose(PS[:, 5, t * 2 * H:(t + 1) * 2 * H], misc[32:48, t * P:(t + 1) * P], ident[32:48, 32:48])
            m.then_inc(ab_turned, 1)
            pe.wait_ge(w_in, 64)
            for t in range(NT):
                o = Z[:, t * H * GK:(t + 1) * H * GK]
                nc.tensor.matmul(o, misc[0:RANK, t * P:(t + 1) * P], w2[:], start=True, stop=False)
                m = nc.tensor.matmul(o, e.ones[0:1, :], gkb[:], start=False, stop=True)
            m.then_inc(z_mm, 1)

        @block.scalar
        def _(act):
            act.wait_ge(ab_turned, 1)
            nc.scalar.copy(ab[:], PS[:, 5, 0:2 * NH].rearrange("p (t h) -> p t h", t=NT)).then_inc(ab_kept, 1)
            act.wait_ge(eps_set, 1)
            nc.scalar.activation(e.rn[:], e.ss[:, :, 0:2 * H], ACT.Sqrt, bias=eps[:, 0:1]).then_inc(rooted, 1)
            act.wait_ge(z_mm, 1)
            nc.scalar.activation(zt[:], Z, ACT.Abs).then_inc(z_tail, 1)
            act.wait_ge(biased, 1)
            nc.scalar.activation(at[:], ax[:], ACT.Abs).then_inc(a_tail, 1)
            act.wait_ge(z_tail, 1)
            nc.scalar.activation(zt[:], zt[:], ACT.Exp, scale=-1.0).then_inc(z_tail, 1)
            act.wait_ge(a_tail, 1)
            nc.scalar.activation(at[:], at[:], ACT.Exp, scale=-1.0).then_inc(a_tail, 1)
            act.wait_ge(w_in, 64)
            nc.scalar.activation(alog[:], alog[:], ACT.Exp).then_inc(a_exp, 1)
            act.wait_ge(ab_kept, 1)
            nc.scalar.activation(e.beta[:], ab[:, :, H:2 * H], ACT.Exp, scale=-1.0).then_inc(b_exp, 1)
            act.wait_ge(z_tail, 2)
            nc.scalar.activation(zt[:], zt[:], ACT.Ln, bias=1.0).then_inc(z_tail, 1)
            act.wait_ge(a_tail, 2)
            nc.scalar.activation(at[:], at[:], ACT.Ln, bias=1.0).then_inc(a_tail, 1)

        @block.vector
        def _(dve):
            nc.vector.memset(eps[:], EPS).then_inc(eps_set, 1)
            dve.wait_ge(ab_kept, 1)
            dve.wait_ge(w_in, 64)
            nc.vector.tensor_tensor(ax[:], ab[:, :, 0:H], bc(dtb[:].rearrange("p (o h) -> p o h", o=1), (P, NT, H)),
                                    ALU.add).then_inc(biased, 1)
            dve.wait_ge(rooted, 1)
            nc.vector.reciprocal(e.rn[:], e.rn[:]).then_inc(inverted, 1)
            dve.wait_ge(inverted, 1)
            nc.vector.tensor_scalar(e.rn[:, :, 0:H], e.rn[:, :, 0:H], float(DK) ** -0.5, None, ALU.mult).then_inc(scaled, 1)
            dve.wait_ge(b_exp, 1)
            nc.vector.tensor_scalar(e.beta[:], e.beta[:], 1.0, None, ALU.add).then_inc(b_one, 1)
            dve.wait_ge(b_one, 1)
            nc.vector.reciprocal(e.beta[:], e.beta[:]).then_inc(beta_done, 1)
            dve.wait_ge(beta_done, 1)
            nc.vector.tensor_tensor(e.rkb[:], e.beta[:], e.rn[:, :, H:2 * H], ALU.mult).then_inc(scaled, 1)
            dve.wait_ge(a_exp, 1)
            dve.wait_ge(a_tail, 3)
            nc.vector.scalar_tensor_tensor(out=ax[:], in0=ax[:], scalar=0.0, in1=at[:], op0=ALU.max, op1=ALU.add
                                           ).then_inc(a_soft, 1)
            dve.wait_ge(a_soft, 1)
            nc.vector.scalar_tensor_tensor(out=e.gdn[:], in0=ax[:], scalar=-1.0,
                                           in1=bc(alog[:].rearrange("p (o h) -> p o h", o=1), (P, NT, H)),
                                           op0=ALU.mult, op1=ALU.mult).then_inc(decay, 1)
            dve.wait_ge(z_tail, 3)
            nc.vector.scalar_tensor_tensor(out=e.ggla[:].rearrange("p t c -> p (t c)"), in0=Z, scalar=0.0, in1=zt[:],
                                           op0=ALU.min, op1=ALU.subtract).then_inc(z_done, 1)



class Count:

    def __init__(self, sem, per):
        self.sem, self.per = sem, per

    def wait(self, eng, t, k=None):
        eng.wait_ge(self.sem, t * self.per + (self.per if k is None else k))


def recurrences(e):
    nc, d, PS, ident, c = e.nc, e.d, e.PS, e.ident, e.const
    qkv, rest = e.scr["qkv"], e.scr["rest"]
    HE = H * DK
    NL = len(LEVELS)
    with e.stage() as ctx:
        lq = e.sb(ctx, "tile_qkv", [P, 2, QKV])
        lr = e.sb(ctx, "tile_gla", [P, 2, 2, HE])
        ug = e.sb(ctx, "upto_g", [P, H, P])
        dec = e.sb(ctx, "decay", [P, H, P])
        gwide = e.sb(ctx, "g_wide", [P, H, DK])
        gs = e.sb(ctx, "gla_g", [P, H * GK])
        qn = e.sb(ctx, "q_normed", [P, H, DK])
        kn = e.sb(ctx, "k_normed", [P, H, DK])
        kb = e.sb(ctx, "k_beta", [P, H, DK])
        kd = e.sb(ctx, "k_decayed", [P, H, DK])
        bv = e.sb(ctx, "v_beta", [P, H, DK])
        small = e.sb(ctx, "small_exps", [P, 2 * H])
        egl = e.sb(ctx, "egl", [P, H // 2, BS])
        rkd = e.sb(ctx, "rk_decayed", [P, H])
        be = e.sb(ctx, "beta_eg", [P, H])
        kde = e.sb(ctx, "gla_k_exp", [P, H * GK])
        kdg = e.sb(ctx, "gla_k_decayed", [P, H * GK])
        gqt = e.sb(ctx, "gla_qT", [P, 2, P])
        gkt = e.sb(ctx, "gla_kT", [P, 2, P])
        ex = e.sb(ctx, "gla_exps", [P, 2, NL + 1, P])
        qe = e.sb(ctx, "gla_q_exp", [P, 2, NL + 1, P])
        ke = e.sb(ctx, "gla_k_exps", [P, 2, NL, P])
        ga = e.sb(ctx, "gla_pairs", [P, H, P])
        qt = e.sb(ctx, "qT", [P, H // 2, P])
        kt = e.sb(ctx, "kT", [P, H // 2, P])
        kbt = e.sb(ctx, "kbT", [P, H // 2, P])
        bt = e.sb(ctx, "minus_aT", [P, H, P])
        pt = e.sb(ctx, "qk_pairs", [P, H, P])
        u = e.sb(ctx, "inverse_T", [P, H, P])
        tt = e.sb(ctx, "inverse", [P, H, P])
        z = e.sb(ctx, "z", [P, H, P])
        tmp = e.sb(ctx, "ks_scaled", [P, HE])
        rr = e.sb(ctx, "rhs", [P, HE])
        vn = e.sb(ctx, "v_new", [P, HE])
        tmq = e.sb(ctx, "qs_scaled", [P, HE])
        S = e.sb(ctx, "dn_state", [P, H // 2, DK])
        GS = e.sb(ctx, "gla_state", [P, 2, DK])
        Ss = e.sb(ctx, "dn_states", [P, H // 2, BS, DK])
        GSs = e.sb(ctx, "gla_states", [P, 2, BS, DK])
        mk = e.sb(ctx, "stream_masked", [P, 2, BS, P])
        vm = ug[:].rearrange("p h t -> p (h t)")[:, 0:2 * BS * DK].rearrange("p (s b v) -> p s b v", s=2, b=BS)
        Ssd, GSsd = mk[:, 0, 0:4].rearrange("p a t -> p (a t)"), mk[:, 1, 0:4].rearrange("p a t -> p (a t)")

        def count(name, per=1):
            return Count(e.sem(ctx, name), per)
        load0, load1, states_in = e.sem(ctx, "tile_in0", "tile_in1", "states_in")
        load = [load0, load1]
        end = {k: e.sem(ctx, f"end_{k}") for k in ("pe", "act", "dve", "pool")}
        cleared, state_zero, states_out, ga_zero = e.sem(ctx, "pairs_zero", "state_zero", "states_out", "pairs_rezero")
        ug_ready, scaled, gwide_ready, gs_ready = count("ug_ready"), count("scaled", 4), count("gwide_ready"), count("gla_g_ready")
        dec_sum, dec_exp, dec_masked = count("dec_sum"), count("dec_exp"), count("dec_masked")
        small_mm, small_exp, rkd_ready, kd_ready = count("small_mm"), count("small_exp"), count("rkd_ready"), count("kd_ready")
        gla_turned, gla_ready, e_mm, e_exp = count("gla_turned"), count("glaT_ready"), count("e_mm", 2), count("e_exp", 2)
        qe_ready, kdg_ready = count("qe_ready", 2), count("kdg_ready")
        turned, tready = count("qk_turned", 3), count("qkT_ready", 3)
        a_mm, p_mm, bt_ready, pt_ready = count("a_mm"), count("p_mm"), count("bt_ready"), count("pt_ready")
        u_init, u_first, t_turned, t_first = count("u_init"), count("u_first"), count("t_turned", 2), count("t_first", 2)
        z_mm, z_copied = count("z_mm", 2 * (NL - 1)), count("z_copied", 2 * (NL - 1))
        du_mm, dt_mm = count("du_mm", 2 * (NL - 1)), count("dt_mm", 2 * (NL - 2))
        u_put, t_put = count("u_put", 2 * (NL - 1)), count("t_put", 2 * (NL - 2))
        ga_mm, ga_put = count("gla_pairs_mm", NL + 1), count("gla_pairs_put", NL + 1)
        be_ready, ks_mm, qs_mm, ks_scaled, r_ready = count("be_ready"), count("ks_mm"), count("qs_mm"), count("ks_scaled"), count("r_ready")
        v_mm, v_ready, qs_scaled, o_mm = count("v_mm"), count("v_ready"), count("qs_scaled"), count("o_mm")
        go_mm, go_copied, gstate_mm, state_mm = count("go_mm"), count("go_copied"), count("gstate_mm"), count("state_mm")
        mk_ready, mk_used = e.sem(ctx, "masked_ready", "masked_used")
        vm_ready, vm_used, sd_ready, s_done = e.sem(ctx, "vm_ready", "vm_used", "sd_ready", "states_done")
        gd_ready = e.sem(ctx, "gla_sd_ready")
        block = ctx.enter_context(nc.Block())

        def levels(sample):
            return range(1, 4 if sample else NL)

        def pairs_jobs(sample):
            return list(range(4 if sample else NL)) + [NL]

        def at(h):
            return h % 2 * 4 + h // 2

        def gla_at(h):
            return h % 2 * 4 + h % 4 // 2 * 2 + h // 4

        row_done = count("row_done", 4 * (NL + 1) + 4 + 4)

        def each(eng, tile):
            with eng.Fori(0, NPT // 2) as i:
                tile(i, 0, False)
                tile(i, 1, False)
            tile(NPT // 2, 0, True)

        def start(eng, t, me):
            for k, s in end.items():
                if k != me:
                    eng.wait_ge(s, t + 2)
            e.apart(eng)

        def half(ap, g):
            return ap[:, 4 * g:4 * g + 4]

        def bank2(b):
            return PS[:, b:b + 2, :].rearrange("p b (h t) -> p (b h) t", h=4)

        def wide(ap, n):
            return bc(ap.rearrange("p (h o) -> p h o", o=1), (P, ap.shape[1], n))

        def over_heads(ap, h=H):
            return bc(ap.rearrange("p (o t) -> p o t", o=1), (P, h, P))

        def hv(ap):
            return ap.rearrange("p (h v) -> p h v", h=H)

        @block.sync
        def _(sp):
            for m in range(H // 2):
                sp.dma_start(Ss[:, m], d["state_dn"][0].rearrange("b h k v -> b (h k) v")[:, m * P:(m + 1) * P]
                             .rearrange("b p v -> p b v")).then_inc(states_in, 16)
            for m in range(2):
                sp.dma_start(GSs[:, m], d["state_gla"][0].rearrange("b h k v -> b (h k) v")[:, m * P:(m + 1) * P]
                             .rearrange("b p v -> p b v")).then_inc(states_in, 16)

            def tile(i, s, sample):
                t = i * 2 + s
                for x in end.values():
                    sp.wait_ge(x, t + 1)
                sp.dma_start(lq[:, s], qkv[ds(t * P, P)]).then_inc(load[s], 16)
                sp.dma_start(lr[:, s], rest[ds(t * P, P), 2:4]).then_inc(load[s], 16)
            each(sp, tile)
            for x in end.values():
                sp.wait_ge(x, NPT + 2)
            sp.dma_start(d["dn_p"].rearrange("n b h k v -> (n b h k) v").rearrange("(m p) v -> p m v", p=P), S[:]
                         ).then_inc(states_out, 16)
            sp.dma_start(d["gla_p"].rearrange("n b h k v -> (n b h k) v").rearrange("(m p) v -> p m v", p=P), GS[:]
                         ).then_inc(states_out, 16)
            sp.wait_ge(s_done, 6)
            for m in range(H // 2):
                sp.dma_start(d["dn_s"][0].rearrange("b h k v -> b (h k) v")[:, m * P:(m + 1) * P]
                             .rearrange("b p v -> p b v"), Ss[:, m]).then_inc(states_out, 16)
            for m in range(2):
                sp.dma_start(d["gla_s"][0].rearrange("b h k v -> b (h k) v")[:, m * P:(m + 1) * P]
                             .rearrange("b p v -> p b v"), GSs[:, m]).then_inc(states_out, 16)
            sp.wait_ge(states_out, 16 * 8)

        @block.gpsimd
        def _(pool):
            pool.sem_inc(end["pool"], 2)
            tt_ = nc.gpsimd.tensor_tensor

            def tile(i, s, sample):
                t = i * 2 + s
                start(pool, t, "pool")
                upto = c("upto_s" if sample else "upto_p")
                col = lambda ap, a=0, b=H: ap[:, ds(t, 1), a:b].rearrange("p o h -> p (o h)")
                g = col(e.gdn)
                for r in range(2):
                    k = tt_(ug[:, 4 * r:4 * r + 4], over_heads(upto, 4),
                            wide(g.rearrange("p (m r) -> p r m", r=2)[:, r], P), ALU.mult)
                k.then_inc(ug_ready.sem, 1)
                nc.gpsimd.tensor_copy(gwide[:], wide(g, DK)).then_inc(gwide_ready.sem, 1)
                nc.gpsimd.tensor_copy(gs[:], e.ggla[:, ds(t, 1)].rearrange("p o c -> p (o c)")).then_inc(gs_ready.sem, 1)
                pool.wait_ge(load[s], (i + 1) * 32)
                e.apart(pool)
                q, k, v = (hv(lq[:, s, n * HE:(n + 1) * HE]) for n in range(3))
                tt_(qn[:], q, wide(col(e.rn), DK), ALU.mult).then_inc(scaled.sem, 1)
                tt_(kn[:], k, wide(col(e.rn, H, 2 * H), DK), ALU.mult).then_inc(scaled.sem, 1)
                tt_(kb[:], k, wide(col(e.rkb), DK), ALU.mult).then_inc(scaled.sem, 1)
                dec_exp.wait(pool, t)
                e.apart(pool)
                tt_(dec[:], dec[:], over_heads(upto), ALU.mult).then_inc(dec_masked.sem, 1)
                tt_(bv[:], v, wide(col(e.beta), DK), ALU.mult).then_inc(scaled.sem, 1)
                small_exp.wait(pool, t)
                e.apart(pool)
                tt_(rkd[:], col(e.rn, H, 2 * H), small[:, H:2 * H], ALU.mult).then_inc(rkd_ready.sem, 1)
                rkd_ready.wait(pool, t)
                e.apart(pool)
                m = tt_(kd[:], k, wide(rkd[:], DK), ALU.mult)
                m.then_inc(end["pool"], 1)
            each(pool, tile)

        @block.tensor
        def _(pe):
            pe.sem_inc(end["pe"], 2)
            pe.sem_inc(mk_used, 2)
            pe.sem_inc(vm_used, 2)
            mm = nc.tensor.matmul

            def rows(h, n):
                per = P // n
                return slice(n * (h % per), n * (h % per) + n), h // per

            def pairs(sample, j, n, t):
                if n:
                    ga_put.wait(pe, t, n)
                else:
                    pt_ready.wait(pe, t)
                    qe_ready.wait(pe, t)
                for q in range(4):
                    if q > 1:
                        row_done.wait(pe, t, 4 * n + q - 1)
                    for h in (q, q + 4):
                        r, m = rows(h, GK)
                        w = gkt[r, m] if j == NL else ke[r, m, j]
                        x = gqt[r, m] if j == NL else qe[r, m, j]
                        a = gla_at(h)
                        k = mm(PS[:, 1 + a // 4, (a % 4) * P:(a % 4 + 1) * P], w, x, start=True, stop=True)
                    k.then_inc(row_done.sem, 1)
                row_done.wait(pe, t, 4 * n + 4)
                pe.sem_inc(ga_mm.sem, 1)

            def tile(i, s, sample):
                t = i * 2 + s
                start(pe, t, "pe")
                upto, after = (c("upto_s"), c("after_s")) if sample else (c("upto_p"), c("after_p"))
                ug_ready.wait(pe, t)
                for g in range(2):
                    k = mm(PS[:, 1 + g, :], after, half(ug, g).rearrange("p h t -> p (h t)"), start=True, stop=True)
                k.then_inc(dec_sum.sem, 1)
                gwide_ready.wait(pe, t)
                gt = e.gdn[:, ds(t, 1), :].rearrange("p o h -> p (o h)")
                nb = BS if sample else 1
                ends = c("streams") if sample else e.ones[:, 0:1]
                mm(PS[:, 0, 0:H], upto, gt, start=True, stop=True)
                mm(PS[:, 0, H:2 * H], after, gt, start=True, stop=True)
                for m in range(H // 2):
                    mm(PS[:, 0, 16 + m * nb:16 + (m + 1) * nb], gwide[:, 2 * m:2 * m + 2].rearrange("p h v -> p (h v)"),
                       ends, start=True, stop=True)
                mm(PS[:, 0, 256:512], after, e.ggla[:, ds(t, 1)].rearrange("p o c -> p (o c)"),
                   start=True, stop=True).then_inc(small_mm.sem, 1)
                pe.wait_ge(load[s], (i + 1) * 32)
                for m in range(4):
                    k = pe.transpose(PS[:, 3, m * P:(m + 1) * P], lr[:, s, 0, m * P:(m + 1) * P], ident)
                k.then_inc(gla_turned.sem, 1)
                gs_ready.wait(pe, t)
                sp_ = c("spans")
                for m in range(2):
                    w = gs[:, m * P:(m + 1) * P]
                    mm(PS[:, 4 + 2 * m, :], w, sp_[:, 0:4 * P], start=True, stop=True)
                    mm(PS[:, 5 + 2 * m, 0:3 * P], w, sp_[:, 4 * P:7 * P], start=True, stop=True)
                    mm(PS[:, 5 + 2 * m, 3 * P:4 * P], w, upto, start=True, stop=True).then_inc(e_mm.sem, 1)
                for n, (src, bank) in enumerate(((qn, 3), (kn, 0), (kb, 4))):
                    scaled.wait(pe, t, n + 1)
                    (lambda: gla_ready.wait(pe, t), lambda: small_exp.wait(pe, t), lambda: e_exp.wait(pe, t, 1))[n]()
                    for m in range(4):
                        k = pe.transpose(PS[:, bank, m * P:(m + 1) * P],
                                         src[:, 2 * m:2 * m + 2].rearrange("p h v -> p (h v)"), ident)
                    k.then_inc(turned.sem, 1)
                tready.wait(pe, t)
                e_exp.wait(pe, t)
                for out, moving, done in ((6, kbt, a_mm), (1, qt, p_mm)):
                    if out == 1:
                        dec_exp.wait(pe, t)
                    for h in range(H):
                        r, m = rows(h, DK)
                        k = mm(PS[:, out + h % 2, m * P:(m + 1) * P], kt[r, m], moving[r, m], start=True, stop=True)
                    k.then_inc(done.sem, 1)
                u_first.wait(pe, t)
                for g, bank in enumerate((3, 0)):
                    for h in range(4):
                        k = pe.transpose(PS[:, bank, h * P:(h + 1) * P], u[:, 4 * g + h], ident)
                    k.then_inc(t_turned.sem, 1)
                jobs = pairs_jobs(sample)
                done_jobs = 0
                for li, l in enumerate(levels(sample)):
                    last = l == levels(sample)[-1]
                    for g, bank in enumerate((3, 0)):
                        if li:
                            t_put.wait(pe, t, 2 * (li - 1) + g + 1)
                        else:
                            t_first.wait(pe, t, g + 1)
                        for h in range(4):
                            k = mm(PS[:, bank, h * P:(h + 1) * P], bt[:, 4 * g + h], tt[:, 4 * g + h], start=True, stop=True)
                        k.then_inc(z_mm.sem, 1)
                    take = len(jobs) - done_jobs if last else max(1, -(-(len(jobs) - done_jobs) // (len(levels(sample)) - li)))
                    for n in range(done_jobs, done_jobs + take):
                        pairs(sample, jobs[n], n, t)
                    done_jobs += take
                    for g in range(2):
                        z_copied.wait(pe, t, 2 * li + g + 1)
                        if li:
                            u_put.wait(pe, t, 2 * (li - 1) + g + 1)
                        for h in range(4):
                            k = mm(PS[:, 4 + g, h * P:(h + 1) * P], z[:, 4 * g + h], u[:, 4 * g + h], start=True, stop=True)
                        k.then_inc(du_mm.sem, 1)
                        if last:
                            continue
                        if not li:
                            bt_ready.wait(pe, t)
                        for h in range(4):
                            k = mm(PS[:, 6 + g, h * P:(h + 1) * P], u[:, 4 * g + h], z[:, 4 * g + h], start=True, stop=True)
                        k.then_inc(dt_mm.sem, 1)
                nl, nj = len(levels(sample)), len(jobs)
                rd = 4 * nj
                if not sample:
                    for q in range(2):
                        for out, w, done in ((3, kt, ks_mm), (0, qt, qs_mm)):
                            if q:
                                row_done.wait(pe, t, rd - 1)
                            for h in range(q, H, 2):
                                r, m = rows(h, DK)
                                k = mm(PS[:, out, h * DK:(h + 1) * DK], w[r, m], S[r, m], start=True, stop=True)
                            k.then_inc(row_done.sem, 1)
                            rd += 1
                            if q:
                                row_done.wait(pe, t, rd)
                                pe.sem_inc(done.sem, 1)
                else:
                    pe.wait_ge(states_in, 16 * 6)
                    for n in range(8):
                        out, done = ((3, ks_mm), (0, qs_mm))[n // 4]
                        pe.wait_ge(mk_ready, n + 1)
                        for hh in range(2):
                            if n % 4 or hh:
                                row_done.wait(pe, t, rd)
                            h = 2 * (n % 4) + hh
                            r, m = rows(h, DK)
                            for b in range(BS):
                                k = mm(PS[:, out, h * DK:(h + 1) * DK], mk[r, n % 2, b], Ss[r, m, b],
                                       start=(b == 0), stop=(b == BS - 1))
                            k.then_inc(row_done.sem, 1)
                            rd += 1
                        row_done.wait(pe, t, rd)
                        pe.sem_inc(mk_used, 1)
                        if n % 4 == 3:
                            pe.sem_inc(done.sem, 1)
                ga_put.wait(pe, t, nj)
                if sample:
                    pe.wait_ge(mk_ready, 10)
                for q in range(4):
                    if q:
                        row_done.wait(pe, t, rd)
                    for h in (q, q + 4):
                        r, m = rows(h, GK)
                        o = PS[:, 1, h * DK:(h + 1) * DK]
                        if sample:
                            for b in range(BS):
                                k = mm(o, mk[r, m, b], GSs[r, m, b], start=(h == 0 and b == 0), stop=False,
                                       skip_group_check=True)
                        else:
                            k = mm(o, qe[r, m, NL], GS[r, m], start=(h == 0), stop=False, skip_group_check=True)
                    k.then_inc(row_done.sem, 1)
                    rd += 1
                row_done.wait(pe, t, rd)
                if sample:
                    pe.sem_inc(mk_used, 2)
                assert sample or rd == row_done.per
                for h in range(H):
                    k = mm(PS[:, 1, h * DK:(h + 1) * DK], ga[:, gla_at(h)], lr[:, s, 1, h * DK:(h + 1) * DK],
                           start=False, stop=(h == H - 1), skip_group_check=True)
                k.then_inc(go_mm.sem, 1)
                if not sample:
                    kdg_ready.wait(pe, t)
                    for h in range(H):
                        r, m = rows(h, GK)
                        k = mm(PS[r, 2, m * DK:(m + 1) * DK], kdg[:, h * GK:(h + 1) * GK],
                               lr[:, s, 1, h * DK:(h + 1) * DK], start=True, stop=True)
                    k.then_inc(gstate_mm.sem, 1)
                r_ready.wait(pe, t)
                u_put.wait(pe, t, 2 * nl)
                for h in range(H):
                    k = mm(PS[:, 4, h * DK:(h + 1) * DK], u[:, at(h)], rr[:, h * DK:(h + 1) * DK], start=True, stop=True)
                k.then_inc(v_mm.sem, 1)
                v_ready.wait(pe, t)
                for h in range(H):
                    k = mm(PS[:, 5, h * DK:(h + 1) * DK], pt[:, at(h)], vn[:, h * DK:(h + 1) * DK], start=True, stop=True)
                k.then_inc(o_mm.sem, 1)
                pe.wait_ge(end["pool"], t + 3)
                if not sample:
                    for h in range(H):
                        r, m = rows(h, DK)
                        k = mm(PS[r, 6, m * DK:(m + 1) * DK], kd[:, h].rearrange("p v -> p v"),
                               vn[:, h * DK:(h + 1) * DK], start=True, stop=True)
                    k.then_inc(end["pe"], 1)
                else:
                    for n in range(2 * H):
                        gla = n >= H
                        h = n % H
                        pe.wait_ge(vm_ready, n + 1)
                        if gla:
                            r, m = rows(h, GK)
                            bank, w = (6, 7)[m], kdg[:, h * GK:(h + 1) * GK]
                            if h % 4 == 0:
                                pe.wait_ge(s_done, (1, 4)[m])
                        else:
                            r, m = rows(h, DK)
                            bank, w = (6, 2, 3, 7)[m], kd[:, h]
                        k = mm(PS[r, bank, :], w, vm[:, n % 2].rearrange("p b v -> p (b v)"), start=True, stop=True)
                        k.then_inc(vm_used, 1)
            each(pe, tile)

        @block.scalar
        def _(act):
            act.sem_inc(end["act"], 2)
            copy, exp = nc.scalar.copy, lambda o, x, **k: nc.scalar.activation(o, x, ACT.Exp, **k)

            def tile(i, s, sample):
                t = i * 2 + s
                nb = BS if sample else 1
                start(act, t, "act")
                dec_sum.wait(act, t)
                exp(dec[:], bank2(1)).then_inc(dec_exp.sem, 1)
                small_mm.wait(act, t)
                exp(small[:], PS[:, 0, 0:2 * H])
                exp(egl[:, :, 0:nb], PS[:, 0, 16:16 + 4 * nb].rearrange("p (m b) -> p m b", m=4))
                exp(kde[:], PS[:, 0, 256:512], scale=1.0 / 16).then_inc(small_exp.sem, 1)
                gla_turned.wait(act, t)
                nc.scalar.activation(gqt[:], PS[:, 3, 0:2 * P].rearrange("p (m t) -> p m t", m=2), ACT.Copy,
                                     scale=float(GK) ** -0.5)
                copy(gkt[:], PS[:, 3, 2 * P:4 * P].rearrange("p (m t) -> p m t", m=2)).then_inc(gla_ready.sem, 1)
                for m in range(2):
                    e_mm.wait(act, t, m + 1)
                    exp(ex[:, m], bank2(4 + 2 * m), scale=1.0 / 16).then_inc(e_exp.sem, 1)
                for n, (dst, bank) in enumerate(((qt, 3), (kt, 0), (kbt, 4))):
                    turned.wait(act, t, n + 1)
                    copy(dst[:], PS[:, bank, :].rearrange("p (m t) -> p m t", m=4)).then_inc(tready.sem, 1)
                for g, bank in enumerate((3, 0)):
                    t_turned.wait(act, t, g + 1)
                    copy(half(tt, g), PS[:, bank, :].rearrange("p (h t) -> p h t", h=4)).then_inc(t_first.sem, 1)
                for li in range(len(levels(sample))):
                    for g, bank in enumerate((3, 0)):
                        z_mm.wait(act, t, 2 * li + g + 1)
                        copy(half(z, g), PS[:, bank, :].rearrange("p (h t) -> p h t", h=4)).then_inc(z_copied.sem, 1)
                go_mm.wait(act, t)
                copy(e.o_all[:, ds(t, 1), HE:2 * HE].rearrange("p o v -> p (o v)"), PS[:, 1, :]).then_inc(go_copied.sem, 1)
                v_mm.wait(act, t)
                copy(vn[:], PS[:, 4, :]).then_inc(v_ready.sem, 1)
                v_ready.wait(act, t)
                act.sem_inc(end["act"], 1)
            each(act, tile)

        @block.vector
        def _(dve):
            v = nc.vector
            tt_ = v.tensor_tensor
            v.memset(S[:], 0.0)
            v.memset(GS[:], 0.0).then_inc(state_zero, 1)
            v.memset(ga[:], 0.0).then_inc(cleared, 1)
            dve.wait_ge(cleared, 1)
            dve.wait_ge(state_zero, 1)
            dve.sem_inc(end["dve"], 2)

            def place(sample, j, n, t):
                ga_mm.wait(dve, t, n + 1)
                e.apart(dve)
                v.copy_predicated(ga[:], over_heads(c("up")[:, j * P:(j + 1) * P]), bank2(1)).then_inc(ga_put.sem, 1)

            def tile(i, s, sample):
                t = i * 2 + s
                start(dve, t, "dve")
                v.tensor_copy(u[:], over_heads(ident)).then_inc(u_init.sem, 1)
                if sample:
                    v.memset(ga[:], 0.0).then_inc(ga_zero, 1)
                gla_ready.wait(dve, t)
                for m in range(2):
                    e_exp.wait(dve, t, m + 1)
                    tt_(qe[:, m], ex[:, m], over_heads(gqt[:, m], NL + 1), ALU.mult)
                    tt_(ke[:, m], ex[:, m, 0:NL], over_heads(gkt[:, m], NL), ALU.mult).then_inc(qe_ready.sem, 1)
                small_exp.wait(dve, t)
                dve.wait_ge(load[s], (i + 1) * 32)
                tt_(kdg[:], lr[:, s, 0, 2 * P:4 * P], kde[:], ALU.mult).then_inc(kdg_ready.sem, 1)
                tt_(be[:], e.beta[:, ds(t, 1)].rearrange("p o h -> p (o h)"), small[:, 0:H], ALU.mult).then_inc(be_ready.sem, 1)
                a_mm.wait(dve, t)
                dec_masked.wait(dve, t)
                v.scalar_tensor_tensor(out=bt[:].rearrange("p h t -> p (h t)"),
                                       in0=PS[:, 6:8, :].rearrange("p b n -> p (b n)"), scalar=-1.0,
                                       in1=dec[:].rearrange("p h t -> p (h t)"), op0=ALU.mult, op1=ALU.mult
                                       ).then_inc(bt_ready.sem, 1)
                bt_ready.wait(dve, t)
                u_init.wait(dve, t)
                e.apart(dve)
                v.copy_predicated(u[:], over_heads(c("up")[:, 0:P]), bt[:]).then_inc(u_first.sem, 1)
                p_mm.wait(dve, t)
                tt_(pt[:], bank2(1), dec[:], ALU.mult).then_inc(pt_ready.sem, 1)
                if sample:
                    dve.wait_ge(ga_zero, 1)
                jobs, n = pairs_jobs(sample), 0
                lv = levels(sample)
                for li, l in enumerate(lv):
                    last = l == lv[-1]
                    take = len(jobs) - n if last else max(1, -(-(len(jobs) - n) // (len(lv) - li)))
                    for j in range(n, n + take):
                        place(sample, jobs[j], j, t)
                    n += take
                    for g in range(2):
                        (du_mm.wait(dve, t, 2 * li + g + 1) if last else dt_mm.wait(dve, t, 2 * li + g + 1))
                        if li:
                            u_put.wait(dve, t, 2 * (li - 1) + g + 1)
                        else:
                            u_first.wait(dve, t)
                        e.apart(dve)
                        v.copy_predicated(half(u, g), over_heads(c("up")[:, l * P:(l + 1) * P], 4),
                                          PS[:, 4 + g, :].rearrange("p (h t) -> p h t", h=4)).then_inc(u_put.sem, 1)
                        if not last:
                            v.copy_predicated(half(tt, g), over_heads(c("low")[:, l * P:(l + 1) * P], 4),
                                              PS[:, 6 + g, :].rearrange("p (h t) -> p h t", h=4)).then_inc(t_put.sem, 1)
                if sample:
                    for k in range(10):
                        dve.wait_ge(mk_used, k + 1)
                        x = kt[:, k] if k < 4 else qt[:, k - 4] if k < 8 else qe[:, k - 8, NL]
                        tt_(mk[:, k % 2], over_heads(x), c("stream_cols").rearrange("p (b t) -> p b t", b=BS),
                            ALU.mult).then_inc(mk_ready, 1)
                ks_mm.wait(dve, t)
                be_ready.wait(dve, t)
                tt_(hv(tmp[:]), hv(PS[:, 3, :]), wide(be[:], DK), ALU.mult).then_inc(ks_scaled.sem, 1)
                ks_scaled.wait(dve, t)
                scaled.wait(dve, t)
                tt_(hv(rr[:]), bv[:], hv(tmp[:]), ALU.subtract).then_inc(r_ready.sem, 1)
                qs_mm.wait(dve, t)
                tt_(hv(tmq[:]), hv(PS[:, 0, :]), wide(small[:, 0:H], DK), ALU.mult).then_inc(qs_scaled.sem, 1)
                if not sample:
                    gstate_mm.wait(dve, t)
                    for m in range(2):
                        v.scalar_tensor_tensor(out=GS[:, m], in0=GS[:, m], scalar=ex[:, m, NL, P - 1:P],
                                               in1=PS[:, 2, m * DK:(m + 1) * DK], op0=ALU.mult, op1=ALU.add)
                o_mm.wait(dve, t)
                qs_scaled.wait(dve, t)
                tt_(e.o_all[:, ds(t, 1), 0:HE].rearrange("p o v -> p (o v)"), tmq[:], PS[:, 5, :], ALU.add)
                if not sample:
                    dve.wait_ge(end["pe"], t + 3)
                    for m in range(H // 2):
                        k = v.scalar_tensor_tensor(out=S[:, m], in0=S[:, m], scalar=egl[:, m, 0:1],
                                                   in1=PS[:, 6, m * DK:(m + 1) * DK], op0=ALU.mult, op1=ALU.add)
                    k.then_inc(end["dve"], 1)
                else:
                    v_ready.wait(dve, t)
                    dve.wait_ge(mk_used, 12)

                    def values(n):
                        dve.wait_ge(vm_used, n + 1)
                        src = vn[:, (n % H) * DK:(n % H + 1) * DK] if n < H else lr[:, s, 1, (n - H) * DK:(n - H + 1) * DK]
                        tt_(vm[:, n % 2], bc(src.rearrange("p (o v) -> p o v", o=1), (P, BS, DK)),
                            wide(c("streams"), DK), ALU.mult).then_inc(vm_ready, 1)

                    def update(st, bank, decay, buf, k, used):
                        tt_(buf.rearrange("p (b v) -> p b v", b=BS), st, decay, ALU.mult).then_inc(sd_ready, 1)
                        dve.wait_ge(vm_used, used + 2)
                        dve.wait_ge(sd_ready, k)
                        tt_(st, buf.rearrange("p (b v) -> p b v", b=BS), PS[:, bank, :].rearrange("p (b v) -> p b v", b=BS),
                            ALU.add).then_inc(s_done, 1)
                    for m in range(H // 2):
                        values(2 * m)
                        values(2 * m + 1)
                        update(Ss[:, m], (6, 2, 3, 7)[m], wide(egl[:, m], DK), (Ssd, GSsd)[m % 2], m + 1, 2 * m + 2)
                    for m in range(2):
                        for hh in range(4):
                            values(H + 4 * m + hh)
                        last = ex[:, m, NL].rearrange("p (b l) -> p b l", b=BS)[:, :, LS - 1:LS]
                        update(GSs[:, m], 6 + m, bc(last, (P, BS, DK)), (Ssd, GSsd)[m % 2], m + 5, H + 4 * m + 4)
            each(dve, tile)


def gate_outputs(e, oT):
    nc, d, PS, ident = e.nc, e.d, e.PS, e.ident
    NH = 2 * H
    with e.stage() as ctx:
        gate = e.sb(ctx, "gate_rows", [P, 2, 2 * H * DK])
        gain = e.sb(ctx, "head_gains", [P, 2, DK])
        sq = e.sb(ctx, "o_sq", [P, 2, 2 * H * DK])
        og = e.sb(ctx, "o_gated", [P, 2, 2 * H * DK])
        ss = e.sb(ctx, "o_ss", [P, 2, NH])
        eps = e.sb(ctx, "o_eps", [P, 1])
        g0, g1, gain_in, eps_set, squared, summed, rooted, inverted, normed, gained, gated, turned, low, high = e.sem(
            ctx, "gate_in0", "gate_in1", "head_gain_in", "o_eps_set", "o_squared", "o_summed", "o_rooted", "o_inverted",
            "o_normed", "o_gained", "o_gated", "o_turned", "oT_low", "oT_high")
        gate_in = [g0, g1]
        block = ctx.enter_context(nc.Block())

        def each(eng, tile):
            with eng.Fori(0, NPT // 2) as i:
                tile(i, 0)
                tile(i, 1)
            tile(NPT // 2, 0)

        @block.sync
        def _(sp):
            sp.dma_start(gain[:, 0], d["dn_out_norm"].broadcast_to((P, DK))).then_inc(gain_in, 16)
            sp.dma_start(gain[:, 1], d["gla_out_norm"].broadcast_to((P, DK))).then_inc(gain_in, 16)

            def tile(i, s):
                t = i * 2 + s
                sp.wait_ge(gated, t + 1)
                sp.dma_start(gate[:, s], e.scr["rest"][ds(t * P, P), 0:2].rearrange("t g c -> t (g c)")
                             ).then_inc(gate_in[s], 16)
            each(sp, tile)

        @block.gpsimd
        def _(pool):
            def tile(i, s):
                t = i * 2 + s
                o = e.o_all[:, ds(t, 1)].rearrange("p o c -> p (o c)")
                pool.wait_ge(summed, t + 1)
                e.apart(pool)
                nc.gpsimd.tensor_tensor(sq[:, s], o, o, ALU.mult).then_inc(squared, 1)
            each(pool, tile)

        @block.scalar
        def _(act):
            act.sem_inc(low, 2)
            act.wait_ge(eps_set, 1)

            def tile(i, s):
                t = i * 2 + s
                act.wait_ge(summed, t + 3)
                nc.scalar.activation(ss[:, s], ss[:, s], ACT.Sqrt, scale=1.0 / DK, bias=eps[:, 0:1]).then_inc(rooted, 1)
                act.wait_ge(turned, t * 2 + 5)
                nc.scalar.copy(oT[:, 0:4, ds(t * P, P)], PS[:, 2 * s, :].rearrange("p (k t) -> p k t", k=4)).then_inc(low, 1)
                act.wait_ge(turned, t * 2 + 6)
                nc.scalar.copy(oT[:, 4:8, ds(t * P, P)], PS[:, 2 * s + 1, :].rearrange("p (k t) -> p k t", k=4)).then_inc(high, 1)
            act.sem_inc(high, 2)
            each(act, tile)

        @block.vector
        def _(dve):
            dve.sem_inc(gated, 2)
            dve.sem_inc(summed, 2)
            nc.vector.memset(eps[:], EPS).then_inc(eps_set, 1)
            dve.wait_ge(gain_in, 32)

            def tile(i, s):
                t = i * 2 + s
                heads = lambda ap: ap.rearrange("p (h v) -> p h v", v=DK)
                dve.wait_ge(squared, t + 1)
                nc.vector.reduce_sum(ss[:, s], heads(sq[:, s]), AX_X).then_inc(summed, 1)
                dve.wait_ge(rooted, t + 1)
                nc.vector.reciprocal(ss[:, s], ss[:, s]).then_inc(inverted, 1)
                dve.wait_ge(inverted, t + 1)
                o = e.o_all[:, ds(t, 1)].rearrange("p o c -> p (o c)")
                dve.wait_ge(turned, t * 2 + 2)
                nc.vector.tensor_tensor(heads(og[:, s]), heads(o), bc(ss[:, s].rearrange("p (h o) -> p h o", o=1), (P, NH, DK)),
                                        ALU.mult).then_inc(normed, 1)
                dve.wait_ge(normed, t + 1)
                for m in range(2):
                    x = heads(og[:, s, m * 512:(m + 1) * 512])
                    k = nc.vector.tensor_tensor(x, x, bc(gain[:, m:m + 1], (P, H, DK)), ALU.mult)
                k.then_inc(gained, 1)
                dve.wait_ge(gained, t + 1)
                dve.wait_ge(gate_in[s], (i + 1) * 16)
                nc.vector.tensor_tensor(og[:, s], og[:, s], gate[:, s], ALU.mult).then_inc(gated, 1)
            each(dve, tile)

        @block.tensor
        def _(pe):
            pe.sem_inc(turned, 4)

            def tile(i, s):
                t = i * 2 + s
                pe.wait_ge(gated, t + 3)
                for h, out in enumerate((low, high)):
                    pe.wait_ge(out, t + 1)
                    for k in range(4):
                        m = pe.transpose(PS[:, 2 * s + h, k * P:(k + 1) * P],
                                         og[:, s, (h * 4 + k) * P:(h * 4 + k + 1) * P], ident)
                    m.then_inc(turned, 1)
            each(pe, tile)



def qkv_projection(e, hT):
    nc, d, PS, ident = e.nc, e.d, e.PS, e.ident
    wv = d["c_w_qkv"][0].rearrange("(k p) n -> p k n", p=P)
    qk, vr = e.scr["qk"], e.scr["v"]
    KR = 5
    with e.stage() as ctx:
        ws = e.sb(ctx, "w_qk", [P, 2, KT, P])
        cols = e.sb(ctx, "qk_cols", [P, 2, T])
        krow = e.sb(ctx, "k_rows", [P, 2, KR, P])
        w0, w1, mm, kept, turned, kcopied, st0, st1, kst0, kst1 = e.sem(
            ctx, "wqk_in0", "wqk_in1", "qk_mm", "qk_kept", "k_turned", "k_copied", "qk_stored0", "qk_stored1",
            "k_stored0", "k_stored1")
        w_in, stored, kstored = [w0, w1], [st0, st1], [kst0, kst1]
        block = ctx.enter_context(nc.Block())
        NB = 2 * KT
        ckp = d["c_k_p"].rearrange("n b r h c -> (n b r) (h c)").rearrange("(j p) c -> p j c", p=P)
        cks = d["c_k_s"].rearrange("n b r h c -> (n b r) (h c)")

        @block.gpsimd
        def _(pool):
            for s in range(2):
                pool.dma_start(ws[:, s], wv[:, :, s * P:(s + 1) * P]).then_inc(w_in[s], 16)
            with pool.Fori(1, NB // 2) as i:
                for s in range(2):
                    pool.wait_ge(mm, i * 2 - 1 + s)
                    e.apart(pool)
                    pool.dma_start(ws[:, s], wv[:, :, ds(i * 256 + s * P, P)]).then_inc(w_in[s], 16)

        @block.sync
        def _(sp):
            for s in range(2):
                sp.sem_inc(stored[s], 16)
                sp.sem_inc(kstored[s], 16)

            def store(i, s):
                sp.wait_ge(kept, i * 2 + s + 3)
                sp.dma_start(qk[ds(i * 2 + s, 1)].rearrange("o p t -> p (o t)"), cols[:, s]).then_inc(stored[s], 16)
            with sp.Fori(0, NB // 4) as i:
                store(i, 0)
                store(i, 1)
            with sp.Fori(0, NB // 4) as i:
                for s in range(2):
                    store(i + NB // 4, s)
                    sp.wait_ge(kcopied, (i * 2 + s) * 2 + 6)
                    c = ds(i * 256 + s * P, P)
                    sp.dma_start(ckp[:, :, c], krow[:, s, 0:KR - 1]).then_inc(kstored[s], 16)
                    sp.dma_start(cks[:, c], krow[:, s, KR - 1]).then_inc(kstored[s], 16)
            for s in range(2):
                sp.wait_ge(stored[s], 16 * (NB // 2 + 1))
                sp.wait_ge(kstored[s], 16 * (NB // 2 + 1))

        @block.tensor
        def _(pe):
            def multiply(i, s):
                pe.wait_ge(w_in[s], (i + 1) * 16)
                pe.wait_ge(kept, i * 2 + s + 1)
                product(nc, PS, 3 * s, lambda k: ws[:, s, k], lambda k, j: hT[:, k, j * GN:(j + 1) * GN],
                        range(KT)).then_inc(mm, 1)

            def turn(i, s):
                pe.wait_ge(kept, (i * 2 + s) + KT + 3)
                for h, ts in enumerate((range(4), range(4, 5))):
                    pe.wait_ge(kcopied, (i * 2 + s) * 2 + h + 3)
                    for n in ts:
                        m = pe.transpose(PS[:, 6 + h, (n % 4) * P:(n % 4 + 1) * P],
                                         cols[:, s, (NT - KR + n) * P:(NT - KR + n + 1) * P], ident)
                    m.then_inc(turned, 1)
            with pe.Fori(0, NB // 4) as i:
                multiply(i, 0)
                multiply(i, 1)
            multiply(NB // 4, 0)
            with pe.Fori(0, NB // 4 - 1) as i:
                multiply(i + NB // 4, 1)
                turn(i, 0)
                multiply(i + NB // 4 + 1, 0)
                turn(i, 1)
            multiply(NB // 2 - 1, 1)
            turn(NB // 4 - 1, 0)
            turn(NB // 4 - 1, 1)

        @block.scalar
        def _(act):
            act.sem_inc(kept, 2)

            def keep(i, s):
                act.wait_ge(mm, i * 2 + s + 1)
                act.wait_ge(stored[s], (i + 1) * 16)
                nc.scalar.copy(groups(cols[:, s]), PS[:, 3 * s:3 * s + G, 0:GN]).then_inc(kept, 1)
            with act.Fori(0, NB // 4) as i:
                keep(i, 0)
                keep(i, 1)
            with act.Fori(0, NB // 4) as i:
                for s in range(2):
                    act.wait_ge(mm, (i + NB // 4) * 2 + s + 1)
                    act.wait_ge(stored[s], (i + NB // 4 + 1) * 16)
                    act.wait_ge(kcopied, (i * 2 + s) * 2 + 2)
                    nc.scalar.copy(groups(cols[:, s]), PS[:, 3 * s:3 * s + G, 0:GN]).then_inc(kept, 1)

        @block.vector
        def _(dve):
            dve.sem_inc(kcopied, 4)
            with dve.Fori(0, NB // 4) as i:
                for s in range(2):
                    dve.wait_ge(kstored[s], (i * 32) + 16)
                    dve.wait_ge(turned, (i * 2 + s) * 2 + 1)
                    nc.vector.tensor_copy(krow[:, s, 0:4], PS[:, 6, :].rearrange("p (j c) -> p j c", j=4)).then_inc(kcopied, 1)
                    dve.wait_ge(turned, (i * 2 + s) * 2 + 2)
                    nc.vector.tensor_copy(krow[:, s, 4], PS[:, 7, 0:P]).then_inc(kcopied, 1)


def v_projection(e, hT):
    nc, d, PS = e.nc, e.d, e.PS
    wv = d["c_w_qkv"][0].rearrange("(k p) n -> p k n", p=P)
    cvp = d["c_v_p"].rearrange("n b r h c -> (n b r) (h c)")
    cvs = d["c_v_s"].rearrange("n b r h c -> (n b r) (h c)")
    with e.stage() as ctx:
        w = e.sb(ctx, "w_v", [P, 2, KT, 512])
        out = e.sb(ctx, "v_rows", [P, 2, D])
        w0, w1, mm, copied, s0, s1 = e.sem(ctx, "wv_in0", "wv_in1", "v_mm", "v_copied", "v_out0", "v_out1")
        w_in, stored = [w0, w1], [s0, s1]
        block = ctx.enter_context(nc.Block())

        @block.sync
        def _(sp):
            for j in range(2):
                sp.dma_start(w[:, j], wv[:, :, 2 * D + j * 512:2 * D + (j + 1) * 512]).then_inc(w_in[j], 16)
            for t in range(NT):
                sp.wait_ge(copied, 2 * t + 2)
                sp.dma_start(e.scr["v"][t * P:(t + 1) * P], out[:, t % 2]).then_inc(stored[t % 2], 16)
                if t >= NT - 5:
                    dst = cvs if t == NT - 1 else cvp[(t - 4) * P:(t - 3) * P]
                    sp.dma_start(dst, out[:, t % 2]).then_inc(stored[t % 2], 16)
            sp.wait_ge(stored[0], 16 * 8)
            sp.wait_ge(stored[1], 16 * 6)

        @block.tensor
        def _(pe):
            for t in range(NT):
                for j in range(2):
                    n = 2 * t + j
                    pe.wait_ge(w_in[j], 16)
                    if n >= 4:
                        pe.wait_ge(copied, n - 3)
                    for k in range(KT):
                        m = nc.tensor.matmul(PS[:, n % 4, :], hT[:, k, t * P:(t + 1) * P], w[:, j, k],
                                             start=(k == 0), stop=(k == KT - 1))
                    m.then_inc(mm, 1)

        @block.scalar
        def _(act):
            total = [0, 0]
            for t in range(NT):
                if t >= 2:
                    act.wait_ge(stored[t % 2], 16 * total[t % 2])
                for j in range(2):
                    act.wait_ge(mm, 2 * t + j + 1)
                    nc.scalar.copy(out[:, t % 2, j * 512:(j + 1) * 512], PS[:, (2 * t + j) % 4, :]).then_inc(copied, 1)
                total[t % 2] += 2 if t >= NT - 5 else 1


def bias_rows(e):
    nc, d = e.nc, e.d
    with e.stage() as ctx:
        ext = e.sb(ctx, "bias_ext", [CH, RL])
        b_in, b_ext, b_out = e.sem(ctx, "bias_in", "bias_extended", "bias_out")
        block = ctx.enter_context(nc.Block())

        @block.sync
        def _(sp):
            sp.dma_start(ext[:, 127:RL], d["bias_falling"][0]).then_inc(b_in, 16)
            sp.wait_ge(b_ext, 1)
            sp.dma_start(e.scr["bias"], ext[:]).then_inc(b_out, 16)
            sp.wait_ge(b_out, 16)
            windows = bass.AP(e.scr["bias"].tensor, 127, [[RL, CH], [-1, P], [1, 2 * P]])
            sp.dma_start(e.scr["near"], windows).then_inc(b_out, 16)
            sp.wait_ge(b_out, 32)

        @block.vector
        def _(dve):
            dve.wait_ge(b_in, 16)
            nc.vector.tensor_copy(ext[:, 0:127], ext[:, 127:128].broadcast_to((CH, 127))).then_inc(b_ext, 1)


def attention(e, oT):
    nc, d, PS, ident, c = e.nc, e.d, e.PS, e.ident, e.const
    KW = 5 * P
    NPAIR = CH // 2
    NK = PAST // P
    NS = P + LS
    SCALE = float(HD) ** -0.5
    ck = d["cache_c_k"][0].rearrange("b r h c -> b r (h c)")
    cv = d["cache_c_v"][0].rearrange("b r h c -> b r (h c)")
    with e.stage() as ctx:
        qh = e.sb(ctx, "q_pair", [P, 2, T])
        kh = e.sb(ctx, "k_pair", [P, 2, T])
        vh = e.sb(ctx, "v_pair", [P, 2, NT, P])
        qs = e.sb(ctx, "q_pair_scaled", [P, T])
        qbd = e.sb(ctx, "q_streams", [P, BS, 2, LS])
        bias = e.sb(ctx, "bias_pair", [P, 2, 2, KW])
        near = e.sb(ctx, "bias_near", [P, 2, NS])
        biass = e.sb(ctx, "bias_samples", [P, 2, KW])
        sc = e.sb(ctx, "minus_scores", [P, 2, KW])
        pr = e.sb(ctx, "probs", [P, 2, KW])
        prt = e.sb(ctx, "probsT", [P, 2, KW])
        mn = e.sb(ctx, "minus_max", [P, 2, 1])
        sm = e.sb(ctx, "prob_sum", [P, 2, 1])
        rs = e.sb(ctx, "prob_sum_inv", [P, 2, 1])
        ot = e.sb(ctx, "o_tok", [P, NPT, P])
        kc = e.sb(ctx, "cache_k", [P, 2, NK, P])
        vc = e.sb(ctx, "cache_v", [P, 2, BS, NK, P])
        kct = e.sb(ctx, "cache_kT", [P, 2, PAST])
        NU = 2 * NPT
        N = NU + 2

        def count(name, per=1):
            return Count(e.sem(ctx, name), per)
        in0, in1, v0, v1, k0, k1 = e.sem(ctx, "pair_in0", "pair_in1", "cache_v_in0", "cache_v_in1", "cache_k_in0", "cache_k_in1")
        pair_in, vc_in, kc_in = [in0, in1], [v0, v1], [k0, k1]
        NIN = 5 + 2 * 4
        qbd_zero = e.sem(ctx, "qbd_zero")
        q_scaled, qbd_ready, bias_ready, biass_ready = count("q_scaled"), count("qbd_ready"), count("bias_ready"), count("bias_s_ready")
        s_mm, s_red, p_exp, r_inv = count("score_mm", NU), count("score_max", N), count("prob_exp", N), count("sum_inverse", N)
        p_turned, p_kept = count("probs_turned", N), count("probsT_kept", N)
        o_mm, o_div, p_norm = count("o_mm", NU), count("o_divided", NU), count("probs_normed", 2)
        ot_turned, ot_kept = count("o_turned", 2), count("oT_kept", 2)
        kc_turned, kc_kept, kc_used = count("cache_turned", BS), count("cache_kT_kept", BS), count("cache_kT_used", BS)
        so_mm = count("sample_o_mm")
        pair_end = {k: e.sem(ctx, f"pair_end_{k}") for k in ("pe", "act", "dve")}
        block = ctx.enter_context(nc.Block())

        def each(eng, pair):
            with eng.Fori(0, NPAIR // 2) as i:
                pair(i, 0)
                pair(i, 1)

        def start(eng, i, me):
            for k, s in pair_end.items():
                if k != me:
                    eng.wait_ge(s, i + 2)

        def width(u):
            return min(u // 2 + 1, 5) * P

        @block.sync
        def _(sp):
            def pair(i2, s):
                i = i2 * 2 + s
                for x in pair_end.values():
                    sp.wait_ge(x, i + 1)
                put = lambda dst, src: sp.dma_start(dst, src).then_inc(pair_in[s], 16)
                put(qh[:, s], e.scr["qk"][ds(i, 1)].rearrange("o p t -> p (o t)"))
                put(kh[:, s], e.scr["qk"][ds(i + NPAIR, 1)].rearrange("o p t -> p (o t)"))
                for hp in range(2):
                    row = e.scr["near"][ds(i * 2 + hp, 1)].rearrange("o r j -> (o r) j")
                    put(bias[:, s, hp, 3 * P:5 * P], row)
                    for b in range(4):
                        r = 2 * LS * b + LS * hp
                        put(near[r:r + LS, s], row[0:LS, 0:NS])
                put(vh[:, s], e.scr["v"].rearrange("(t p) c -> p t c", p=P)[:, :, ds(i * P, P)])
            each(sp, pair)

        @block.gpsimd
        def _(pool):
            def pair(i2, s):
                i = i2 * 2 + s
                for x in pair_end.values():
                    pool.wait_ge(x, i + 1)
                e.apart(pool)
                for b in range(BS):
                    pool.dma_start(vc[:, s, b], cv[b].rearrange("(r p) c -> p r c", p=P)[:, :, ds(i * P, P)]
                                   ).then_inc(vc_in[s], 16)
                for b in range(BS):
                    pool.wait_ge(kc_turned.sem, i * BS + b + 1)
                    e.apart(pool)
                    pool.dma_start(kc[:, b % 2], ck[b].rearrange("(r p) c -> p r c", p=P)[:, :, ds(i * P, P)]
                                   ).then_inc(kc_in[b % 2], 16)
            each(pool, pair)

        @block.tensor
        def _(pe):
            pe.sem_inc(pair_end["pe"], 2)
            pe.sem_inc(kc_turned.sem, 2)
            mm = nc.tensor.matmul

            def pair(i2, s):
                i = i2 * 2 + s
                start(pe, i, "pe")
                q_scaled.wait(pe, i)

                def score(u):
                    t, hp, w = u // 2, u % 2, width(u)
                    r = slice(hp * HD, hp * HD + HD)
                    if u > 1:
                        s_red.wait(pe, i, u - 1)
                    k0 = (t + 1) * P - w
                    m = mm(PS[:, 2 * hp, 0:min(w, 512)], qs[r, t * P:(t + 1) * P], kh[r, s, k0:k0 + min(w, 512)],
                           start=True, stop=True)
                    if w > 512:
                        m = mm(PS[:, 2 * hp + 1, 0:w - 512], qs[r, t * P:(t + 1) * P], kh[r, s, k0 + 512:k0 + w],
                               start=True, stop=True)
                    m.then_inc(s_mm.sem, 1)

                def turn(u, w):
                    p_exp.wait(pe, i, u + 1)
                    if u:
                        p_kept.wait(pe, i, u)
                    for n in range(w // P):
                        m = pe.transpose(PS[:, 4 + n // 4, (n % 4) * P:(n % 4 + 1) * P], pr[:, u % 2, n * P:(n + 1) * P], ident)
                    m.then_inc(p_turned.sem, 1)

                def product_v(u):
                    t, hp, w = u // 2, u % 2, width(u)
                    p_kept.wait(pe, i, u + 1)
                    if u > 1:
                        o_div.wait(pe, i, u - 1)
                    n = w // P
                    for j in range(n):
                        m = mm(PS[:, 6 + u % 2, 0:HD], prt[:, u % 2, j * P:(j + 1) * P],
                               vh[:, s, t + 1 - n + j, hp * HD:(hp + 1) * HD], start=(j == 0), stop=(j == n - 1))
                    m.then_inc(o_mm.sem, 1)
                for u in range(NU + 2):
                    if u < NU:
                        score(u)
                    if 1 <= u <= NU:
                        turn(u - 1, width(u - 1))
                    if u >= 2:
                        product_v(u - 2)
                qbd_ready.wait(pe, i)
                for b in range(BS + 1):
                    if b < BS:
                        pe.wait_ge(kc_in[b % 2], (i * (BS // 2) + b // 2 + 1) * 16)
                        if b < 2:
                            o_div.wait(pe, i, NU - 1 + b)
                        else:
                            kc_kept.wait(pe, i, b - 1)
                        for n in range(NK):
                            m = pe.transpose(PS[:, 6 + b % 2, n * P:(n + 1) * P], kc[:, b % 2, n], ident)
                        m.then_inc(kc_turned.sem, 1)
                    if b:
                        x = b - 1
                        g, rows = x // 4, slice(32 * (x % 4), 32 * (x % 4) + 32)
                        if x % 4 == 0:
                            s_red.wait(pe, i, NU - 1 + g)
                        kc_kept.wait(pe, i, x + 1)
                        w = qbd[:, x].rearrange("p h q -> p (h q)")
                        mm(PS[rows, 2 * g, :], w, kct[:, x % 2], start=True, stop=True)
                        m = mm(PS[rows, 2 * g + 1, 0:P], w, kh[:, s, LP:T], start=True, stop=True)
                        m.then_inc(kc_used.sem, 1)
                o_div.wait(pe, i)
                p_kept.wait(pe, i, NU)
                for h in range(2):
                    for n in range(4):
                        m = pe.transpose(PS[:, 4 + h, n * P:(n + 1) * P], ot[:, 4 * h + n], ident)
                    m.then_inc(ot_turned.sem, 1)
                pe.wait_ge(vc_in[s], (i2 + 1) * (16 * BS))
                ot_kept.wait(pe, i)
                kc_kept.wait(pe, i)
                for g in range(2):
                    p_norm.wait(pe, i, g + 1)
                    turn(NU + g, KW)
                    p_kept.wait(pe, i, NU + g + 1)
                    for x in range(4):
                        b = 4 * g + x
                        for n in range(NK + 1):
                            w = vc[:, s, b, n] if n < NK else vh[:, s, NT - 1]
                            m = mm(PS[:, 6, 32 * b:32 * b + 32], w, prt[:, g, n * P + 32 * x:n * P + 32 * x + 32],
                                   start=(n == 0), stop=(n == NK))
                m.then_inc(so_mm.sem, 1)
                so_mm.wait(pe, i)
                pe.sem_inc(pair_end["pe"], 1)
            each(pe, pair)

        @block.scalar
        def _(act):
            act.sem_inc(pair_end["act"], 2)

            def pair(i2, s):
                i = i2 * 2 + s
                start(act, i, "act")
                act.wait_ge(pair_in[s], (i2 + 1) * (16 * NIN))
                nc.scalar.activation(qs[:], qh[:, s], ACT.Copy, scale=SCALE).then_inc(q_scaled.sem, 1)

                def exp(u, w):
                    s_red.wait(act, i, u + 1)
                    if u > 1:
                        r_inv.wait(act, i, u - 1)
                    nc.scalar.activation(pr[:, u % 2, 0:w], sc[:, u % 2, 0:w], ACT.Exp, scale=-1.0, bias=mn[:, u % 2, 0:1],
                                         accum_out=sm[:, u % 2, 0:1]).then_inc(p_exp.sem, 1)

                def keep(u, w):
                    p_turned.wait(act, i, u + 1)
                    if 1 < u < NU:
                        o_mm.wait(act, i, u - 1)
                    nc.scalar.copy(prt[:, u % 2, 0:w], PS[:, 4:6, :].rearrange("p b n -> p (b n)")[:, 0:w]).then_inc(p_kept.sem, 1)
                for u in range(NU + 1):
                    if u:
                        keep(u - 1, width(u - 1))
                    if u < NU:
                        exp(u, width(u))
                for b in range(BS):
                    kc_turned.wait(act, i, b + 3)
                    if b > 1:
                        kc_used.wait(act, i, b - 1)
                    nc.scalar.copy(kct[:, b % 2], PS[:, 6 + b % 2, :]).then_inc(kc_kept.sem, 1)
                    if b == 5:
                        exp(NU, KW)
                for h in range(2):
                    ot_turned.wait(act, i, h + 1)
                    nc.scalar.copy(oT[:, ds(i, 1), h * 512:(h + 1) * 512].rearrange("p o t -> p (o t)"),
                                   PS[:, 4 + h, :]).then_inc(ot_kept.sem, 1)
                exp(NU + 1, KW)
                o_mm.wait(act, i)
                keep(NU, KW)
                keep(NU + 1, KW)
                p_kept.wait(act, i)
                act.sem_inc(pair_end["act"], 1)
            each(act, pair)

        @block.vector
        def _(dve):
            v = nc.vector
            v.memset(qbd[:], 0.0).then_inc(qbd_zero, 1)
            dve.wait_ge(qbd_zero, 1)
            dve.sem_inc(pair_end["dve"], 2)

            def pair(i2, s):
                i = i2 * 2 + s
                start(dve, i, "dve")
                dve.wait_ge(pair_in[s], (i2 + 1) * (16 * NIN))
                for hp in range(2):
                    far = bias[:, s, hp, 3 * P:3 * P + 1]
                    v.tensor_scalar(bias[:, s, hp, 0:P], c("far_mask"), far, None, ALU.add)
                    v.tensor_copy(bias[:, s, hp, P:3 * P], far.broadcast_to((P, 2 * P)))
                    m = v.tensor_tensor(bias[:, s, hp, 4 * P:], bias[:, s, hp, 4 * P:], c("own_mask"), ALU.add)
                m.then_inc(bias_ready.sem, 1)
                for g in range(2):
                    v.tensor_copy(biass[:, g, 0:3 * P], near[:, s, 0:1].broadcast_to((P, 3 * P)))
                    v.tensor_copy(biass[:, g, 3 * P:4 * P], near[:, s, 0:P])
                    m = v.tensor_tensor(biass[:, g, 4 * P:].rearrange("p (b q) -> p b q", b=BS),
                                        c("new_mask")[:, g * P:(g + 1) * P].rearrange("p (b q) -> p b q", b=BS),
                                        bc(near[:, s, P:NS].rearrange("p (o q) -> p o q", o=1), (P, BS, LS)), ALU.add)
                m.then_inc(biass_ready.sem, 1)
                q_scaled.wait(dve, i)
                for hp in range(2):
                    r = slice(hp * HD, hp * HD + HD)
                    m = v.tensor_copy(qbd[r, :, hp], qs[r, LP:T].rearrange("p (b q) -> p b q", b=BS))
                m.then_inc(qbd_ready.sem, 1)
                bias_ready.wait(dve, i)
                biass_ready.wait(dve, i)

                def reduce(u, w, b):
                    s_mm.wait(dve, i, u + 1) if u < NU else kc_used.wait(dve, i, 4 * (u - NU) + 4)
                    if u > 1:
                        p_exp.wait(dve, i, u - 1)
                    e.apart(dve)
                    p = PS[:, 2 * (u % 2):2 * (u % 2) + 2, :].rearrange("p b n -> p (b n)")[:, 0:w]
                    v.tensor_tensor_reduce(sc[:, u % 2, 0:w], p, b, -1.0, -NEG, ALU.add, ALU.min, mn[:, u % 2, 0:1]
                                           ).then_inc(s_red.sem, 1)

                def inverse(u):
                    p_exp.wait(dve, i, u + 1)
                    v.reciprocal(rs[:, u % 2], sm[:, u % 2]).then_inc(r_inv.sem, 1)

                def divide(u):
                    o_mm.wait(dve, i, u + 1)
                    r_inv.wait(dve, i, u + 1)
                    v.tensor_scalar(ot[:, u // 2, (u % 2) * HD:(u % 2 + 1) * HD], PS[:, 6 + u % 2, 0:HD],
                                    rs[:, u % 2, 0:1], None, ALU.mult).then_inc(o_div.sem, 1)
                for u in range(NU + 2):
                    if u < NU:
                        reduce(u, width(u), bias[:, s, u % 2, KW - width(u):])
                    if u >= 2:
                        divide(u - 2)
                    if 1 <= u <= NU:
                        inverse(u - 1)
                for g in range(2):
                    reduce(NU + g, KW, biass[:, g])
                for g in range(2):
                    inverse(NU + g)
                    r_inv.wait(dve, i, NU + g + 1)
                    v.tensor_scalar(pr[:, g], pr[:, g], rs[:, g, 0:1], None, ALU.mult).then_inc(p_norm.sem, 1)
                so_mm.wait(dve, i)
                for hp in range(2):
                    r = slice(hp * HD, hp * HD + HD)
                    m = v.tensor_copy(oT[r, ds(i, 1), LP:T].rearrange("p o (b q) -> p (o b) q", b=BS),
                                      PS[r, 6, 0:BS * 2 * LS].rearrange("p (b h q) -> p b h q", b=BS, h=2)[:, :, hp])
                m.then_inc(pair_end["dve"], 1)
            each(dve, pair)



NAMES = ['x_prompt', 'x_sample', 'state_dn_conv', 'state_dn', 'state_gla', 'cache_c_k', 'cache_c_v', 'ab_norm', 'ab_w_in',
         'dn_conv_w', 'dn_a_log', 'dn_dt_bias', 'dn_out_norm', 'gla_gk_w2', 'gla_gk_b', 'gla_out_norm', 'ab_w_out',
         'c_norm', 'c_w_qkv', 'bias_falling', 'c_w_out', 'ffn_norm', 'ffn_w_gu', 'ffn_w_down', 'final_norm',
         'const_f', 'const_u']
OUTS = [("y_prompt", (1, LP, D)), ("y_sample", (BS, LS, D)), ("conv_p", (1, 1, 3, QKV)), ("conv_s", (1, BS, 3, QKV)),
        ("dn_p", (1, 1, H, DK, DK)), ("dn_s", (1, BS, H, DK, DK)), ("gla_p", (1, 1, H, GK, DK)),
        ("gla_s", (1, BS, H, GK, DK)), ("c_k_p", (1, 1, PAST, CH, HD)), ("c_k_s", (1, BS, LS, CH, HD)),
        ("c_v_p", (1, 1, PAST, CH, HD)), ("c_v_s", (1, BS, LS, CH, HD))]


def build_program(nc, d, where, widths):
    e = Env(nc, d)
    with e.top as top:
        for name, shape in (("xT", [D, T]), ("qkv", [T, QKV]), ("rest", [T, 4, H * DK]), ("qk", [2 * KT, P, T]),
                            ("v", [T, D]), ("bias", [CH, RL]), ("near", [CH, P, 2 * P])):
            e.dram(name, shape)
        e.PS = top.enter_context(nc.psum_tensor("PS", [P, 8, 512], F32))
        e.cf = e.sb(top, "consts_f", [P, widths[0]])
        e.cu = e.sb(top, "consts_u", [P, widths[1]], U8)
        e.const = lambda k: (e.cu if k in ("up", "low") else e.cf)[:, where[k][0]:where[k][1]]
        e.ident, e.ones = e.const("ident"), e.const("ones")
        e.gain_of = {"ab": d["ab_norm"][0], "ffn0": d["ffn_norm"][0], "c": d["c_norm"][0], "ffn1": d["ffn_norm"][1],
                     "final": d["final_norm"]}
        e.gains = e.sb(top, "gains", [P, len(e.gain_of) * KT])
        e.passed = e.sem(top, "waits_passed")
        with ExitStack() as mixer:
            e.rn = e.sb(mixer, "qk_norms", [P, NT, 2 * H])
            e.beta = e.sb(mixer, "beta", [P, NT, H])
            e.rkb = e.sb(mixer, "k_norm_beta", [P, NT, H])
            e.gdn = e.sb(mixer, "dn_log_decay", [P, NT, H])
            e.ggla = e.sb(mixer, "gla_log_decay", [P, NT, H * GK])
            with ExitStack() as ctx:
                e.ss = e.sb(ctx, "head_ss", [P, NT, 3 * H])
                e.misc = e.sb(ctx, "misc", [NMISC, T])
                with ExitStack() as inner:
                    hT = e.sb(inner, "hT", [P, KT, T])
                    with ExitStack() as first:
                        e.xT = e.sb(first, "xT", [P, KT, T])
                        load_x(e)
                        rmsnorm(e, "ab", hT)
                    conv_projection(e, hT)
                    rest_projection(e, hT)
                token_scalars(e)
            with ExitStack() as ctx:
                e.o_all = e.sb(ctx, "o_all", [P, NT, 2 * H * DK])
                recurrences(e)
                with ExitStack() as inner:
                    oT = e.sb(inner, "mixer_oT", [P, KT, T])
                    gate_outputs(e, oT)
                    e.xT = e.sb(inner, "xT", [P, KT, T])
                    reload_x(e)
                    project_add(e, d["ab_w_out"][0], oT)
                    save_x(e)
        e.xT = e.sb(top, "xT", [P, KT, T])
        hT = e.sb(top, "hT", [P, KT, T])
        reload_x(e)
        rmsnorm(e, "ffn0", hT)
        ffn(e, d["ffn_w_gu"][0], d["ffn_w_down"][0], hT)
        rmsnorm(e, "c", hT)
        qkv_projection(e, hT)
        v_projection(e, hT)
        bias_rows(e)
        attention(e, hT)
        project_add(e, d["c_w_out"][0], hT)
        rmsnorm(e, "ffn1", hT)
        ffn(e, d["ffn_w_gu"][1], d["ffn_w_down"][1], hT)
        rmsnorm(e, "final", hT)
        write_y(e, hT)


def kernel(**inputs):
    import numpy as _np
    import concourse.bacc as _bacc
    from concourse import mybir as _mybir
    from concourse.bass_utils import run_bass_kernel_spmd as _run

    nc = _bacc.Bacc("TRN2", target_bir_lowering=False, num_devices=1)
    const_f, const_u, where = shape_constants()
    inputs["const_f"], inputs["const_u"] = const_f, const_u
    inputs["bias_falling"] = _np.ascontiguousarray(_np.asarray(inputs["c_rel_bias"])[:, :, ::-1])
    arrays, d = {}, {}
    for name in NAMES:
        a = _np.ascontiguousarray(inputs[name])
        arrays[f"in_{name}_dram"] = a
        d[name] = nc.dram_tensor(f"in_{name}_dram", a.shape, _mybir.dt.from_np(a.dtype), kind="ExternalInput").ap()
    for i, (name, shape) in enumerate(OUTS):
        d[name] = nc.dram_tensor(f"out_{i}_dram", shape, F32, kind="ExternalOutput").ap()
    build_program(nc, d, where, (const_f.shape[1], const_u.shape[1]))
    r = _run(nc, [arrays], core_ids=[0])
    return tuple(r.results[0][f"out_{i}_dram"] for i in range(len(OUTS)))
```

```python
from contextlib import ExitStack, contextmanager

import numpy as np

import concourse.bass as bass
from concourse import mybir

F32 = mybir.dt.float32
F32R = mybir.dt.float32r
U8 = mybir.dt.uint8
ALU = mybir.AluOpType
ACT = mybir.ActivationFunctionType
AX_X = mybir.AxisListType.X
ds = bass.ds

P = 128
D = 1024
KT = D // P
LP, BS, LS = 1024, 8, 16
T = LP + BS * LS
NT = T // P
NPT = LP // P
G, GN = 3, T // 3
H, DK = 8, 64
GK = 32
QKV = 3 * H * DK
NCB = QKV // P
AB_IN = 3616
COL_AB = QKV
COL_GATE = COL_AB + 2 * H
COL_GQK = COL_GATE + H * DK
COL_LR = COL_GQK + 2 * H * GK + H * DK
RANK = 16
CH, HD = 16, 64
PAST = 512
FF = 2816
FC = FF // 256
EPS = 1e-6
NEG = -1e30
LEVELS = [1, 2, 4, 8, 16, 32, 64]
RL = 384
NMISC = 48


def shape_constants():
    a = np.arange(P)
    row, col = a[:, None], a[None, :]
    same = row // LS == col // LS
    f = {"ident": np.eye(P), "ones": np.ones((P, P)),
         "upto_p": row <= col, "upto_s": (row <= col) & same,
         "after_p": row > col, "after_s": (row > col) & same}
    spans = []
    for s in LEVELS:
        mid = col // (2 * s) * (2 * s) + s
        spans.append(np.where(col >= mid, (row >= mid) & (row <= col), (row > col) & (row < mid)))
    f["spans"] = np.concatenate(spans, 1)
    f["streams"] = row // LS == np.arange(BS)[None, :]
    f["stream_cols"] = np.broadcast_to((a[None, :] // LS == np.arange(BS)[:, None]).reshape(1, -1), (P, BS * P))
    f["far_mask"] = np.where((row >= 64) & (col < 64), NEG, 0.0)
    f["own_mask"] = np.where((row < 64) & (col >= 64), NEG, 0.0)
    f["new_mask"] = np.concatenate([np.where(4 * g + row // 32 == col // LS, 0.0, NEG) for g in range(2)], 1)
    u = {}
    up = [(row // (2 * s) == col // (2 * s)) & (row % (2 * s) < s) & (col % (2 * s) >= s) for s in LEVELS]
    u["up"] = np.concatenate(up + [np.eye(P) > 0], 1)
    u["low"] = np.concatenate([m.T for m in up], 1)
    where, n = {}, 0
    for k, v in f.items():
        where[k] = (n, n + v.shape[1])
        n += v.shape[1]
    m = 0
    for k, v in u.items():
        where[k] = (m, m + v.shape[1])
        m += v.shape[1]
    return (np.concatenate([v.astype(np.float32) for v in f.values()], 1),
            np.concatenate([v.astype(np.float32) for v in u.values()], 1), where)


def bc(ap, shape):
    return ap.broadcast_to(shape)


class Env:

    def __init__(self, nc, dram):
        self.nc, self.d = nc, dram
        self.top = ExitStack()
        self.scr = {}
        self.times = {}

    def apart(self, eng):
        eng.sem_inc(self.passed, 1)

    @contextmanager
    def stage(self):
        before = self.nc.snapshot_sems()
        with ExitStack() as ctx:
            yield ctx
        self.nc.clear_and_free_semaphores(self.nc.allocated_since(before))
        self.nc.all_engine_barrier()

    def own(self, name):
        n = self.times[name] = self.times.get(name, 0) + 1
        return name if n == 1 else f"{name}_{n}"

    def sb(self, ctx, name, shape, dt=F32):
        return ctx.enter_context(self.nc.sbuf_tensor(self.own(name), shape, dt))

    def sem(self, ctx, *names):
        out = [self.nc.alloc_semaphore(name=self.own(x)) for x in names]
        return out if len(out) > 1 else out[0]

    def split(self, ctx, name):
        return tuple(self.sb(ctx, f"{name}_{part}", [P, KT, T], F32R) for part in ("high", "low"))

    def dram(self, name, shape, kind="Internal"):
        self.scr[name] = self.nc.dram_tensor(f"{name}_dram", shape, F32, kind=kind).ap()
        return self.scr[name]



def load_x(e):
    nc, d, PS, xT, ident = e.nc, e.d, e.PS, e.xT, e.ident
    xp = d["x_prompt"].rearrange("a s d -> (a s) d")
    xs = d["x_sample"].rearrange("b s d -> (b s) d")
    with e.stage() as ctx:
        tok = e.sb(ctx, "x_tok", [P, 2, D])
        masks = e.sb(ctx, "mask_floats", [P, e.cu.shape[1]])
        gain_rows = e.sb(ctx, "gain_rows", [len(e.gain_of) * KT, P])
        gains_in, gains_turned, gains_kept, masks_kept = e.sem(ctx, "gains_in", "gains_turned", "gains_kept", "masks_kept")
        consts, in0, in1, turned, saved = e.sem(ctx, "consts_in", "x_in0", "x_in1", "x_turned", "xT_saved")
        low_out, high_out = e.sem(ctx, "x_low_out", "x_high_out")
        x_in = [in0, in1]
        block = ctx.enter_context(nc.Block())

        @block.sync
        def _(sp):
            sp.dma_start(e.cf[:], d["const_f"]).then_inc(consts, 16)
            sp.dma_start(masks[:], d["const_u"]).then_inc(consts, 16)
            for n, gain in enumerate(e.gain_of.values()):
                sp.dma_start(gain_rows[n * KT:(n + 1) * KT], gain.rearrange("(k p) -> k p", p=P)).then_inc(gains_in, 16)
            for s in range(2):
                sp.dma_start(tok[:, s], xp[s * P:(s + 1) * P]).then_inc(x_in[s], 16)
            with sp.Fori(1, NPT // 2) as i:
                for s in range(2):
                    sp.wait_ge(turned, i * 4 - 2 + 2 * s)
                    sp.dma_start(tok[:, s], xp[ds(i * 256 + s * P, P)]).then_inc(x_in[s], 16)
            sp.wait_ge(turned, 2 * NPT - 2)
            sp.dma_start(tok[:, 0], xs).then_inc(x_in[0], 16)
            sp.wait_ge(low_out, NT + 2)
            sp.wait_ge(high_out, NT + 2)
            sp.dma_start(e.scr["xT"].rearrange("(k p) t -> p k t", p=P), xT[:]).then_inc(saved, 16)
            sp.wait_ge(saved, 16)

        @block.tensor
        def _(pe):
            pe.wait_ge(consts, 32)
            pe.wait_ge(gains_in, 16 * len(e.gain_of))
            r = len(e.gain_of) * KT
            pe.transpose(PS[:, 7, 0:r], gain_rows[:], ident[0:r, 0:r]).then_inc(gains_turned, 1)

            def tile(i, s):
                t = i * 2 + s
                pe.wait_ge(x_in[s], (i + 1) * 16)
                for h, out in enumerate((low_out, high_out)):
                    pe.wait_ge(out, t + 1)
                    for k in range(4):
                        m = pe.transpose(PS[:, 2 * s + h, k * P:(k + 1) * P],
                                         tok[:, s, (h * 4 + k) * P:(h * 4 + k + 1) * P], ident)
                    m.then_inc(turned, 1)
            with pe.Fori(0, NPT // 2) as i:
                tile(i, 0)
                tile(i, 1)
            tile(NPT // 2, 0)

        def copies(eng, copy, h, out):
            eng.sem_inc(out, 2)

            def tile(i, s):
                t = i * 2 + s
                eng.wait_ge(turned, t * 2 + h + 1)
                copy(xT[:, 4 * h:4 * h + 4, ds(t * P, P)],
                     PS[:, 2 * s + h, :].rearrange("p (k t) -> p k t", k=4)).then_inc(out, 1)
            with eng.Fori(0, NPT // 2) as i:
                tile(i, 0)
                tile(i, 1)
            tile(NPT // 2, 0)

        @block.scalar
        def _(act):
            copies(act, nc.scalar.copy, 0, low_out)

        @block.vector
        def _(dve):
            dve.wait_ge(consts, 32)
            nc.vector.tensor_copy(e.cu[:], masks[:]).then_inc(masks_kept, 1)
            dve.wait_ge(gains_turned, 1)
            nc.vector.tensor_copy(e.gains[:], PS[:, 7, 0:len(e.gain_of) * KT]).then_inc(gains_kept, 1)
            copies(dve, nc.vector.tensor_copy, 1, high_out)


def rmsnorm(e, gain, dst):
    nc, PS, xT = e.nc, e.PS, e.xT
    split = isinstance(dst, tuple)
    with e.stage() as ctx:
        at = list(e.gain_of).index(gain) * KT
        g = e.gains[:, at:at + KT]
        sq = e.sb(ctx, "norm_sq", [P, 2, T])
        acc = e.sb(ctx, "norm_acc", [P, T])
        rstd = e.sb(ctx, "norm_rstd", [P, T])
        eps = e.sb(ctx, "norm_eps", [P, 1])
        eps_set, squared, added, summed, rooted, inverted, normed, high, low = e.sem(
            ctx, "eps_set", "squared", "added", "summed", "rooted", "inverted", "normed", "norm_high", "norm_low")
        block = ctx.enter_context(nc.Block())
        ps = PS[:, 0:G, 0:GN]

        @block.scalar
        def _(act):
            for k in range(KT):
                if k >= 2:
                    act.wait_ge(added, k - 1)
                nc.scalar.activation(sq[:, k % 2], xT[:, k], ACT.Square).then_inc(squared, 1)
            act.wait_ge(eps_set, 1)
            for j in range(G):
                act.wait_ge(summed, j + 1)
                nc.scalar.activation(rstd[:, j * GN:(j + 1) * GN], PS[:, j, 0:GN], ACT.Sqrt,
                                     scale=1.0 / D, bias=eps[:, 0:1]).then_inc(rooted, 1)
            if split:
                for k in range(KT):
                    act.wait_ge(normed, k + 1)
                    nc.scalar.copy(dst[0][:, k], sq[:, k % 2]).then_inc(high, 1)

        @block.tensor
        def _(pe):
            pe.wait_ge(added, KT)
            for j in range(G):
                nc.tensor.matmul(PS[:, j, 0:GN], e.ones, acc[:, j * GN:(j + 1) * GN], start=True, stop=True
                                 ).then_inc(summed, 1)

        @block.vector
        def _(dve):
            nc.vector.memset(eps[:], EPS).then_inc(eps_set, 1)
            for k in range(KT):
                dve.wait_ge(squared, k + 1)
                if k == 0:
                    nc.vector.tensor_copy(acc[:], sq[:, 0]).then_inc(added, 1)
                else:
                    dve.wait_ge(added, k)
                    nc.vector.tensor_tensor(acc[:], acc[:], sq[:, k % 2], ALU.add).then_inc(added, 1)
            for j in range(G):
                dve.wait_ge(rooted, j + 1)
                r = rstd[:, j * GN:(j + 1) * GN]
                nc.vector.reciprocal(r, r).then_inc(inverted, 1)
            dve.wait_ge(inverted, G)
            dve.wait_ge(added, KT)
            for k in range(KT):
                if split and k >= 2:
                    dve.wait_ge(high, k - 1)
                    dve.wait_ge(low, k - 1)
                nc.vector.scalar_tensor_tensor(out=sq[:, k % 2] if split else dst[:, k], in0=xT[:, k],
                                               scalar=g[:, k:k + 1], in1=rstd[:],
                                               op0=ALU.mult, op1=ALU.mult).then_inc(normed, 1)

        if split:
            @block.gpsimd
            def _(pool):
                for k in range(KT):
                    pool.wait_ge(high, k + 1)
                    nc.gpsimd.tensor_tensor(dst[1][:, k], sq[:, k % 2], dst[0][:, k], ALU.subtract).then_inc(low, 1)


def reload_x(e):
    with e.stage() as ctx:
        loaded = e.sem(ctx, "xT_loaded")
        block = ctx.enter_context(e.nc.Block())

        @block.sync
        def _(sp):
            sp.dma_start(e.xT[:], e.scr["xT"].rearrange("(k p) t -> p k t", p=P)).then_inc(loaded, 16)
            sp.wait_ge(loaded, 16)


def save_x(e):
    with e.stage() as ctx:
        saved = e.sem(ctx, "xT_saved")
        block = ctx.enter_context(e.nc.Block())

        @block.sync
        def _(sp):
            sp.dma_start(e.scr["xT"].rearrange("(k p) t -> p k t", p=P), e.xT[:]).then_inc(saved, 16)
            sp.wait_ge(saved, 16)


def rows_split(nc, out, hT, t, w, k, first, last):
    c = slice(t * P, (t + 1) * P)
    for p, (h, x) in enumerate(((0, 0), (0, 1), (1, 0))):
        m = nc.tensor.matmul(out, hT[h][:, k, c], w[:, x, k], start=first and p == 0, stop=last and p == 2)
    return m


def product_split(nc, PS, banks, w, src, kts):
    last = len(kts) - 1
    for n, k in enumerate(kts):
        (wh, wl) = w(k)
        for p, j in [(p, j) for p in range(3) for j in range(G)]:
            sh, sl = src(k, j)
            m = nc.tensor.matmul(PS[:, banks + j, 0:GN], wl if p == 2 else wh, sl if p == 1 else sh,
                                 start=(n == 0 and p == 0), stop=(n == last and p == 2))
    return m


def split_tile(e, pool, i, s, raw, ws, w_in, mm, high, split):
    n = i * 2 + s
    pool.wait_ge(w_in[s], (i + 1) * 16)
    pool.wait_ge(mm, n + 1)
    e.apart(pool)
    e.nc.gpsimd.tensor_copy(ws[:, s, 0], raw[:, s]).then_inc(high, 1)
    pool.wait_ge(high, n + 1)
    e.apart(pool)
    e.nc.gpsimd.tensor_tensor(ws[:, s, 1], raw[:, s], ws[:, s, 0], ALU.subtract).then_inc(split, 1)


def parts(hT):
    return lambda k, j: (hT[0][:, k, j * GN:(j + 1) * GN], hT[1][:, k, j * GN:(j + 1) * GN])


def groups(ap):
    return ap.rearrange("p (g n) -> p g n", g=G)



def ffn(e, w_gu, w_down, hT):
    nc, PS, xT = e.nc, e.PS, e.xT
    wv = w_gu.rearrange("(k p) n -> p k n", p=P)
    with e.stage() as ctx:
        raw = e.sb(ctx, "w_gu_raw", [P, 2, KT, P])
        rawd = e.sb(ctx, "w_down_raw", [P, 2, D])
        w = e.sb(ctx, "w_gu_split", [P, 2, 2, KT, P], F32R)
        wd = e.sb(ctx, "w_down_split", [P, 2, 2, D], F32R)
        sg = e.sb(ctx, "ffn_act", [P, T])
        act_t = e.sb(ctx, "ffn_act_split", [P, 2, 2, T], F32R)
        g_in, u_in, d_in, gu_split, d_split, gu_mm, down_mm, silu_done, multiplied, act_hi, act_lo, x_added, hi_done = e.sem(
            ctx, "w_gate_in", "w_up_in", "w_down_in", "gu_split", "down_split", "gu_mm", "down_mm", "silu_done",
            "multiplied", "act_hi", "act_lo", "x_added", "w_hi_done")
        gu_in = [g_in, u_in]
        block = ctx.enter_context(nc.Block())
        A, B = 0, 3

        @block.sync
        def _(sp):
            def gate_up(i, f):
                for s in range(2):
                    if not isinstance(i, int) or f:
                        sp.wait_ge(gu_split, i * 4 + f * 2 + s - 1)
                    sp.dma_start(raw[:, s], wv[:, :, ds(i * 256 + s * FF + f * P, P)]).then_inc(gu_in[s], 16)

            def down(i):
                sp.wait_ge(d_split, i + 1)
                sp.dma_start(rawd[:], w_down[ds(i * 256, 256)].rearrange("(k p) n -> p k n", p=P)).then_inc(d_in, 16)
            gate_up(0, 0)
            with sp.Fori(0, FC - 1) as i:
                gate_up(i, 1)
                down(i)
                gate_up(i + 1, 0)
            gate_up(FC - 1, 1)
            down(FC - 1)

        @block.gpsimd
        def _(pool):
            p = nc.gpsimd
            pool.sem_inc(d_split, 1)

            def gate_up(i, f):
                for s in range(2):
                    pool.wait_ge(gu_in[s], (i * 2 + f + 1) * 16)
                    pool.wait_ge(gu_mm, i * 4 + f * 2 + s + 1)
                    e.apart(pool)
                    p.tensor_copy(w[:, s, 0], raw[:, s]).then_inc(hi_done, 1)
                    pool.wait_ge(hi_done, i * 5 + 2 * f + s + 1)
                    e.apart(pool)
                    p.tensor_tensor(w[:, s, 1], raw[:, s], w[:, s, 0], ALU.subtract).then_inc(gu_split, 1)

            def down(i):
                pool.wait_ge(d_in, (i + 1) * 16)
                pool.wait_ge(down_mm, (i + 1) * KT)
                e.apart(pool)
                p.tensor_copy(wd[:, 0], rawd[:]).then_inc(hi_done, 1)
                pool.wait_ge(hi_done, i * 5 + 5)
                e.apart(pool)
                p.tensor_tensor(wd[:, 1], rawd[:], wd[:, 0], ALU.subtract).then_inc(d_split, 1)
            gate_up(0, 0)
            with pool.Fori(0, FC - 1) as i:
                gate_up(i, 1)
                down(i)
                gate_up(i + 1, 0)
            gate_up(FC - 1, 1)
            down(FC - 1)

        @block.tensor
        def _(pe):
            pe.sem_inc(gu_mm, 2)
            pe.sem_inc(down_mm, KT)

            def gate_up(i, f):
                for s, banks in enumerate((A, B)):
                    pe.wait_ge(gu_split, i * 4 + f * 2 + s + 1)
                    if f == 0:
                        pe.wait_ge((silu_done, multiplied)[s], i * 2 + 1)
                    elif isinstance(i, int) and i == 0:
                        pe.wait_ge((silu_done, multiplied)[s], 2)
                    else:
                        pe.wait_ge(x_added, i * KT + 7 + s)
                    product_split(nc, PS, banks, lambda k: (w[:, s, 0, k], w[:, s, 1, k]),
                                  parts(hT), range(KT)).then_inc(gu_mm, 1)

            def down(i, after):
                pe.wait_ge(d_split, i + 2)
                pe.wait_ge(act_lo, i * 2 + 3)
                for n in range(KT):
                    if n < 2:
                        pe.wait_ge((silu_done, multiplied)[n], after + 1)
                    else:
                        pe.wait_ge(x_added, i * KT + 8 + n - 1)
                    c = slice(n * P, (n + 1) * P)
                    product_split(nc, PS, (A, B)[n % 2], lambda k: (wd[:, 0, k, c], wd[:, 1, k, c]),
                                  parts((act_t[:, 0], act_t[:, 1])), range(2)).then_inc(down_mm, 1)
            gate_up(0, 0)
            gate_up(0, 1)
            with pe.Fori(1, FC) as i:
                gate_up(i, 0)
                down(i - 1, i * 2 + 1)
                gate_up(i, 1)
            down(FC - 1, FC * 2)

        @block.scalar
        def _(act):
            act.sem_inc(silu_done, 1)
            with act.Fori(0, FC) as i:
                for f in range(2):
                    act.wait_ge(gu_mm, i * 4 + f * 2 + 3)
                    act.wait_ge(act_lo, i * 2 + f + 1)
                    nc.scalar.activation(groups(sg[:]), PS[:, A:A + G, 0:GN], ACT.Silu).then_inc(silu_done, 1)
                    act.wait_ge(multiplied, i * 2 + f + 2)
                    act.wait_ge(down_mm, (i + 1) * KT)
                    nc.scalar.copy(act_t[:, 0, f], sg[:]).then_inc(act_hi, 1)

        @block.vector
        def _(dve):
            dve.sem_inc(x_added, 8)
            dve.sem_inc(act_lo, 1)
            dve.sem_inc(multiplied, 1)

            def add(i):
                dve.wait_ge(x_added, i * KT + 8)
                for n in range(KT):
                    dve.wait_ge(down_mm, i * KT + n + 9)
                    b = (A, B)[n % 2]
                    nc.vector.tensor_tensor(groups(xT[:, n]), groups(xT[:, n]), PS[:, b:b + G, 0:GN],
                                            ALU.add).then_inc(x_added, 1)

            def activation(i, f, between=None):
                dve.wait_ge(gu_mm, i * 4 + f * 2 + 4)
                dve.wait_ge(silu_done, i * 2 + f + 2)
                nc.vector.tensor_tensor(groups(sg[:]), groups(sg[:]), PS[:, B:B + G, 0:GN], ALU.mult).then_inc(multiplied, 1)
                if between:
                    between()
                dve.wait_ge(act_hi, i * 2 + f + 1)
                nc.vector.tensor_tensor(act_t[:, 1, f], sg[:], act_t[:, 0, f], ALU.subtract).then_inc(act_lo, 1)
            activation(0, 0)
            activation(0, 1)
            with dve.Fori(1, FC) as i:
                activation(i, 0, lambda: add(i - 1))
                activation(i, 1)
            add(FC - 1)


def project_add(e, w, src, pair):
    nc, PS, xT = e.nc, e.PS, e.xT
    wv = w.rearrange("(k p) n -> p k n", p=P)
    hi, lo = pair
    with e.stage() as ctx:
        raw = e.sb(ctx, "w_raw", [P, 2, KT, P])
        ws = e.sb(ctx, "w_split", [P, 2, 2, KT, P], F32R)
        in0, in1, high, split, src_high, src_low, mm, added = e.sem(
            ctx, "w_in0", "w_in1", "w_high", "w_low", "src_high", "src_low", "out_mm", "out_added")
        w_in = [in0, in1]
        block = ctx.enter_context(nc.Block())

        @block.sync
        def _(sp):
            for s in range(2):
                sp.dma_start(raw[:, s], wv[:, :, s * P:(s + 1) * P]).then_inc(w_in[s], 16)
            with sp.Fori(1, KT // 2) as i:
                for s in range(2):
                    sp.wait_ge(split, i * 2 - 1 + s)
                    sp.dma_start(raw[:, s], wv[:, :, ds(i * 256 + s * P, P)]).then_inc(w_in[s], 16)

        @block.gpsimd
        def _(pool):
            with pool.Fori(0, KT // 2) as i:
                for s in range(2):
                    split_tile(e, pool, i, s, raw, ws, w_in, mm, high, split)

        @block.tensor
        def _(pe):
            pe.sem_inc(mm, 2)

            def multiply(i, s, first=False):
                pe.wait_ge(split, i * 2 + s + 1)
                pe.wait_ge(added, i * 2 + s + 1)

                def weights(k):
                    if first:
                        pe.wait_ge(src_low, k + 1)
                    return ws[:, s, 0, k], ws[:, s, 1, k]
                product_split(nc, PS, 3 * s, weights, parts(pair), range(KT)).then_inc(mm, 1)
            multiply(0, 0, src is not None)
            multiply(0, 1)
            with pe.Fori(1, KT // 2) as i:
                multiply(i, 0)
                multiply(i, 1)

        if src is not None:
            @block.scalar
            def _(act):
                for k in range(KT):
                    nc.scalar.copy(hi[:, k], src[:, k]).then_inc(src_high, 1)

        @block.vector
        def _(dve):
            dve.sem_inc(added, 2)
            if src is not None:
                for k in range(KT):
                    dve.wait_ge(src_high, k + 1)
                    nc.vector.tensor_tensor(lo[:, k], src[:, k], hi[:, k], ALU.subtract).then_inc(src_low, 1)
            with dve.Fori(0, KT // 2) as i:
                for s in range(2):
                    dve.wait_ge(mm, i * 2 + s + 3)
                    x = xT[:, ds(i * 2 + s, 1)].rearrange("p o (g n) -> p (o g) n", g=G)
                    nc.vector.tensor_tensor(x, x, PS[:, 3 * s:3 * s + G, 0:GN], ALU.add).then_inc(added, 1)


def write_y(e, yT):
    nc, d, PS, ident = e.nc, e.d, e.PS, e.ident
    yp = d["y_prompt"].rearrange("a s d -> (a s) d")
    ys = d["y_sample"].rearrange("b s d -> (b s) d")
    with e.stage() as ctx:
        stage = e.sb(ctx, "y_stage", [P, 2, P * KT])
        tok = e.sb(ctx, "y_tok", [P, 2, D])
        staged, turned, low, high, o0, o1 = e.sem(ctx, "y_staged", "y_turned", "y_low", "y_high", "y_out0", "y_out1")
        outs = [o0, o1]
        block = ctx.enter_context(nc.Block())

        def each(eng, body):
            with eng.Fori(0, NPT // 2) as i:
                body(i, 0)
                body(i, 1)
            body(NPT // 2, 0)

        @block.gpsimd
        def _(pool):
            def tile(i, s):
                t = i * 2 + s
                pool.wait_ge(turned, t * 2 + 2)
                e.apart(pool)
                nc.gpsimd.tensor_copy(stage[:, s].rearrange("p (k t) -> p k t", k=KT),
                                      yT[:, :, ds(t * P, P)]).then_inc(staged, 1)
            each(pool, tile)

        @block.tensor
        def _(pe):
            pe.sem_inc(turned, 4)

            def tile(i, s):
                t = i * 2 + s
                pe.wait_ge(staged, t + 1)
                for h, out in enumerate((low, high)):
                    pe.wait_ge(out, t + 1)
                    for k in range(4):
                        m = pe.transpose(PS[:, 2 * s + h, k * P:(k + 1) * P],
                                         stage[:, s, (h * 4 + k) * P:(h * 4 + k + 1) * P], ident)
                    m.then_inc(turned, 1)
            each(pe, tile)

        def copies(eng, copy, h, out):
            eng.sem_inc(out, 2)

            def tile(i, s):
                t = i * 2 + s
                eng.wait_ge(turned, t * 2 + h + 5)
                eng.wait_ge(outs[s], (i + 1) * 16)
                copy(tok[:, s, h * 512:(h + 1) * 512], PS[:, 2 * s + h, :]).then_inc(out, 1)
            each(eng, tile)

        @block.scalar
        def _(act):
            copies(act, nc.scalar.copy, 0, low)

        @block.vector
        def _(dve):
            copies(dve, nc.vector.tensor_copy, 1, high)

        @block.sync
        def _(sp):
            for s in range(2):
                sp.sem_inc(outs[s], 16)

            def tile(i, s):
                t = i * 2 + s
                sp.wait_ge(low, t + 3)
                sp.wait_ge(high, t + 3)
            with sp.Fori(0, NPT // 2) as i:
                for s in range(2):
                    tile(i, s)
                    sp.dma_start(yp[ds(i * 256 + s * P, P)], tok[:, s]).then_inc(outs[s], 16)
            tile(NPT // 2, 0)
            sp.dma_start(ys, tok[:, 0]).then_inc(outs[0], 16)
            sp.wait_ge(outs[0], 16 * (NPT // 2 + 2))
            sp.wait_ge(outs[1], 16 * (NPT // 2 + 1))

def conv_projection(e, hT):
    nc, d, PS, ident = e.nc, e.d, e.PS, e.ident
    wv = d["ab_w_in"][0].rearrange("(k p) n -> p k n", p=P)
    rows = e.scr["qkv"].rearrange("(t p) c -> p t c", p=P)
    W = 4
    NS = BS * (W - 1)
    with e.stage() as ctx:
        wraw = e.sb(ctx, "w_conv_in", [P, 2, KT, P])
        ws = e.sb(ctx, "w_conv_split", [P, 2, 2, KT, P], F32R)
        srow = e.sb(ctx, "state_rows", [NS + W, QKV])
        taps = e.sb(ctx, "state_taps", [P, NCB, NS + W])
        raw = e.sb(ctx, "conv_raw", [P, 2, LP + W - 1])
        raws = e.sb(ctx, "conv_raw_s", [P, 2, BS, LS + W - 1])
        acc = e.sb(ctx, "conv_acc", [P, 2, T])
        sil = e.sb(ctx, "conv_silu", [P, 2, T])
        tok = e.sb(ctx, "conv_tok", [P, 2, NT, P])
        sq = e.sb(ctx, "conv_sq", [P, 2, NT * P])
        newest = e.sb(ctx, "conv_newest", [P, 2, NS + W - 1])
        newrows = e.sb(ctx, "newest_rows", [NS + W - 1, QKV])
        (state_in, state_turned, state_kept, w0, w1, mm, raw_ready, state_put, conv_step, conv_done, gathered, silu_done,
         turned, tok_ready, squared, ss_done, stored0, stored1, rows_out, new_turned, new_kept, pad, w_high, w_low) = e.sem(
            ctx, "state_in", "state_turned", "state_kept", "w_in0", "w_in1", "conv_mm", "raw_ready", "state_put",
            "conv_step", "conv_done", "gathered", "silu_done", "tok_turned", "tok_ready", "squared", "ss_done",
            "tok_stored0", "tok_stored1", "newest_out", "new_turned", "new_kept", "pad_set",
            "w_high", "w_low")
        w_in, stored = [w0, w1], [stored0, stored1]
        NP2 = NCB // 2
        block = ctx.enter_context(nc.Block())

        @block.sync
        def _(sp):
            sp.dma_start(srow[0:NS], d["state_dn_conv"][0].rearrange("b w c -> (b w) c")).then_inc(state_in, 16)
            sp.dma_start(srow[NS:NS + W], d["dn_conv_w"][0]).then_inc(state_in, 16)
            for s in range(2):
                sp.sem_inc(stored[s], 16)
            with sp.Fori(0, NP2) as i:
                for s in range(2):
                    sp.wait_ge(tok_ready, i * 6 + s * 3 + 5)
                    sp.dma_start(rows[:, :, ds(i * 256 + s * P, P)], tok[:, s]).then_inc(stored[s], 16)
            sp.wait_ge(stored[0], 16 * (NP2 + 1))
            sp.wait_ge(stored[1], 16 * (NP2 + 1))
            sp.wait_ge(new_kept, NCB)
            nw = newrows[:]
            sp.dma_start(d["conv_p"].rearrange("n b w c -> (n b w) c"), nw[0:W - 1]).then_inc(rows_out, 16)
            sp.dma_start(d["conv_s"].rearrange("n b w c -> (n b w) c"), nw[W - 1:NS + W - 1]).then_inc(rows_out, 16)
            sp.wait_ge(rows_out, 32)

        @block.gpsimd
        def _(pool):
            pool.sem_inc(squared, 2)

            def square(i, s):
                pool.wait_ge(tok_ready, i * 6 + s * 3 + 5)
                pool.wait_ge(ss_done, i * 2 + s + 1)
                e.apart(pool)
                nc.gpsimd.tensor_tensor(sq[:, s], tok[:, s].rearrange("p t c -> p (t c)"),
                                        tok[:, s].rearrange("p t c -> p (t c)"), ALU.mult).then_inc(squared, 1)
            for s in range(2):
                pool.dma_start(wraw[:, s], wv[:, :, s * P:(s + 1) * P]).then_inc(w_in[s], 16)

            def split(i, s, more=True):
                split_tile(e, pool, i, s, wraw, ws, w_in, mm, w_high, w_low)
                if more:
                    pool.wait_ge(w_low, i * 2 + s + 1)
                    e.apart(pool)
                    pool.dma_start(wraw[:, s], wv[:, :, ds(i * 256 + 256 + s * P, P)]).then_inc(w_in[s], 16)
            split(0, 0)
            split(0, 1)
            with pool.Fori(0, NP2 - 2) as i:
                for s in range(2):
                    split(i + 1, s)
                    square(i, s)
            for s in range(2):
                split(NP2 - 1, s, False)
                square(NP2 - 2, s)
            square(NP2 - 1, 0)
            square(NP2 - 1, 1)

        @block.tensor
        def _(pe):
            pe.sem_inc(new_turned, 2)
            pe.sem_inc(mm, 2)
            pe.wait_ge(state_in, 32)
            for n in range(NCB):
                m = pe.transpose(PS[:, 6, n * (NS + W):(n + 1) * (NS + W)], srow[:, n * P:(n + 1) * P],
                                 ident[0:NS + W, 0:NS + W])
            m.then_inc(state_turned, 1)

            def multiply(i, s):
                pe.wait_ge(w_low, i * 2 + s + 1)
                pe.wait_ge(raw_ready, i * 2 + s + 1)
                product_split(nc, PS, 3 * s, lambda k: (ws[:, s, 0, k], ws[:, s, 1, k]), parts(hT),
                              range(KT)).then_inc(mm, 1)

            def turn(i, s):
                pe.wait_ge(silu_done, i * 2 + s + 3)
                for c in range(3):
                    bank = 6 + (s * 3 + c) % 2
                    pe.wait_ge(tok_ready, i * 6 + s * 3 + c + 1)
                    if c == 2:
                        pe.wait_ge(gathered, i * 2 + s + 1)
                        pe.transpose(PS[0:NS + W - 1, bank, 384:512], newest[:, s], ident).then_inc(new_turned, 1)
                    for t in range(3):
                        m = pe.transpose(PS[:, bank, t * P:(t + 1) * P], sil[:, s, (3 * c + t) * P:(3 * c + t + 1) * P],
                                         ident)
                    m.then_inc(turned, 1)

            pe.wait_ge(state_kept, 1)
            multiply(0, 0)
            with pe.Fori(0, NP2 - 1) as i:
                multiply(i, 1)
                turn(i, 0)
                multiply(i + 1, 0)
                turn(i, 1)
            multiply(NP2 - 1, 1)
            turn(NP2 - 1, 0)
            turn(NP2 - 1, 1)

        @block.scalar
        def _(act):
            act.sem_inc(raw_ready, 2)
            act.sem_inc(tok_ready, 2)
            act.sem_inc(silu_done, 2)
            act.wait_ge(state_turned, 1)
            nc.scalar.copy(taps[:], PS[:, 6, 0:NCB * (NS + W)].rearrange("p (n r) -> p n r", n=NCB)).then_inc(state_kept, 1)
            act.wait_ge(pad, 1)

            def copy_raw(i, s):
                act.wait_ge(mm, i * 2 + s + 3)
                act.wait_ge(conv_done, i * 2 + s + 1)
                b = 3 * s
                o = W - 1
                nc.scalar.copy(raw[:, s, o:o + 2 * GN].rearrange("p (g n) -> p g n", g=2), PS[:, b:b + 2, 0:GN])
                nc.scalar.copy(raw[:, s, o + 2 * GN:o + LP], PS[:, b + 2, 0:LP - 2 * GN])
                nc.scalar.copy(raws[:, s, :, o:], PS[:, b + 2, LP - 2 * GN:GN].rearrange("p (b l) -> p b l", b=BS)
                               ).then_inc(raw_ready, 1)

            def silu(i, s):
                act.wait_ge(conv_step, (i * 2 + s) * 8 + 8)
                nc.scalar.activation(sil[:, s], acc[:, s], ACT.Silu).then_inc(silu_done, 1)

            def copy_tok(i, s):
                act.wait_ge(stored[s], (i + 1) * 16)
                act.wait_ge(squared, i * 2 + s + 1)
                for c in range(3):
                    bank = 6 + (s * 3 + c) % 2
                    act.wait_ge(turned, i * 6 + s * 3 + c + 1)
                    if c == 2:
                        nc.scalar.copy(newrows[:, ds(i * 256 + s * P, P)],
                                       PS[0:NS + W - 1, bank, 384:512]).then_inc(new_kept, 1)
                    nc.scalar.copy(tok[:, s, 3 * c:3 * c + 3], PS[:, bank, 0:384].rearrange("p (t c) -> p t c", t=3)
                                   ).then_inc(tok_ready, 1)

            copy_raw(0, 0)
            with act.Fori(0, NP2 - 1) as i:
                silu(i, 0)
                copy_raw(i, 1)
                copy_tok(i, 0)
                silu(i, 1)
                copy_raw(i + 1, 0)
                copy_tok(i, 1)
            silu(NP2 - 1, 0)
            copy_raw(NP2 - 1, 1)
            copy_tok(NP2 - 1, 0)
            silu(NP2 - 1, 1)
            copy_tok(NP2 - 1, 1)

        @block.vector
        def _(dve):
            dve.sem_inc(conv_done, 2)
            dve.sem_inc(ss_done, 2)
            nc.vector.memset(raw[:, :, 0:W - 1], 0.0).then_inc(pad, 1)
            dve.wait_ge(state_kept, 1)
            dve.wait_ge(pad, 1)

            def conv(i, s):
                n = i * 2 + s
                dve.wait_ge(conv_done, n + 1)
                nc.vector.tensor_copy(raws[:, s, :, 0:W - 1],
                                      taps[:, ds(n, 1), 0:NS].rearrange("p o (b w) -> p (o b) w", b=BS)).then_inc(state_put, 1)
                dve.wait_ge(raw_ready, n + 3)
                dve.wait_ge(state_put, n + 1)
                dve.wait_ge(silu_done, n + 1)
                ap, as_ = acc[:, s, 0:LP], acc[:, s, LP:T].rearrange("p (b l) -> p b l", b=BS)
                for w in range(W):
                    c = taps[:, ds(n, 1), NS + w:NS + w + 1].rearrange("p o w -> p (o w)")
                    if w == 0:
                        nc.vector.tensor_scalar(ap, raw[:, s, 0:LP], c, None, ALU.mult).then_inc(conv_step, 1)
                        nc.vector.tensor_scalar(as_, raws[:, s, :, 0:LS], c, None, ALU.mult).then_inc(conv_step, 1)
                    else:
                        dve.wait_ge(conv_step, n * 8 + 2 * w - 1)
                        nc.vector.scalar_tensor_tensor(out=ap, in0=raw[:, s, w:w + LP], scalar=c, in1=ap,
                                                       op0=ALU.mult, op1=ALU.add).then_inc(conv_step, 1)
                        dve.wait_ge(conv_step, n * 8 + 2 * w)
                        nc.vector.scalar_tensor_tensor(out=as_, in0=raws[:, s, :, w:w + LS], scalar=c, in1=as_,
                                                       op0=ALU.mult, op1=ALU.add).then_inc(conv_step, 1)
                dve.wait_ge(new_turned, n + 1)
                nc.vector.tensor_copy(newest[:, s, 0:W - 1], raw[:, s, LP:LP + W - 1])
                nc.vector.tensor_copy(newest[:, s, W - 1:].rearrange("p (b w) -> p b w", b=BS),
                                      raws[:, s, :, LS:]).then_inc(gathered, 1)
                dve.wait_ge(gathered, n + 1)
                dve.sem_inc(conv_done, 1)

            def sums(i, s):
                n = i * 2 + s
                dve.wait_ge(squared, n + 3)
                nc.vector.reduce_sum(e.ss[:, :, ds(n * 2, 2)], sq[:, s].rearrange("p (t h c) -> p t h c", t=NT, h=2),
                                     AX_X).then_inc(ss_done, 1)

            conv(0, 0)
            with dve.Fori(0, NP2 - 1) as i:
                conv(i, 1)
                sums(i, 0)
                conv(i + 1, 0)
                sums(i, 1)
            conv(NP2 - 1, 1)
            sums(NP2 - 1, 0)
            sums(NP2 - 1, 1)


def rest_projection(e, hT):
    nc, d, PS = e.nc, e.d, e.PS
    wv = d["ab_w_in"][0].rearrange("(k p) n -> p k n", p=P)
    rows = e.scr["rest"]
    with e.stage() as ctx:
        raw = e.sb(ctx, "w_rest_raw", [P, 2, KT // 2, 512])
        ws = e.sb(ctx, "w_rest_split", [P, 2, 2, KT, 512], F32R)
        wm = e.sb(ctx, "w_misc", [P, KT, NMISC])
        wms = e.sb(ctx, "w_misc_split", [P, 2, KT, NMISC], F32R)
        out = e.sb(ctx, "rest_rows", [P, 4, 512])
        in0, in1, w_high, w_low, misc_in, wm_zero, misc_mm, misc_kept, mm, copied, s0, s1, s2, s3 = e.sem(
            ctx, "w_in0", "w_in1", "w_high", "w_low", "misc_in", "misc_zero", "misc_mm", "misc_kept", "rest_mm",
            "rest_copied", "rest_out0", "rest_out1", "rest_out2", "rest_out3")
        w_in, stored = [in0, in1], [s0, s1, s2, s3]
        block = ctx.enter_context(nc.Block())
        N = 2 * NT
        COLS = [COL_GATE, COL_GQK, 2 * COL_GATE, COL_GQK + 512]

        @block.gpsimd
        def _(pool):
            nc.gpsimd.memset(wm[:], 0.0).then_inc(wm_zero, 1)
            pool.wait_ge(wm_zero, 1)
            pool.dma_start(wm[:, :, 0:RANK], wv[:, :, COL_LR:COL_LR + RANK]).then_inc(misc_in, 16)
            pool.dma_start(wm[:, :, 32:48], wv[:, :, COL_AB:COL_AB + 2 * H]).then_inc(misc_in, 16)

            def load(b, h):
                k = slice(h * (KT // 2), (h + 1) * (KT // 2))
                pool.dma_start(raw[:, h], wv[:, k, COLS[b]:COLS[b] + 512]).then_inc(w_in[h], 16)
            load(0, 0)
            load(0, 1)
            pool.wait_ge(misc_in, 32)
            nc.gpsimd.tensor_copy(wms[:, 0], wm[:]).then_inc(w_high, 1)
            pool.wait_ge(w_high, 1)
            nc.gpsimd.tensor_tensor(wms[:, 1], wm[:], wms[:, 0], ALU.subtract).then_inc(w_low, 1)
            for b in range(4):
                for h in range(2):
                    k = slice(h * (KT // 2), (h + 1) * (KT // 2))
                    n = 2 * b + h
                    pool.wait_ge(w_in[h], 16 * (b + 1))
                    if b >= 2 and h == 0:
                        pool.wait_ge(mm, (b - 1) * NT)
                    nc.gpsimd.tensor_copy(ws[:, b % 2, 0, k], raw[:, h]).then_inc(w_high, 1)
                    pool.wait_ge(w_high, n + 2)
                    nc.gpsimd.tensor_tensor(ws[:, b % 2, 1, k], raw[:, h], ws[:, b % 2, 0, k],
                                            ALU.subtract).then_inc(w_low, 1)
                    if b < 3:
                        pool.wait_ge(w_low, n + 2)
                        load(b + 1, h)

        @block.sync
        def _(sp):
            for s in range(4):
                sp.sem_inc(stored[s], 16)
            with sp.Fori(0, 2) as i:
                for q in range(2):
                    for t in range(NT):
                        n = q * NT + t
                        sp.wait_ge(copied, i * N + n + 4)
                        sp.dma_start(rows[t * P:(t + 1) * P, ds(i + 2 * q, 1)].rearrange("t o c -> t (o c)"),
                                       out[:, n % 2 + 2 * q]).then_inc(stored[n % 2 + 2 * q], 16)
            for s, per in enumerate((5, 4, 4, 5)):
                sp.wait_ge(stored[s], 16 * (2 * per + 1))

        @block.tensor
        def _(pe):
            pe.wait_ge(w_low, 1)
            src = parts(hT)
            for k in range(KT):
                for p in range(3):
                    for j in range(G):
                        m = nc.tensor.matmul(PS[0:NMISC, j, 0:GN], wms[:, int(p == 2), k], src(k, j)[int(p == 1)],
                                             start=(k == 0 and p == 0), stop=(k == KT - 1 and p == 2))
            m.then_inc(misc_mm, 1)
            with pe.Fori(0, 2) as i:
                for q in range(2):
                    for t in range(NT):
                        n = q * NT + t
                        pe.wait_ge(copied, i * N + n + 1)
                        for k in range(KT):
                            if t == 0 and k % (KT // 2) == 0:
                                pe.wait_ge(w_low, i * 4 + 2 * q + k // (KT // 2) + 2)
                            m = rows_split(nc, PS[:, 4 + n % 3, :], hT, t, ws[:, q], k, k == 0, k == KT - 1)
                        m.then_inc(mm, 1)

        @block.scalar
        def _(act):
            act.sem_inc(copied, 3)
            act.wait_ge(misc_mm, 1)
            nc.scalar.copy(groups(e.misc[:]), PS[0:NMISC, 0:G, 0:GN]).then_inc(misc_kept, 1)
            with act.Fori(0, 2) as i:
                for q, f in enumerate((ACT.Silu, ACT.Copy)):
                    for t in range(NT):
                        n = q * NT + t
                        act.wait_ge(mm, i * N + n + 1)
                        slot = n % 2 + 2 * q
                        per = len([m for m in range(q * NT, q * NT + NT) if m % 2 == n % 2])
                        act.wait_ge(stored[slot], i * (16 * per) + 16 * ((n - q * NT) // 2 + 1))
                        nc.scalar.activation(out[:, slot], PS[:, 4 + n % 3, :], f).then_inc(copied, 1)



def token_scalars(e):
    nc, d, PS, ident, misc = e.nc, e.d, e.PS, e.ident, e.misc
    NH, NZ = NT * H, NT * H * GK
    with e.stage() as ctx:
        w2 = e.sb(ctx, "gk_w2", [RANK, H * GK])
        gkb = e.sb(ctx, "gk_b", [1, H * GK])
        alog = e.sb(ctx, "a_log", [P, H])
        dtb = e.sb(ctx, "dt_bias", [P, H])
        eps = e.sb(ctx, "l2_eps", [P, 1])
        zt = e.sb(ctx, "z_tail", [P, NZ])
        at = e.sb(ctx, "a_tail", [P, NT, H])
        ax = e.sb(ctx, "a_biased", [P, NT, H])
        ab = e.sb(ctx, "ab_tok", [P, NT, 2 * H])
        w_in, z_mm, ab_turned, ab_kept, eps_set, rooted, z_tail, z_done, biased, a_tail, a_exp, decay, b_exp, b_one, \
            inverted, scaled, beta_done, a_soft, a_neg = e.sem(
                ctx, "gk_in", "z_mm", "ab_turned", "ab_kept", "l2_eps_set", "norm_rooted", "z_tail_step", "z_done",
                "a_is_biased", "a_tail_step", "a_log_exp", "decay_done", "b_exp", "b_plus_one", "norm_inverted",
                "norm_scaled", "beta_done", "a_softplus", "a_negated")
        block = ctx.enter_context(nc.Block())
        Z = PS[:, 0:5, :].rearrange("p b n -> p (b n)")[:, 0:NZ]

        @block.sync
        def _(sp):
            sp.dma_start(w2[:], d["gla_gk_w2"][0]).then_inc(w_in, 16)
            sp.dma_start(gkb[:], d["gla_gk_b"]).then_inc(w_in, 16)
            sp.dma_start(alog[:], d["dn_a_log"].broadcast_to((P, H))).then_inc(w_in, 16)
            sp.dma_start(dtb[:], d["dn_dt_bias"].broadcast_to((P, H))).then_inc(w_in, 16)

        @block.tensor
        def _(pe):
            for t in range(NT):
                m = pe.transpose(PS[:, 5, t * 2 * H:(t + 1) * 2 * H], misc[32:48, t * P:(t + 1) * P], ident[32:48, 32:48])
            m.then_inc(ab_turned, 1)
            pe.wait_ge(w_in, 64)
            for t in range(NT):
                o = Z[:, t * H * GK:(t + 1) * H * GK]
                nc.tensor.matmul(o, misc[0:RANK, t * P:(t + 1) * P], w2[:], start=True, stop=False)
                m = nc.tensor.matmul(o, e.ones[0:1, :], gkb[:], start=False, stop=True)
            m.then_inc(z_mm, 1)

        @block.scalar
        def _(act):
            act.wait_ge(ab_turned, 1)
            nc.scalar.copy(ab[:], PS[:, 5, 0:2 * NH].rearrange("p (t h) -> p t h", t=NT)).then_inc(ab_kept, 1)
            act.wait_ge(eps_set, 1)
            nc.scalar.activation(e.rn[:], e.ss[:, :, 0:2 * H], ACT.Sqrt, bias=eps[:, 0:1]).then_inc(rooted, 1)
            act.wait_ge(z_mm, 1)
            nc.scalar.activation(zt[:], Z, ACT.Abs).then_inc(z_tail, 1)
            act.wait_ge(biased, 1)
            nc.scalar.activation(at[:], ax[:], ACT.Abs).then_inc(a_tail, 1)
            act.wait_ge(z_tail, 1)
            nc.scalar.activation(zt[:], zt[:], ACT.Exp, scale=-1.0).then_inc(z_tail, 1)
            act.wait_ge(a_tail, 1)
            nc.scalar.activation(at[:], at[:], ACT.Exp, scale=-1.0).then_inc(a_tail, 1)
            act.wait_ge(w_in, 64)
            nc.scalar.activation(alog[:], alog[:], ACT.Exp).then_inc(a_exp, 1)
            act.wait_ge(ab_kept, 1)
            nc.scalar.activation(e.beta[:], ab[:, :, H:2 * H], ACT.Exp, scale=-1.0).then_inc(b_exp, 1)
            act.wait_ge(z_tail, 2)
            nc.scalar.activation(zt[:], zt[:], ACT.Ln, bias=1.0).then_inc(z_tail, 1)
            act.wait_ge(a_tail, 2)
            nc.scalar.activation(at[:], at[:], ACT.Ln, bias=1.0).then_inc(a_tail, 1)

        @block.vector
        def _(dve):
            nc.vector.memset(eps[:], EPS).then_inc(eps_set, 1)
            dve.wait_ge(ab_kept, 1)
            dve.wait_ge(w_in, 64)
            nc.vector.tensor_tensor(ax[:], ab[:, :, 0:H], bc(dtb[:].rearrange("p (o h) -> p o h", o=1), (P, NT, H)),
                                    ALU.add).then_inc(biased, 1)
            dve.wait_ge(rooted, 1)
            nc.vector.reciprocal(e.rn[:], e.rn[:]).then_inc(inverted, 1)
            dve.wait_ge(inverted, 1)
            nc.vector.tensor_scalar(e.rn[:, :, 0:H], e.rn[:, :, 0:H], float(DK) ** -0.5, None, ALU.mult).then_inc(scaled, 1)
            dve.wait_ge(b_exp, 1)
            nc.vector.tensor_scalar(e.beta[:], e.beta[:], 1.0, None, ALU.add).then_inc(b_one, 1)
            dve.wait_ge(b_one, 1)
            nc.vector.reciprocal(e.beta[:], e.beta[:]).then_inc(beta_done, 1)
            dve.wait_ge(beta_done, 1)
            nc.vector.tensor_tensor(e.rkb[:], e.beta[:], e.rn[:, :, H:2 * H], ALU.mult).then_inc(scaled, 1)
            dve.wait_ge(a_exp, 1)
            dve.wait_ge(a_tail, 3)
            nc.vector.scalar_tensor_tensor(out=ax[:], in0=ax[:], scalar=0.0, in1=at[:], op0=ALU.max, op1=ALU.add
                                           ).then_inc(a_soft, 1)
            dve.wait_ge(a_soft, 1)
            nc.vector.scalar_tensor_tensor(out=e.gdn[:], in0=ax[:], scalar=-1.0,
                                           in1=bc(alog[:].rearrange("p (o h) -> p o h", o=1), (P, NT, H)),
                                           op0=ALU.mult, op1=ALU.mult).then_inc(decay, 1)
            dve.wait_ge(z_tail, 3)
            nc.vector.scalar_tensor_tensor(out=e.ggla[:].rearrange("p t c -> p (t c)"), in0=Z, scalar=0.0, in1=zt[:],
                                           op0=ALU.min, op1=ALU.subtract).then_inc(z_done, 1)



class Count:

    def __init__(self, sem, per):
        self.sem, self.per = sem, per

    def wait(self, eng, t, k=None):
        eng.wait_ge(self.sem, t * self.per + (self.per if k is None else k))


def recurrences(e):
    nc, d, PS, ident, c = e.nc, e.d, e.PS, e.ident, e.const
    qkv, rest = e.scr["qkv"], e.scr["rest"]
    HE = H * DK
    NL = len(LEVELS)
    with e.stage() as ctx:
        lq = e.sb(ctx, "tile_qkv", [P, 2, QKV])
        lr = e.sb(ctx, "tile_gla", [P, 2, 2, HE])
        ug = e.sb(ctx, "upto_g", [P, H, P])
        dec = e.sb(ctx, "decay", [P, H, P])
        gwide = e.sb(ctx, "g_wide", [P, H, DK])
        gs = e.sb(ctx, "gla_g", [P, H * GK])
        qn = e.sb(ctx, "q_normed", [P, H, DK])
        kn = e.sb(ctx, "k_normed", [P, H, DK])
        kb = e.sb(ctx, "k_beta", [P, H, DK])
        kd = e.sb(ctx, "k_decayed", [P, H, DK])
        bv = e.sb(ctx, "v_beta", [P, H, DK])
        small = e.sb(ctx, "small_exps", [P, 2 * H])
        egl = e.sb(ctx, "egl", [P, H // 2, BS])
        rkd = e.sb(ctx, "rk_decayed", [P, H])
        be = e.sb(ctx, "beta_eg", [P, H])
        kde = e.sb(ctx, "gla_k_exp", [P, H * GK])
        kdg = e.sb(ctx, "gla_k_decayed", [P, H * GK])
        gqt = e.sb(ctx, "gla_qT", [P, 2, P])
        gkt = e.sb(ctx, "gla_kT", [P, 2, P])
        ex = e.sb(ctx, "gla_exps", [P, 2, NL + 1, P])
        qe = e.sb(ctx, "gla_q_exp", [P, 2, P])
        gqbd = e.sb(ctx, "gla_q_heads", [P, 2, 4, P])
        qj = e.sb(ctx, "gla_q_size", [P, 2, 2, 4, P])
        ke = e.sb(ctx, "gla_k_exps", [P, 2, NL, P])
        ga = e.sb(ctx, "gla_pairs", [P, H, P])
        qt = e.sb(ctx, "qT", [P, H // 2, P])
        kt = e.sb(ctx, "kT", [P, H // 2, P])
        kbt = e.sb(ctx, "kbT", [P, H // 2, P])
        bt = e.sb(ctx, "minus_aT", [P, H, P])
        pt = e.sb(ctx, "qk_pairs", [P, H, P])
        u = e.sb(ctx, "inverse_T", [P, H, P])
        tt = e.sb(ctx, "inverse", [P, H, P])
        z = e.sb(ctx, "z", [P, H, P])
        tmp = e.sb(ctx, "ks_scaled", [P, HE])
        rr = e.sb(ctx, "rhs", [P, HE])
        vn = e.sb(ctx, "v_new", [P, HE])
        tmq = e.sb(ctx, "qs_scaled", [P, HE])
        S = e.sb(ctx, "dn_state", [P, H // 2, 2, DK])
        GS = e.sb(ctx, "gla_state", [P, 2, 4, DK])
        Ss = e.sb(ctx, "dn_states", [P, H // 2, BS, DK])
        GSs = e.sb(ctx, "gla_states", [P, 2, BS, DK])
        mk = e.sb(ctx, "stream_masked", [P, 2, BS, P])
        vm = ug[:].rearrange("p h t -> p (h t)")[:, 0:2 * BS * DK].rearrange("p (s b v) -> p s b v", s=2, b=BS)
        Ssd, GSsd = mk[:, 0, 0:4].rearrange("p a t -> p (a t)"), mk[:, 1, 0:4].rearrange("p a t -> p (a t)")

        def count(name, per=1):
            return Count(e.sem(ctx, name), per)
        load0, load1, states_in = e.sem(ctx, "tile_in0", "tile_in1", "states_in")
        load = [load0, load1]
        end = {k: e.sem(ctx, f"end_{k}") for k in ("pe", "act", "dve", "pool")}
        cleared, state_zero, states_out, ga_zero = e.sem(ctx, "pairs_zero", "state_zero", "states_out", "pairs_rezero")
        ug_ready, scaled, gwide_ready, gs_ready = count("ug_ready"), count("scaled", 4), count("gwide_ready"), count("gla_g_ready")
        dec_sum, dec_exp, dec_masked = count("dec_sum"), count("dec_exp"), count("dec_masked")
        small_mm, small_exp, rkd_ready, kd_ready = count("small_mm"), count("small_exp"), count("rkd_ready"), count("kd_ready")
        gla_turned, gla_ready, e_mm, e_exp = count("gla_turned"), count("glaT_ready"), count("e_mm", 2), count("e_exp", 2)
        qe_ready, kdg_ready = count("qe_ready", 2), count("kdg_ready")
        gqbd_ready, qj_ready = count("gla_q_heads_ready"), count("gla_q_size_ready", NL)
        turned, tready = count("qk_turned", 3), count("qkT_ready", 3)
        a_mm, p_mm, bt_ready, pt_ready = count("a_mm"), count("p_mm"), count("bt_ready"), count("pt_ready")
        u_init, u_first, t_turned, t_first = count("u_init"), count("u_first"), count("t_turned", 2), count("t_first", 2)
        z_mm, z_copied = count("z_mm", 2 * (NL - 1)), count("z_copied", 2 * (NL - 1))
        du_mm, dt_mm = count("du_mm", 2 * (NL - 1)), count("dt_mm", 2 * (NL - 2))
        u_put, t_put = count("u_put", 2 * (NL - 1)), count("t_put", 2 * (NL - 2))
        ga_mm, ga_put = count("gla_pairs_mm", NL + 1), count("gla_pairs_put", NL + 1)
        be_ready, ks_mm, qs_mm, ks_scaled, r_ready = count("be_ready"), count("ks_mm"), count("qs_mm"), count("ks_scaled"), count("r_ready")
        v_mm, v_ready, qs_scaled, o_mm = count("v_mm"), count("v_ready"), count("qs_scaled"), count("o_mm")
        go_mm, go_copied, gstate_mm, state_mm = count("go_mm"), count("go_copied"), count("gstate_mm"), count("state_mm")
        mk_ready, mk_used = e.sem(ctx, "masked_ready", "masked_used")
        vm_ready, vm_used, sd_ready, s_done = e.sem(ctx, "vm_ready", "vm_used", "sd_ready", "states_done")
        gd_ready = e.sem(ctx, "gla_sd_ready")
        block = ctx.enter_context(nc.Block())

        def levels(sample):
            return range(1, 4 if sample else NL)

        def pairs_jobs(sample):
            return list(range(4 if sample else NL)) + [NL]

        def at(h):
            return h % 2 * 4 + h // 2

        def gla_at(h):
            return h

        row_done = e.sem(ctx, "row_done")

        def each(eng, tile):
            with eng.Fori(0, NPT // 2) as i:
                tile(i, 0, False)
                tile(i, 1, False)
            tile(NPT // 2, 0, True)

        def start(eng, t, me):
            for k, s in end.items():
                if k != me:
                    eng.wait_ge(s, t + 2)
            e.apart(eng)

        def half(ap, g):
            return ap[:, 4 * g:4 * g + 4]

        def bank2(b):
            return PS[:, b:b + 2, :].rearrange("p b (h t) -> p (b h) t", h=4)

        def wide(ap, n):
            return bc(ap.rearrange("p (h o) -> p h o", o=1), (P, ap.shape[1], n))

        def over_heads(ap, h=H):
            return bc(ap.rearrange("p (o t) -> p o t", o=1), (P, h, P))

        def hv(ap):
            return ap.rearrange("p (h v) -> p h v", h=H)

        @block.sync
        def _(sp):
            for m in range(H // 2):
                sp.dma_start(Ss[:, m], d["state_dn"][0].rearrange("b h k v -> b (h k) v")[:, m * P:(m + 1) * P]
                             .rearrange("b p v -> p b v")).then_inc(states_in, 16)
            for m in range(2):
                sp.dma_start(GSs[:, m], d["state_gla"][0].rearrange("b h k v -> b (h k) v")[:, m * P:(m + 1) * P]
                             .rearrange("b p v -> p b v")).then_inc(states_in, 16)

            def tile(i, s, sample):
                t = i * 2 + s
                for x in end.values():
                    sp.wait_ge(x, t + 1)
                sp.dma_start(lq[:, s], qkv[ds(t * P, P)]).then_inc(load[s], 16)
                sp.dma_start(lr[:, s], rest[ds(t * P, P), 2:4]).then_inc(load[s], 16)
            each(sp, tile)
            for x in end.values():
                sp.wait_ge(x, NPT + 2)
            for h in range(2):
                r = slice(h * DK, (h + 1) * DK)
                sp.dma_start(d["dn_p"][0, 0].rearrange("(m h) k v -> h k m v", h=2)[h], S[r, :, h]).then_inc(states_out, 16)
            for h in range(4):
                r = slice(h * GK, (h + 1) * GK)
                sp.dma_start(d["gla_p"][0, 0].rearrange("(m h) k v -> h k m v", h=4)[h], GS[r, :, h]).then_inc(states_out, 16)
            sp.wait_ge(s_done, 6)
            for m in range(H // 2):
                sp.dma_start(d["dn_s"][0].rearrange("b h k v -> b (h k) v")[:, m * P:(m + 1) * P]
                             .rearrange("b p v -> p b v"), Ss[:, m]).then_inc(states_out, 16)
            for m in range(2):
                sp.dma_start(d["gla_s"][0].rearrange("b h k v -> b (h k) v")[:, m * P:(m + 1) * P]
                             .rearrange("b p v -> p b v"), GSs[:, m]).then_inc(states_out, 16)
            sp.wait_ge(states_out, 16 * 12)

        @block.gpsimd
        def _(pool):
            pool.sem_inc(end["pool"], 2)
            tt_ = nc.gpsimd.tensor_tensor

            def tile(i, s, sample):
                t = i * 2 + s
                start(pool, t, "pool")
                upto = c("upto_s" if sample else "upto_p")
                col = lambda ap, a=0, b=H: ap[:, ds(t, 1), a:b].rearrange("p o h -> p (o h)")
                g = col(e.gdn)
                for r in range(2):
                    k = tt_(ug[:, 4 * r:4 * r + 4], over_heads(upto, 4),
                            wide(g.rearrange("p (m r) -> p r m", r=2)[:, r], P), ALU.mult)
                k.then_inc(ug_ready.sem, 1)
                nc.gpsimd.tensor_copy(gwide[:], wide(g, DK)).then_inc(gwide_ready.sem, 1)
                nc.gpsimd.tensor_copy(gs[:], e.ggla[:, ds(t, 1)].rearrange("p o c -> p (o c)")).then_inc(gs_ready.sem, 1)
                pool.wait_ge(load[s], (i + 1) * 32)
                e.apart(pool)
                q, k, v = (hv(lq[:, s, n * HE:(n + 1) * HE]) for n in range(3))
                tt_(qn[:], q, wide(col(e.rn), DK), ALU.mult).then_inc(scaled.sem, 1)
                tt_(kn[:], k, wide(col(e.rn, H, 2 * H), DK), ALU.mult).then_inc(scaled.sem, 1)
                tt_(kb[:], k, wide(col(e.rkb), DK), ALU.mult).then_inc(scaled.sem, 1)
                dec_exp.wait(pool, t)
                e.apart(pool)
                tt_(dec[:], dec[:], over_heads(upto), ALU.mult).then_inc(dec_masked.sem, 1)
                tt_(bv[:], v, wide(col(e.beta), DK), ALU.mult).then_inc(scaled.sem, 1)
                small_exp.wait(pool, t)
                e.apart(pool)
                tt_(rkd[:], col(e.rn, H, 2 * H), small[:, H:2 * H], ALU.mult).then_inc(rkd_ready.sem, 1)
                rkd_ready.wait(pool, t)
                e.apart(pool)
                m = tt_(kd[:], k, wide(rkd[:], DK), ALU.mult)
                m.then_inc(end["pool"], 1)
            each(pool, tile)

        @block.tensor
        def _(pe):
            pe.sem_inc(end["pe"], 2)
            pe.sem_inc(mk_used, 2)
            pe.sem_inc(vm_used, 2)
            mm = nc.tensor.matmul

            def rows(h, n):
                per = P // n
                return slice(n * (h % per), n * (h % per) + n), h // per

            def pairs(j, n, t):
                if n:
                    ga_put.wait(pe, t, n)
                else:
                    pt_ready.wait(pe, t)
                    qe_ready.wait(pe, t)
                    gqbd_ready.wait(pe, t)
                if j != NL:
                    qj_ready.wait(pe, t, n + 1)
                for m in range(2):
                    w = gkt[:, m] if j == NL else ke[:, m, j]
                    x = gqbd[:, m] if j == NL else qj[:, n % 2, m]
                    k = mm(PS[:, 1 + m, :], w, x.rearrange("p h t -> p (h t)"), start=True, stop=True)
                k.then_inc(ga_mm.sem, 1)

            def tile(i, s, sample):
                t = i * 2 + s
                start(pe, t, "pe")
                upto, after = (c("upto_s"), c("after_s")) if sample else (c("upto_p"), c("after_p"))
                ug_ready.wait(pe, t)
                for g in range(2):
                    k = mm(PS[:, 1 + g, :], after, half(ug, g).rearrange("p h t -> p (h t)"), start=True, stop=True)
                k.then_inc(dec_sum.sem, 1)
                gwide_ready.wait(pe, t)
                gt = e.gdn[:, ds(t, 1), :].rearrange("p o h -> p (o h)")
                nb = BS if sample else 1
                ends = c("streams") if sample else e.ones[:, 0:1]
                mm(PS[:, 0, 0:H], upto, gt, start=True, stop=True)
                mm(PS[:, 0, H:2 * H], after, gt, start=True, stop=True)
                for m in range(H // 2):
                    mm(PS[:, 0, 16 + m * nb:16 + (m + 1) * nb], gwide[:, 2 * m:2 * m + 2].rearrange("p h v -> p (h v)"),
                       ends, start=True, stop=True)
                mm(PS[:, 0, 256:512], after, e.ggla[:, ds(t, 1)].rearrange("p o c -> p (o c)"),
                   start=True, stop=True).then_inc(small_mm.sem, 1)
                pe.wait_ge(load[s], (i + 1) * 32)
                for m in range(4):
                    k = pe.transpose(PS[:, 3, m * P:(m + 1) * P], lr[:, s, 0, m * P:(m + 1) * P], ident)
                k.then_inc(gla_turned.sem, 1)
                gs_ready.wait(pe, t)
                sp_ = c("spans")
                for m in range(2):
                    w = gs[:, m * P:(m + 1) * P]
                    mm(PS[:, 4 + 2 * m, :], w, sp_[:, 0:4 * P], start=True, stop=True)
                    mm(PS[:, 5 + 2 * m, 0:3 * P], w, sp_[:, 4 * P:7 * P], start=True, stop=True)
                    mm(PS[:, 5 + 2 * m, 3 * P:4 * P], w, upto, start=True, stop=True).then_inc(e_mm.sem, 1)
                for n, (src, bank) in enumerate(((qn, 3), (kn, 0), (kb, 4))):
                    scaled.wait(pe, t, n + 1)
                    (lambda: gla_ready.wait(pe, t), lambda: small_exp.wait(pe, t), lambda: e_exp.wait(pe, t, 1))[n]()
                    for m in range(4):
                        k = pe.transpose(PS[:, bank, m * P:(m + 1) * P],
                                         src[:, 2 * m:2 * m + 2].rearrange("p h v -> p (h v)"), ident)
                    k.then_inc(turned.sem, 1)
                tready.wait(pe, t)
                e_exp.wait(pe, t)
                for out, moving, done in ((6, kbt, a_mm), (1, qt, p_mm)):
                    if out == 1:
                        dec_exp.wait(pe, t)
                    for h in range(H):
                        r, m = rows(h, DK)
                        k = mm(PS[:, out + h % 2, m * P:(m + 1) * P], kt[r, m], moving[r, m], start=True, stop=True)
                    k.then_inc(done.sem, 1)
                u_first.wait(pe, t)
                for g, bank in enumerate((3, 0)):
                    for h in range(4):
                        k = pe.transpose(PS[:, bank, h * P:(h + 1) * P], u[:, 4 * g + h], ident)
                    k.then_inc(t_turned.sem, 1)
                jobs = pairs_jobs(sample)
                done_jobs = 0
                for li, l in enumerate(levels(sample)):
                    last = l == levels(sample)[-1]
                    for g, bank in enumerate((3, 0)):
                        if li:
                            t_put.wait(pe, t, 2 * (li - 1) + g + 1)
                        else:
                            t_first.wait(pe, t, g + 1)
                        for h in range(4):
                            k = mm(PS[:, bank, h * P:(h + 1) * P], bt[:, 4 * g + h], tt[:, 4 * g + h], start=True, stop=True)
                        k.then_inc(z_mm.sem, 1)
                    take = len(jobs) - done_jobs if last else max(1, -(-(len(jobs) - done_jobs) // (len(levels(sample)) - li)))
                    for n in range(done_jobs, done_jobs + take):
                        pairs(jobs[n], n, t)
                    done_jobs += take
                    for g in range(2):
                        z_copied.wait(pe, t, 2 * li + g + 1)
                        if li:
                            u_put.wait(pe, t, 2 * (li - 1) + g + 1)
                        for h in range(4):
                            k = mm(PS[:, 4 + g, h * P:(h + 1) * P], z[:, 4 * g + h], u[:, 4 * g + h], start=True, stop=True)
                        k.then_inc(du_mm.sem, 1)
                        if last:
                            continue
                        if not li:
                            bt_ready.wait(pe, t)
                        for h in range(4):
                            k = mm(PS[:, 6 + g, h * P:(h + 1) * P], u[:, 4 * g + h], z[:, 4 * g + h], start=True, stop=True)
                        k.then_inc(dt_mm.sem, 1)
                nl, nj = len(levels(sample)), len(jobs)
                rd = 0
                if not sample:
                    for out, w, done in ((3, kt, ks_mm), (0, qt, qs_mm)):
                        for m in range(H // 2):
                            k = mm(PS[:, out, m * P:(m + 1) * P], w[:, m], S[:, m].rearrange("p h v -> p (h v)"),
                                   start=True, stop=True)
                        k.then_inc(done.sem, 1)
                else:
                    pe.wait_ge(states_in, 16 * 6)
                    for n in range(8):
                        out, done = ((3, ks_mm), (0, qs_mm))[n // 4]
                        pe.wait_ge(mk_ready, n + 1)
                        for hh in range(2):
                            if n % 4 or hh:
                                pe.wait_ge(row_done, rd)
                            h = 2 * (n % 4) + hh
                            r, m = rows(h, DK)
                            for b in range(BS):
                                k = mm(PS[:, out, h * DK:(h + 1) * DK], mk[r, n % 2, b], Ss[r, m, b],
                                       start=(b == 0), stop=(b == BS - 1))
                            k.then_inc(row_done, 1)
                            rd += 1
                        pe.wait_ge(row_done, rd)
                        pe.sem_inc(mk_used, 1)
                        if n % 4 == 3:
                            pe.sem_inc(done.sem, 1)
                ga_put.wait(pe, t, nj)
                if sample:
                    pe.wait_ge(mk_ready, 10)
                if sample:
                    for q in range(4):
                        if q:
                            pe.wait_ge(row_done, rd)
                        for h in (q, q + 4):
                            r, m = rows(h, GK)
                            for b in range(BS):
                                k = mm(PS[:, 1, h * DK:(h + 1) * DK], mk[r, m, b], GSs[r, m, b],
                                       start=(h == 0 and b == 0), stop=False, skip_group_check=True)
                        k.then_inc(row_done, 1)
                        rd += 1
                    pe.wait_ge(row_done, rd)
                    pe.sem_inc(mk_used, 2)
                else:
                    for m in range(2):
                        mm(PS[:, 1, m * 256:(m + 1) * 256], qe[:, m], GS[:, m].rearrange("p h v -> p (h v)"),
                           start=(m == 0), stop=False, skip_group_check=True)
                for h in range(H):
                    k = mm(PS[:, 1, h * DK:(h + 1) * DK], ga[:, gla_at(h)], lr[:, s, 1, h * DK:(h + 1) * DK],
                           start=False, stop=(h == H - 1), skip_group_check=True)
                k.then_inc(go_mm.sem, 1)
                if not sample:
                    kdg_ready.wait(pe, t)
                    for m in range(2):
                        k = mm(PS[:, 2, m * 256:(m + 1) * 256], kdg[:, m * P:(m + 1) * P],
                               lr[:, s, 1, m * 256:(m + 1) * 256], start=True, stop=True)
                    k.then_inc(gstate_mm.sem, 1)
                r_ready.wait(pe, t)
                u_put.wait(pe, t, 2 * nl)
                for h in range(H):
                    k = mm(PS[:, 4, h * DK:(h + 1) * DK], u[:, at(h)], rr[:, h * DK:(h + 1) * DK], start=True, stop=True)
                k.then_inc(v_mm.sem, 1)
                v_ready.wait(pe, t)
                for h in range(H):
                    k = mm(PS[:, 5, h * DK:(h + 1) * DK], pt[:, at(h)], vn[:, h * DK:(h + 1) * DK], start=True, stop=True)
                k.then_inc(o_mm.sem, 1)
                pe.wait_ge(end["pool"], t + 3)
                if not sample:
                    for m in range(H // 2):
                        k = mm(PS[:, 6, m * P:(m + 1) * P], kd[:, 2 * m:2 * m + 2].rearrange("p h v -> p (h v)"),
                               vn[:, m * P:(m + 1) * P], start=True, stop=True)
                    k.then_inc(end["pe"], 1)
                else:
                    for n in range(2 * H):
                        gla = n >= H
                        h = n % H
                        pe.wait_ge(vm_ready, n + 1)
                        if gla:
                            r, m = rows(h, GK)
                            bank, w = (6, 7)[m], kdg[:, h * GK:(h + 1) * GK]
                            if h % 4 == 0:
                                pe.wait_ge(s_done, (1, 4)[m])
                        else:
                            r, m = rows(h, DK)
                            bank, w = (6, 2, 3, 7)[m], kd[:, h]
                        k = mm(PS[r, bank, :], w, vm[:, n % 2].rearrange("p b v -> p (b v)"), start=True, stop=True)
                        k.then_inc(vm_used, 1)
            each(pe, tile)

        @block.scalar
        def _(act):
            act.sem_inc(end["act"], 2)
            copy, exp = nc.scalar.copy, lambda o, x, **k: nc.scalar.activation(o, x, ACT.Exp, **k)

            def tile(i, s, sample):
                t = i * 2 + s
                nb = BS if sample else 1
                start(act, t, "act")
                dec_sum.wait(act, t)
                exp(dec[:], bank2(1)).then_inc(dec_exp.sem, 1)
                small_mm.wait(act, t)
                exp(small[:], PS[:, 0, 0:2 * H])
                exp(egl[:, :, 0:nb], PS[:, 0, 16:16 + 4 * nb].rearrange("p (m b) -> p m b", m=4))
                exp(kde[:], PS[:, 0, 256:512], scale=1.0 / 16).then_inc(small_exp.sem, 1)
                gla_turned.wait(act, t)
                nc.scalar.activation(gqt[:], PS[:, 3, 0:2 * P].rearrange("p (m t) -> p m t", m=2), ACT.Copy,
                                     scale=float(GK) ** -0.5)
                copy(gkt[:], PS[:, 3, 2 * P:4 * P].rearrange("p (m t) -> p m t", m=2)).then_inc(gla_ready.sem, 1)
                for m in range(2):
                    e_mm.wait(act, t, m + 1)
                    exp(ex[:, m], bank2(4 + 2 * m), scale=1.0 / 16).then_inc(e_exp.sem, 1)
                for n, (dst, bank) in enumerate(((qt, 3), (kt, 0), (kbt, 4))):
                    turned.wait(act, t, n + 1)
                    copy(dst[:], PS[:, bank, :].rearrange("p (m t) -> p m t", m=4)).then_inc(tready.sem, 1)
                for g, bank in enumerate((3, 0)):
                    t_turned.wait(act, t, g + 1)
                    copy(half(tt, g), PS[:, bank, :].rearrange("p (h t) -> p h t", h=4)).then_inc(t_first.sem, 1)
                for li in range(len(levels(sample))):
                    for g, bank in enumerate((3, 0)):
                        z_mm.wait(act, t, 2 * li + g + 1)
                        copy(half(z, g), PS[:, bank, :].rearrange("p (h t) -> p h t", h=4)).then_inc(z_copied.sem, 1)
                go_mm.wait(act, t)
                copy(e.o_all[:, ds(t, 1), HE:2 * HE].rearrange("p o v -> p (o v)"), PS[:, 1, :]).then_inc(go_copied.sem, 1)
                v_mm.wait(act, t)
                copy(vn[:], PS[:, 4, :]).then_inc(v_ready.sem, 1)
                v_ready.wait(act, t)
                act.sem_inc(end["act"], 1)
            each(act, tile)

        @block.vector
        def _(dve):
            v = nc.vector
            tt_ = v.tensor_tensor
            v.memset(S[:], 0.0)
            v.memset(GS[:], 0.0).then_inc(state_zero, 1)
            v.memset(gqbd[:], 0.0)
            v.memset(ga[:], 0.0).then_inc(cleared, 1)
            dve.wait_ge(cleared, 1)
            dve.wait_ge(state_zero, 1)
            dve.sem_inc(end["dve"], 2)

            def place(sample, j, n, t):
                ga_mm.wait(dve, t, n + 1)
                e.apart(dve)
                v.copy_predicated(ga[:], over_heads(c("up")[:, j * P:(j + 1) * P]), bank2(1)).then_inc(ga_put.sem, 1)

            def tile(i, s, sample):
                t = i * 2 + s
                start(dve, t, "dve")
                v.tensor_copy(u[:], over_heads(ident)).then_inc(u_init.sem, 1)
                if sample:
                    v.memset(ga[:], 0.0).then_inc(ga_zero, 1)
                gla_ready.wait(dve, t)
                for h in range(4):
                    r = slice(h * GK, (h + 1) * GK)
                    k = v.tensor_copy(gqbd[r, :, h], gqt[r])
                k.then_inc(gqbd_ready.sem, 1)
                jobs, n = pairs_jobs(sample), 0

                def q_size(n):
                    if jobs[n] == NL:
                        return
                    if n == 0:
                        gqbd_ready.wait(dve, t)
                    for m in range(2):
                        k = tt_(qj[:, n % 2, m], over_heads(ex[:, m, jobs[n]], 4), gqbd[:, m], ALU.mult)
                    k.then_inc(qj_ready.sem, 1)
                for m in range(2):
                    e_exp.wait(dve, t, m + 1)
                    tt_(qe[:, m], ex[:, m, NL], gqt[:, m], ALU.mult)
                    tt_(ke[:, m], ex[:, m, 0:NL], over_heads(gkt[:, m], NL), ALU.mult).then_inc(qe_ready.sem, 1)
                small_exp.wait(dve, t)
                dve.wait_ge(load[s], (i + 1) * 32)
                tt_(kdg[:], lr[:, s, 0, 2 * P:4 * P], kde[:], ALU.mult).then_inc(kdg_ready.sem, 1)
                tt_(be[:], e.beta[:, ds(t, 1)].rearrange("p o h -> p (o h)"), small[:, 0:H], ALU.mult).then_inc(be_ready.sem, 1)
                a_mm.wait(dve, t)
                dec_masked.wait(dve, t)
                v.scalar_tensor_tensor(out=bt[:].rearrange("p h t -> p (h t)"),
                                       in0=PS[:, 6:8, :].rearrange("p b n -> p (b n)"), scalar=-1.0,
                                       in1=dec[:].rearrange("p h t -> p (h t)"), op0=ALU.mult, op1=ALU.mult
                                       ).then_inc(bt_ready.sem, 1)
                bt_ready.wait(dve, t)
                u_init.wait(dve, t)
                e.apart(dve)
                v.copy_predicated(u[:], over_heads(c("up")[:, 0:P]), bt[:]).then_inc(u_first.sem, 1)
                p_mm.wait(dve, t)
                tt_(pt[:], bank2(1), dec[:], ALU.mult).then_inc(pt_ready.sem, 1)
                q_size(0)
                q_size(1)
                if sample:
                    dve.wait_ge(ga_zero, 1)
                lv = levels(sample)
                for li, l in enumerate(lv):
                    last = l == lv[-1]
                    take = len(jobs) - n if last else max(1, -(-(len(jobs) - n) // (len(lv) - li)))
                    for j in range(n, n + take):
                        place(sample, jobs[j], j, t)
                        if j + 2 < len(jobs):
                            q_size(j + 2)
                    n += take
                    for g in range(2):
                        (du_mm.wait(dve, t, 2 * li + g + 1) if last else dt_mm.wait(dve, t, 2 * li + g + 1))
                        if li:
                            u_put.wait(dve, t, 2 * (li - 1) + g + 1)
                        else:
                            u_first.wait(dve, t)
                        e.apart(dve)
                        v.copy_predicated(half(u, g), over_heads(c("up")[:, l * P:(l + 1) * P], 4),
                                          PS[:, 4 + g, :].rearrange("p (h t) -> p h t", h=4)).then_inc(u_put.sem, 1)
                        if not last:
                            v.copy_predicated(half(tt, g), over_heads(c("low")[:, l * P:(l + 1) * P], 4),
                                              PS[:, 6 + g, :].rearrange("p (h t) -> p h t", h=4)).then_inc(t_put.sem, 1)
                if sample:
                    for k in range(10):
                        dve.wait_ge(mk_used, k + 1)
                        x = kt[:, k] if k < 4 else qt[:, k - 4] if k < 8 else qe[:, k - 8]
                        tt_(mk[:, k % 2], over_heads(x), c("stream_cols").rearrange("p (b t) -> p b t", b=BS),
                            ALU.mult).then_inc(mk_ready, 1)
                ks_mm.wait(dve, t)
                be_ready.wait(dve, t)
                tt_(hv(tmp[:]), hv(PS[:, 3, :]), wide(be[:], DK), ALU.mult).then_inc(ks_scaled.sem, 1)
                ks_scaled.wait(dve, t)
                scaled.wait(dve, t)
                tt_(hv(rr[:]), bv[:], hv(tmp[:]), ALU.subtract).then_inc(r_ready.sem, 1)
                qs_mm.wait(dve, t)
                tt_(hv(tmq[:]), hv(PS[:, 0, :]), wide(small[:, 0:H], DK), ALU.mult).then_inc(qs_scaled.sem, 1)
                if not sample:
                    gstate_mm.wait(dve, t)
                    for h in range(H):
                        r, m = slice(h % 4 * GK, (h % 4 + 1) * GK), h // 4
                        v.scalar_tensor_tensor(out=GS[r, m, h % 4], in0=GS[r, m, h % 4], scalar=ex[r, m, NL, P - 1:P],
                                               in1=PS[r, 2, h * DK:(h + 1) * DK], op0=ALU.mult, op1=ALU.add)
                o_mm.wait(dve, t)
                qs_scaled.wait(dve, t)
                tt_(e.o_all[:, ds(t, 1), 0:HE].rearrange("p o v -> p (o v)"), tmq[:], PS[:, 5, :], ALU.add)
                if not sample:
                    dve.wait_ge(end["pe"], t + 3)
                    for h in range(H):
                        r, m, o = slice(h % 2 * DK, (h % 2 + 1) * DK), h // 2, h % 2
                        k = v.scalar_tensor_tensor(out=S[r, m, o], in0=S[r, m, o], scalar=egl[r, m, 0:1],
                                                   in1=PS[r, 6, h * DK:(h + 1) * DK], op0=ALU.mult, op1=ALU.add)
                    k.then_inc(end["dve"], 1)
                else:
                    v_ready.wait(dve, t)
                    dve.wait_ge(mk_used, 12)

                    def values(n):
                        dve.wait_ge(vm_used, n + 1)
                        src = vn[:, (n % H) * DK:(n % H + 1) * DK] if n < H else lr[:, s, 1, (n - H) * DK:(n - H + 1) * DK]
                        tt_(vm[:, n % 2], bc(src.rearrange("p (o v) -> p o v", o=1), (P, BS, DK)),
                            wide(c("streams"), DK), ALU.mult).then_inc(vm_ready, 1)

                    def update(st, bank, decay, buf, k, used):
                        tt_(buf.rearrange("p (b v) -> p b v", b=BS), st, decay, ALU.mult).then_inc(sd_ready, 1)
                        dve.wait_ge(vm_used, used + 2)
                        dve.wait_ge(sd_ready, k)
                        tt_(st, buf.rearrange("p (b v) -> p b v", b=BS), PS[:, bank, :].rearrange("p (b v) -> p b v", b=BS),
                            ALU.add).then_inc(s_done, 1)
                    for m in range(H // 2):
                        values(2 * m)
                        values(2 * m + 1)
                        update(Ss[:, m], (6, 2, 3, 7)[m], wide(egl[:, m], DK), (Ssd, GSsd)[m % 2], m + 1, 2 * m + 2)
                    for m in range(2):
                        for hh in range(4):
                            values(H + 4 * m + hh)
                        last = ex[:, m, NL].rearrange("p (b l) -> p b l", b=BS)[:, :, LS - 1:LS]
                        update(GSs[:, m], 6 + m, bc(last, (P, BS, DK)), (Ssd, GSsd)[m % 2], m + 5, H + 4 * m + 4)
            each(dve, tile)


def gate_outputs(e, oT):
    nc, d, PS, ident = e.nc, e.d, e.PS, e.ident
    NH = 2 * H
    with e.stage() as ctx:
        gate = e.sb(ctx, "gate_rows", [P, 2, 2 * H * DK])
        gain = e.sb(ctx, "head_gains", [P, 2, DK])
        sq = e.sb(ctx, "o_sq", [P, 2, 2 * H * DK])
        og = e.sb(ctx, "o_gated", [P, 2, 2 * H * DK])
        ss = e.sb(ctx, "o_ss", [P, 2, NH])
        eps = e.sb(ctx, "o_eps", [P, 1])
        g0, g1, gain_in, eps_set, squared, summed, rooted, inverted, normed, gained, gated, turned, high, low = e.sem(
            ctx, "gate_in0", "gate_in1", "head_gain_in", "o_eps_set", "o_squared", "o_summed", "o_rooted", "o_inverted",
            "o_normed", "o_gained", "o_gated", "o_turned", "oT_high_part", "oT_low_part")
        gate_in = [g0, g1]
        block = ctx.enter_context(nc.Block())

        def each(eng, tile):
            with eng.Fori(0, NPT // 2) as i:
                tile(i, 0)
                tile(i, 1)
            tile(NPT // 2, 0)

        @block.sync
        def _(sp):
            sp.dma_start(gain[:, 0], d["dn_out_norm"].broadcast_to((P, DK))).then_inc(gain_in, 16)
            sp.dma_start(gain[:, 1], d["gla_out_norm"].broadcast_to((P, DK))).then_inc(gain_in, 16)

            def tile(i, s):
                t = i * 2 + s
                sp.wait_ge(gated, t + 1)
                sp.dma_start(gate[:, s], e.scr["rest"][ds(t * P, P), 0:2].rearrange("t g c -> t (g c)")
                             ).then_inc(gate_in[s], 16)
            each(sp, tile)

        @block.gpsimd
        def _(pool):
            def tile(i, s):
                t = i * 2 + s
                o = e.o_all[:, ds(t, 1)].rearrange("p o c -> p (o c)")
                pool.wait_ge(summed, t + 1)
                e.apart(pool)
                nc.gpsimd.tensor_tensor(sq[:, s], o, o, ALU.mult).then_inc(squared, 1)
            each(pool, tile)

        @block.scalar
        def _(act):
            act.sem_inc(high, 4)
            act.wait_ge(eps_set, 1)

            def tile(i, s):
                t = i * 2 + s
                act.wait_ge(summed, t + 3)
                nc.scalar.activation(ss[:, s], ss[:, s], ACT.Sqrt, scale=1.0 / DK, bias=eps[:, 0:1]).then_inc(rooted, 1)
                for h in range(2):
                    act.wait_ge(turned, t * 2 + 5 + h)
                    nc.scalar.copy(oT[0][:, 4 * h:4 * h + 4, ds(t * P, P)],
                                   PS[:, 2 * s + h, :].rearrange("p (k t) -> p k t", k=4)).then_inc(high, 1)
            each(act, tile)

        @block.vector
        def _(dve):
            dve.sem_inc(gated, 2)
            dve.sem_inc(low, 4)
            dve.sem_inc(summed, 2)
            nc.vector.memset(eps[:], EPS).then_inc(eps_set, 1)
            dve.wait_ge(gain_in, 32)

            def tile(i, s):
                t = i * 2 + s
                heads = lambda ap: ap.rearrange("p (h v) -> p h v", v=DK)
                dve.wait_ge(squared, t + 1)
                nc.vector.reduce_sum(ss[:, s], heads(sq[:, s]), AX_X).then_inc(summed, 1)
                dve.wait_ge(rooted, t + 1)
                nc.vector.reciprocal(ss[:, s], ss[:, s]).then_inc(inverted, 1)
                dve.wait_ge(inverted, t + 1)
                o = e.o_all[:, ds(t, 1)].rearrange("p o c -> p (o c)")
                dve.wait_ge(turned, t * 2 + 2)
                nc.vector.tensor_tensor(heads(og[:, s]), heads(o), bc(ss[:, s].rearrange("p (h o) -> p h o", o=1), (P, NH, DK)),
                                        ALU.mult).then_inc(normed, 1)
                dve.wait_ge(normed, t + 1)
                for m in range(2):
                    x = heads(og[:, s, m * 512:(m + 1) * 512])
                    k = nc.vector.tensor_tensor(x, x, bc(gain[:, m:m + 1], (P, H, DK)), ALU.mult)
                k.then_inc(gained, 1)
                dve.wait_ge(gained, t + 1)
                dve.wait_ge(gate_in[s], (i + 1) * 16)
                nc.vector.tensor_tensor(og[:, s], og[:, s], gate[:, s], ALU.mult).then_inc(gated, 1)

            def low_part(i, s):
                t = i * 2 + s
                for h in range(2):
                    dve.wait_ge(high, t * 2 + 5 + h)
                    c = ds(t * P, P)
                    nc.vector.tensor_tensor(oT[1][:, 4 * h:4 * h + 4, c],
                                            PS[:, 2 * s + h, :].rearrange("p (k t) -> p k t", k=4),
                                            oT[0][:, 4 * h:4 * h + 4, c], ALU.subtract).then_inc(low, 1)
            tile(0, 0)
            with dve.Fori(0, NPT // 2 - 1) as i:
                tile(i, 1)
                low_part(i, 0)
                tile(i + 1, 0)
                low_part(i, 1)
            tile(NPT // 2 - 1, 1)
            low_part(NPT // 2 - 1, 0)
            tile(NPT // 2, 0)
            low_part(NPT // 2 - 1, 1)
            low_part(NPT // 2, 0)

        @block.tensor
        def _(pe):
            pe.sem_inc(turned, 4)

            def tile(i, s):
                t = i * 2 + s
                pe.wait_ge(gated, t + 3)
                for h in range(2):
                    pe.wait_ge(low, t * 2 + h + 1)
                    for k in range(4):
                        m = pe.transpose(PS[:, 2 * s + h, k * P:(k + 1) * P],
                                         og[:, s, (h * 4 + k) * P:(h * 4 + k + 1) * P], ident)
                    m.then_inc(turned, 1)
            each(pe, tile)



def qkv_projection(e, hT):
    nc, d, PS, ident = e.nc, e.d, e.PS, e.ident
    wv = d["c_w_qkv"][0].rearrange("(k p) n -> p k n", p=P)
    qk, vr = e.scr["qk"], e.scr["v"]
    KR = 5
    with e.stage() as ctx:
        wraw = e.sb(ctx, "w_qk", [P, 2, KT, P])
        ws = e.sb(ctx, "w_qk_split", [P, 2, 2, KT, P], F32R)
        cols = e.sb(ctx, "qk_cols", [P, 2, T])
        krow = e.sb(ctx, "k_rows", [P, 2, KR, P])
        w_high, w_low, w0, w1, mm, kept, turned, kcopied, st0, st1, kst0, kst1 = e.sem(
            ctx, "w_high", "w_low", "wqk_in0", "wqk_in1", "qk_mm", "qk_kept", "k_turned", "k_copied", "qk_stored0", "qk_stored1",
            "k_stored0", "k_stored1")
        w_in, stored, kstored = [w0, w1], [st0, st1], [kst0, kst1]
        block = ctx.enter_context(nc.Block())
        NB = 2 * KT
        ckp = d["c_k_p"].rearrange("n b r h c -> (n b r) (h c)").rearrange("(j p) c -> p j c", p=P)
        cks = d["c_k_s"].rearrange("n b r h c -> (n b r) (h c)")

        @block.gpsimd
        def _(pool):
            for s in range(2):
                pool.dma_start(wraw[:, s], wv[:, :, s * P:(s + 1) * P]).then_inc(w_in[s], 16)
            with pool.Fori(0, NB // 2 - 1) as i:
                for s in range(2):
                    split_tile(e, pool, i, s, wraw, ws, w_in, mm, w_high, w_low)
                    pool.wait_ge(w_low, i * 2 + s + 1)
                    e.apart(pool)
                    pool.dma_start(wraw[:, s], wv[:, :, ds(i * 256 + 256 + s * P, P)]).then_inc(w_in[s], 16)
            for s in range(2):
                split_tile(e, pool, NB // 2 - 1, s, wraw, ws, w_in, mm, w_high, w_low)

        @block.sync
        def _(sp):
            for s in range(2):
                sp.sem_inc(stored[s], 16)
                sp.sem_inc(kstored[s], 16)

            def store(i, s):
                sp.wait_ge(kept, i * 2 + s + 3)
                sp.dma_start(qk[ds(i * 2 + s, 1)].rearrange("o p t -> p (o t)"), cols[:, s]).then_inc(stored[s], 16)
            with sp.Fori(0, NB // 4) as i:
                store(i, 0)
                store(i, 1)
            with sp.Fori(0, NB // 4) as i:
                for s in range(2):
                    store(i + NB // 4, s)
                    sp.wait_ge(kcopied, (i * 2 + s) * 2 + 6)
                    c = ds(i * 256 + s * P, P)
                    sp.dma_start(ckp[:, :, c], krow[:, s, 0:KR - 1]).then_inc(kstored[s], 16)
                    sp.dma_start(cks[:, c], krow[:, s, KR - 1]).then_inc(kstored[s], 16)
            for s in range(2):
                sp.wait_ge(stored[s], 16 * (NB // 2 + 1))
                sp.wait_ge(kstored[s], 16 * (NB // 2 + 1))

        @block.tensor
        def _(pe):
            pe.sem_inc(mm, 2)

            def multiply(i, s):
                pe.wait_ge(w_low, i * 2 + s + 1)
                pe.wait_ge(kept, i * 2 + s + 1)
                product_split(nc, PS, 3 * s, lambda k: (ws[:, s, 0, k], ws[:, s, 1, k]), parts(hT),
                              range(KT)).then_inc(mm, 1)

            def turn(i, s):
                pe.wait_ge(kept, (i * 2 + s) + KT + 3)
                for h, ts in enumerate((range(4), range(4, 5))):
                    pe.wait_ge(kcopied, (i * 2 + s) * 2 + h + 3)
                    for n in ts:
                        m = pe.transpose(PS[:, 6 + h, (n % 4) * P:(n % 4 + 1) * P],
                                         cols[:, s, (NT - KR + n) * P:(NT - KR + n + 1) * P], ident)
                    m.then_inc(turned, 1)
            with pe.Fori(0, NB // 4) as i:
                multiply(i, 0)
                multiply(i, 1)
            multiply(NB // 4, 0)
            with pe.Fori(0, NB // 4 - 1) as i:
                multiply(i + NB // 4, 1)
                turn(i, 0)
                multiply(i + NB // 4 + 1, 0)
                turn(i, 1)
            multiply(NB // 2 - 1, 1)
            turn(NB // 4 - 1, 0)
            turn(NB // 4 - 1, 1)

        @block.scalar
        def _(act):
            act.sem_inc(kept, 2)

            def keep(i, s):
                act.wait_ge(mm, i * 2 + s + 3)
                act.wait_ge(stored[s], (i + 1) * 16)
                nc.scalar.copy(groups(cols[:, s]), PS[:, 3 * s:3 * s + G, 0:GN]).then_inc(kept, 1)
            with act.Fori(0, NB // 4) as i:
                keep(i, 0)
                keep(i, 1)
            with act.Fori(0, NB // 4) as i:
                for s in range(2):
                    act.wait_ge(mm, (i + NB // 4) * 2 + s + 3)
                    act.wait_ge(stored[s], (i + NB // 4 + 1) * 16)
                    act.wait_ge(kcopied, (i * 2 + s) * 2 + 2)
                    nc.scalar.copy(groups(cols[:, s]), PS[:, 3 * s:3 * s + G, 0:GN]).then_inc(kept, 1)

        @block.vector
        def _(dve):
            dve.sem_inc(kcopied, 4)
            with dve.Fori(0, NB // 4) as i:
                for s in range(2):
                    dve.wait_ge(kstored[s], (i * 32) + 16)
                    dve.wait_ge(turned, (i * 2 + s) * 2 + 1)
                    nc.vector.tensor_copy(krow[:, s, 0:4], PS[:, 6, :].rearrange("p (j c) -> p j c", j=4)).then_inc(kcopied, 1)
                    dve.wait_ge(turned, (i * 2 + s) * 2 + 2)
                    nc.vector.tensor_copy(krow[:, s, 4], PS[:, 7, 0:P]).then_inc(kcopied, 1)


def v_projection(e, hT):
    nc, d, PS = e.nc, e.d, e.PS
    wv = d["c_w_qkv"][0].rearrange("(k p) n -> p k n", p=P)
    cvp = d["c_v_p"].rearrange("n b r h c -> (n b r) (h c)")
    cvs = d["c_v_s"].rearrange("n b r h c -> (n b r) (h c)")
    with e.stage() as ctx:
        KQ = KT // 2
        raw = e.sb(ctx, "w_v_raw", [P, 2, 2, 512])
        w = e.sb(ctx, "w_v_split", [P, 2, 2, KT, 512], F32R)
        out = e.sb(ctx, "v_rows", [P, 2, 512])
        in0, in1, w_high, w_low, mm, copied, s0, s1 = e.sem(
            ctx, "wv_in0", "wv_in1", "w_high", "w_low", "v_mm", "v_copied", "v_out0", "v_out1")
        w_in, stored = [in0, in1], [s0, s1]
        block = ctx.enter_context(nc.Block())
        order = [(j, t) for j in range(2) for t in range(NT)]
        newest = [n for n, (j, t) in enumerate(order) if t >= NT - 5]

        def total(s, n):
            return sum(1 + (m in newest) for m in range(n) if m % 2 == s)

        @block.gpsimd
        def _(pool):
            def load(n):
                j, k = n // KQ, n % KQ * 2
                pool.dma_start(raw[:, n % 2], wv[:, k:k + 2, 2 * D + j * 512:2 * D + (j + 1) * 512]).then_inc(w_in[n % 2], 16)
            load(0)
            load(1)
            for n in range(2 * KQ):
                j, k = n // KQ, n % KQ * 2
                pool.wait_ge(w_in[n % 2], 16 * (n // 2 + 1))
                nc.gpsimd.tensor_copy(w[:, j, 0, k:k + 2], raw[:, n % 2]).then_inc(w_high, 1)
                pool.wait_ge(w_high, n + 1)
                nc.gpsimd.tensor_tensor(w[:, j, 1, k:k + 2], raw[:, n % 2], w[:, j, 0, k:k + 2],
                                        ALU.subtract).then_inc(w_low, 1)
                if n + 2 < 2 * KQ:
                    pool.wait_ge(w_low, n + 1)
                    load(n + 2)

        @block.sync
        def _(sp):
            for n, (j, t) in enumerate(order):
                c = slice(j * 512, (j + 1) * 512)
                sp.wait_ge(copied, n + 1)
                sp.dma_start(e.scr["v"][t * P:(t + 1) * P, c], out[:, n % 2]).then_inc(stored[n % 2], 16)
                if n in newest:
                    dst = cvs[:, c] if t == NT - 1 else cvp[(t - 4) * P:(t - 3) * P, c]
                    sp.dma_start(dst, out[:, n % 2]).then_inc(stored[n % 2], 16)
            for s in range(2):
                sp.wait_ge(stored[s], 16 * total(s, len(order)))

        @block.tensor
        def _(pe):
            for n, (j, t) in enumerate(order):
                if n >= 4:
                    pe.wait_ge(copied, n - 3)
                for k in range(KT):
                    if t == 0 and k % 2 == 0:
                        pe.wait_ge(w_low, j * KQ + k // 2 + 1)
                    m = rows_split(nc, PS[:, n % 4, :], hT, t, w[:, j], k, k == 0, k == KT - 1)
                m.then_inc(mm, 1)

        @block.scalar
        def _(act):
            for n in range(len(order)):
                if n >= 2:
                    act.wait_ge(stored[n % 2], 16 * total(n % 2, n))
                act.wait_ge(mm, n + 1)
                nc.scalar.copy(out[:, n % 2], PS[:, n % 4, :]).then_inc(copied, 1)


def bias_rows(e):
    nc, d = e.nc, e.d
    with e.stage() as ctx:
        ext = e.sb(ctx, "bias_ext", [CH, RL])
        b_in, b_ext, b_out = e.sem(ctx, "bias_in", "bias_extended", "bias_out")
        block = ctx.enter_context(nc.Block())

        @block.sync
        def _(sp):
            sp.dma_start(ext[:, 127:RL], d["bias_falling"][0]).then_inc(b_in, 16)
            sp.wait_ge(b_ext, 1)
            sp.dma_start(e.scr["bias"], ext[:]).then_inc(b_out, 16)
            sp.wait_ge(b_out, 16)
            windows = bass.AP(e.scr["bias"].tensor, 127, [[RL, CH], [-1, P], [1, 2 * P]])
            sp.dma_start(e.scr["near"], windows).then_inc(b_out, 16)
            sp.wait_ge(b_out, 32)

        @block.vector
        def _(dve):
            dve.wait_ge(b_in, 16)
            nc.vector.tensor_copy(ext[:, 0:127], ext[:, 127:128].broadcast_to((CH, 127))).then_inc(b_ext, 1)


def attention(e, oT):
    nc, d, PS, ident, c = e.nc, e.d, e.PS, e.ident, e.const
    KW = 5 * P
    NPAIR = CH // 2
    NK = PAST // P
    NS = P + LS
    SCALE = float(HD) ** -0.5
    ck = d["cache_c_k"][0].rearrange("b r h c -> b r (h c)")
    cv = d["cache_c_v"][0].rearrange("b r h c -> b r (h c)")
    with e.stage() as ctx:
        qh = e.sb(ctx, "q_pair", [P, 2, T])
        kh = e.sb(ctx, "k_pair", [P, 2, T])
        vh = e.sb(ctx, "v_pair", [P, 2, NT, P])
        qs = e.sb(ctx, "q_heads_scaled", [P, 2, T])
        qbd = e.sb(ctx, "q_streams", [P, BS, 2, LS])
        bias = e.sb(ctx, "bias_pair", [P, 2, 2, KW])
        near = e.sb(ctx, "bias_near", [P, 2, NS])
        biass = e.sb(ctx, "bias_samples", [P, 2, KW])
        sc = e.sb(ctx, "minus_scores", [P, 2, KW])
        pr = e.sb(ctx, "probs", [P, 2, KW])
        prt = e.sb(ctx, "probsT", [P, 2, KW])
        mn = e.sb(ctx, "minus_max", [P, 2, 1])
        sm = e.sb(ctx, "prob_sum", [P, 2, 1])
        rs = e.sb(ctx, "prob_sum_inv", [P, 2, 1])
        kc = e.sb(ctx, "cache_k", [P, 2, NK, P])
        vc = e.sb(ctx, "cache_v", [P, 2, BS, NK, P])
        kct = e.sb(ctx, "cache_kT", [P, 2, PAST])
        NU = 2 * NPT
        N = NU + 2

        def count(name, per=1):
            return Count(e.sem(ctx, name), per)
        in0, in1, v0, v1, k0, k1 = e.sem(ctx, "pair_in0", "pair_in1", "cache_v_in0", "cache_v_in1", "cache_k_in0", "cache_k_in1")
        pair_in, vc_in, kc_in = [in0, in1], [v0, v1], [k0, k1]
        NIN = 5 + 2 * 4
        zeroed = e.sem(ctx, "queries_zeroed")
        q_scaled, qbd_ready, bias_ready, biass_ready = count("q_scaled", 2), count("qbd_ready"), count("bias_ready"), count("bias_s_ready")
        s_mm, s_red, p_exp, r_inv = count("score_mm", NU), count("score_max", N), count("prob_exp", N), count("sum_inverse", N)
        p_turned, p_kept = count("probs_turned", N), count("probsT_kept", N)
        o_mm, o_kept, p_norm = count("o_mm", NU), count("o_kept", 2), count("probs_normed", N)
        kc_turned, kc_kept, kc_used = count("cache_turned", BS), count("cache_kT_kept", BS), count("cache_kT_used", BS)
        so_mm = count("sample_o_mm")
        pair_end = {k: e.sem(ctx, f"pair_end_{k}") for k in ("pe", "act", "dve")}
        block = ctx.enter_context(nc.Block())

        def each(eng, pair):
            with eng.Fori(0, NPAIR // 2) as i:
                pair(i, 0)
                pair(i, 1)

        def each_ahead(eng, pair):
            last = NPAIR // 2 - 1
            with eng.Fori(0, last) as i:
                pair(i, 0, (i, 1))
                pair(i, 1, (i + 1, 0))
            pair(last, 0, (last, 1))
            pair(last, 1, None)

        def start(eng, i, me):
            for k, s in pair_end.items():
                if k != me:
                    eng.wait_ge(s, i + 2)

        def width(u):
            return min(u // 2 + 1, 5) * P

        @block.sync
        def _(sp):
            def pair(i2, s):
                i = i2 * 2 + s
                for x in pair_end.values():
                    sp.wait_ge(x, i + 1)
                put = lambda dst, src: sp.dma_start(dst, src).then_inc(pair_in[s], 16)
                put(qh[:, s], e.scr["qk"][ds(i, 1)].rearrange("o p t -> p (o t)"))
                put(kh[:, s], e.scr["qk"][ds(i + NPAIR, 1)].rearrange("o p t -> p (o t)"))
                for hp in range(2):
                    row = e.scr["near"][ds(i * 2 + hp, 1)].rearrange("o r j -> (o r) j")
                    put(bias[:, s, hp, 3 * P:5 * P], row)
                    for b in range(4):
                        r = 2 * LS * b + LS * hp
                        put(near[r:r + LS, s], row[0:LS, 0:NS])
                put(vh[:, s], e.scr["v"].rearrange("(t p) c -> p t c", p=P)[:, :, ds(i * P, P)])
            each(sp, pair)

        @block.gpsimd
        def _(pool):
            def pair(i2, s):
                i = i2 * 2 + s
                for x in pair_end.values():
                    pool.wait_ge(x, i + 1)
                e.apart(pool)
                for b in range(BS):
                    pool.dma_start(vc[:, s, b], cv[b].rearrange("(r p) c -> p r c", p=P)[:, :, ds(i * P, P)]
                                   ).then_inc(vc_in[s], 16)
                for b in range(BS):
                    pool.wait_ge(kc_turned.sem, i * BS + b + 1)
                    e.apart(pool)
                    pool.dma_start(kc[:, b % 2], ck[b].rearrange("(r p) c -> p r c", p=P)[:, :, ds(i * P, P)]
                                   ).then_inc(kc_in[b % 2], 16)
            each(pool, pair)

        @block.tensor
        def _(pe):
            pe.sem_inc(pair_end["pe"], 2)
            pe.sem_inc(kc_turned.sem, 2)
            mm = nc.tensor.matmul

            def pair(i2, s):
                i = i2 * 2 + s
                start(pe, i, "pe")

                def score(u):
                    t, hp, w = u // 2, u % 2, width(u)
                    if u > 1:
                        s_red.wait(pe, i, u - 1)
                    else:
                        q_scaled.wait(pe, i, u + 1)
                    k0 = (t + 1) * P - w
                    m = mm(PS[:, 2 * hp, 0:min(w, 512)], qs[:, hp, t * P:(t + 1) * P], kh[:, s, k0:k0 + min(w, 512)],
                           start=True, stop=True)
                    if w > 512:
                        m = mm(PS[:, 2 * hp + 1, 0:w - 512], qs[:, hp, t * P:(t + 1) * P], kh[:, s, k0 + 512:k0 + w],
                               start=True, stop=True)
                    m.then_inc(s_mm.sem, 1)

                def turn(u, w):
                    p_norm.wait(pe, i, u + 1)
                    if u:
                        p_kept.wait(pe, i, u)
                    for n in range(w // P):
                        m = pe.transpose(PS[:, 4 + n // 4, (n % 4) * P:(n % 4 + 1) * P], pr[:, u % 2, n * P:(n + 1) * P], ident)
                    m.then_inc(p_turned.sem, 1)

                def product_v(u):
                    t, hp, w = u // 2, u % 2, width(u)
                    p_kept.wait(pe, i, u + 1)
                    n = w // P
                    for j in range(n):
                        m = mm(PS[hp * HD:(hp + 1) * HD, 6 + t // 4, t % 4 * P:(t % 4 + 1) * P],
                               vh[:, s, t + 1 - n + j, hp * HD:(hp + 1) * HD], prt[:, u % 2, j * P:(j + 1) * P],
                               start=(j == 0), stop=(j == n - 1))
                    m.then_inc(o_mm.sem, 1)
                for u in range(NU + 2):
                    if u < NU:
                        score(u)
                    if 1 <= u <= NU:
                        turn(u - 1, width(u - 1))
                    if u >= 2:
                        product_v(u - 2)
                qbd_ready.wait(pe, i)
                for b in range(BS + 1):
                    if b < BS:
                        pe.wait_ge(kc_in[b % 2], (i * (BS // 2) + b // 2 + 1) * 16)
                        if b < 2:
                            o_kept.wait(pe, i, b + 1)
                        else:
                            kc_kept.wait(pe, i, b - 1)
                        for n in range(NK):
                            m = pe.transpose(PS[:, 6 + b % 2, n * P:(n + 1) * P], kc[:, b % 2, n], ident)
                        m.then_inc(kc_turned.sem, 1)
                    if b:
                        x = b - 1
                        g, rows = x // 4, slice(32 * (x % 4), 32 * (x % 4) + 32)
                        if x % 4 == 0:
                            s_red.wait(pe, i, NU - 1 + g)
                        kc_kept.wait(pe, i, x + 1)
                        w = qbd[:, x].rearrange("p h q -> p (h q)")
                        mm(PS[rows, 2 * g, :], w, kct[:, x % 2], start=True, stop=True)
                        m = mm(PS[rows, 2 * g + 1, 0:P], w, kh[:, s, LP:T], start=True, stop=True)
                        m.then_inc(kc_used.sem, 1)
                pe.wait_ge(vc_in[s], (i2 + 1) * (16 * BS))
                kc_kept.wait(pe, i)
                for g in range(2):
                    turn(NU + g, KW)
                    p_kept.wait(pe, i, NU + g + 1)
                    for x in range(4):
                        b = 4 * g + x
                        for n in range(NK + 1):
                            w = vc[:, s, b, n] if n < NK else vh[:, s, NT - 1]
                            m = mm(PS[:, 6, 32 * b:32 * b + 32], w, prt[:, g, n * P + 32 * x:n * P + 32 * x + 32],
                                   start=(n == 0), stop=(n == NK))
                m.then_inc(so_mm.sem, 1)
                so_mm.wait(pe, i)
                pe.sem_inc(pair_end["pe"], 1)
            each(pe, pair)

        @block.scalar
        def _(act):
            act.sem_inc(pair_end["act"], 2)
            act.wait_ge(zeroed, 1)

            def scale(i2, s):
                act.wait_ge(pair_in[s], (i2 + 1) * (16 * NIN))
                for hp in range(2):
                    r = slice(hp * HD, hp * HD + HD)
                    nc.scalar.activation(qs[r, hp], qh[r, s], ACT.Copy, scale=SCALE).then_inc(q_scaled.sem, 1)

            def pair(i2, s, ahead):
                i = i2 * 2 + s
                start(act, i, "act")

                def exp(u, w):
                    s_red.wait(act, i, u + 1)
                    if u > 1:
                        r_inv.wait(act, i, u - 1)
                        p_turned.wait(act, i, u - 1)
                    nc.scalar.activation(pr[:, u % 2, 0:w], sc[:, u % 2, 0:w], ACT.Exp, scale=-1.0, bias=mn[:, u % 2, 0:1],
                                         accum_out=sm[:, u % 2, 0:1]).then_inc(p_exp.sem, 1)

                def keep(u, w):
                    p_turned.wait(act, i, u + 1)
                    if 1 < u < NU:
                        o_mm.wait(act, i, u - 1)
                    nc.scalar.copy(prt[:, u % 2, 0:w], PS[:, 4:6, :].rearrange("p b n -> p (b n)")[:, 0:w]).then_inc(p_kept.sem, 1)

                def keep_o(h):
                    o_mm.wait(act, i, 8 * h + 8)
                    nc.scalar.copy(oT[:, ds(i, 1), h * 512:(h + 1) * 512].rearrange("p o t -> p (o t)"),
                                   PS[:, 6 + h, :]).then_inc(o_kept.sem, 1)
                for u in range(NU + 1):
                    if u < NU:
                        exp(u, width(u))
                    if u:
                        keep(u - 1, width(u - 1))
                    if u == 11:
                        keep_o(0)
                keep_o(1)
                for b in range(BS):
                    kc_turned.wait(act, i, b + 3)
                    if b > 1:
                        kc_used.wait(act, i, b - 1)
                    nc.scalar.copy(kct[:, b % 2], PS[:, 6 + b % 2, :]).then_inc(kc_kept.sem, 1)
                    if b == 5:
                        exp(NU, KW)
                exp(NU + 1, KW)
                if ahead:
                    s_mm.wait(act, i)
                    qbd_ready.wait(act, i)
                    scale(*ahead)
                o_mm.wait(act, i)
                keep(NU, KW)
                keep(NU + 1, KW)
                p_kept.wait(act, i)
                act.sem_inc(pair_end["act"], 1)
            scale(0, 0)
            each_ahead(act, pair)

        @block.vector
        def _(dve):
            v = nc.vector
            v.memset(qbd[:], 0.0)
            v.memset(qs[:], 0.0).then_inc(zeroed, 1)
            dve.wait_ge(zeroed, 1)
            dve.sem_inc(pair_end["dve"], 2)

            def prepare(i2, s):
                i = i2 * 2 + s
                dve.wait_ge(pair_in[s], (i2 + 1) * (16 * NIN))
                for hp in range(2):
                    far = bias[:, s, hp, 3 * P:3 * P + 1]
                    v.tensor_scalar(bias[:, s, hp, 0:P], c("far_mask"), far, None, ALU.add)
                    v.tensor_copy(bias[:, s, hp, P:3 * P], far.broadcast_to((P, 2 * P)))
                    m = v.tensor_tensor(bias[:, s, hp, 4 * P:], bias[:, s, hp, 4 * P:], c("own_mask"), ALU.add)
                m.then_inc(bias_ready.sem, 1)
                for g in range(2):
                    v.tensor_copy(biass[:, g, 0:3 * P], near[:, s, 0:1].broadcast_to((P, 3 * P)))
                    v.tensor_copy(biass[:, g, 3 * P:4 * P], near[:, s, 0:P])
                    m = v.tensor_tensor(biass[:, g, 4 * P:].rearrange("p (b q) -> p b q", b=BS),
                                        c("new_mask")[:, g * P:(g + 1) * P].rearrange("p (b q) -> p b q", b=BS),
                                        bc(near[:, s, P:NS].rearrange("p (o q) -> p o q", o=1), (P, BS, LS)), ALU.add)
                m.then_inc(biass_ready.sem, 1)
                bias_ready.wait(dve, i)
                biass_ready.wait(dve, i)

            def pair(i2, s, ahead):
                i = i2 * 2 + s
                start(dve, i, "dve")
                q_scaled.wait(dve, i)
                for hp in range(2):
                    r = slice(hp * HD, hp * HD + HD)
                    m = v.tensor_copy(qbd[r, :, hp], qs[r, hp, LP:T].rearrange("p (b q) -> p b q", b=BS))
                m.then_inc(qbd_ready.sem, 1)

                def reduce(u, w, b):
                    s_mm.wait(dve, i, u + 1) if u < NU else kc_used.wait(dve, i, 4 * (u - NU) + 4)
                    if u > 1:
                        p_exp.wait(dve, i, u - 1)
                    e.apart(dve)
                    p = PS[:, 2 * (u % 2):2 * (u % 2) + 2, :].rearrange("p b n -> p (b n)")[:, 0:w]
                    v.tensor_tensor_reduce(sc[:, u % 2, 0:w], p, b, -1.0, -NEG, ALU.add, ALU.min, mn[:, u % 2, 0:1]
                                           ).then_inc(s_red.sem, 1)

                def normalise(u, w):
                    p_exp.wait(dve, i, u + 1)
                    v.reciprocal(rs[:, u % 2], sm[:, u % 2]).then_inc(r_inv.sem, 1)
                    r_inv.wait(dve, i, u + 1)
                    v.tensor_scalar(pr[:, u % 2, 0:w], pr[:, u % 2, 0:w], rs[:, u % 2, 0:1], None, ALU.mult
                                    ).then_inc(p_norm.sem, 1)
                for u in range(NU):
                    reduce(u, width(u), bias[:, s, u % 2, KW - width(u):])
                    normalise(u, width(u))
                for g in range(2):
                    reduce(NU + g, KW, biass[:, g])
                    normalise(NU + g, KW)
                if ahead:
                    prepare(*ahead)
                so_mm.wait(dve, i)
                for hp in range(2):
                    r = slice(hp * HD, hp * HD + HD)
                    m = v.tensor_copy(oT[r, ds(i, 1), LP:T].rearrange("p o (b q) -> p (o b) q", b=BS),
                                      PS[r, 6, 0:BS * 2 * LS].rearrange("p (b h q) -> p b h q", b=BS, h=2)[:, :, hp])
                m.then_inc(pair_end["dve"], 1)
            prepare(0, 0)
            each_ahead(dve, pair)



NAMES = ['x_prompt', 'x_sample', 'state_dn_conv', 'state_dn', 'state_gla', 'cache_c_k', 'cache_c_v', 'ab_norm', 'ab_w_in',
         'dn_conv_w', 'dn_a_log', 'dn_dt_bias', 'dn_out_norm', 'gla_gk_w2', 'gla_gk_b', 'gla_out_norm', 'ab_w_out',
         'c_norm', 'c_w_qkv', 'bias_falling', 'c_w_out', 'ffn_norm', 'ffn_w_gu', 'ffn_w_down', 'final_norm',
         'const_f', 'const_u']
OUTS = [("y_prompt", (1, LP, D)), ("y_sample", (BS, LS, D)), ("conv_p", (1, 1, 3, QKV)), ("conv_s", (1, BS, 3, QKV)),
        ("dn_p", (1, 1, H, DK, DK)), ("dn_s", (1, BS, H, DK, DK)), ("gla_p", (1, 1, H, GK, DK)),
        ("gla_s", (1, BS, H, GK, DK)), ("c_k_p", (1, 1, PAST, CH, HD)), ("c_k_s", (1, BS, LS, CH, HD)),
        ("c_v_p", (1, 1, PAST, CH, HD)), ("c_v_s", (1, BS, LS, CH, HD))]


def build_program(nc, d, where, widths):
    e = Env(nc, d)
    with e.top as top:
        for name, shape in (("xT", [D, T]), ("qkv", [T, QKV]), ("rest", [T, 4, H * DK]), ("qk", [2 * KT, P, T]),
                            ("v", [T, D]), ("bias", [CH, RL]), ("near", [CH, P, 2 * P])):
            e.dram(name, shape)
        e.PS = top.enter_context(nc.psum_tensor("PS", [P, 8, 512], F32))
        e.cf = e.sb(top, "consts_f", [P, widths[0]])
        e.cu = e.sb(top, "consts_u", [P, widths[1]], U8)
        e.const = lambda k: (e.cu if k in ("up", "low") else e.cf)[:, where[k][0]:where[k][1]]
        e.ident, e.ones = e.const("ident"), e.const("ones")
        e.gain_of = {"ab": d["ab_norm"][0], "ffn0": d["ffn_norm"][0], "c": d["c_norm"][0], "ffn1": d["ffn_norm"][1],
                     "final": d["final_norm"]}
        e.gains = e.sb(top, "gains", [P, len(e.gain_of) * KT])
        e.passed = e.sem(top, "waits_passed")
        with ExitStack() as mixer:
            e.rn = e.sb(mixer, "qk_norms", [P, NT, 2 * H])
            e.beta = e.sb(mixer, "beta", [P, NT, H])
            e.rkb = e.sb(mixer, "k_norm_beta", [P, NT, H])
            e.gdn = e.sb(mixer, "dn_log_decay", [P, NT, H])
            e.ggla = e.sb(mixer, "gla_log_decay", [P, NT, H * GK])
            with ExitStack() as ctx:
                e.ss = e.sb(ctx, "head_ss", [P, NT, 3 * H])
                e.misc = e.sb(ctx, "misc", [NMISC, T])
                with ExitStack() as inner:
                    hT = e.split(inner, "hT")
                    with ExitStack() as first:
                        e.xT = e.sb(first, "xT", [P, KT, T])
                        load_x(e)
                        rmsnorm(e, "ab", hT)
                    conv_projection(e, hT)
                    rest_projection(e, hT)
                token_scalars(e)
            with ExitStack() as ctx:
                e.o_all = e.sb(ctx, "o_all", [P, NT, 2 * H * DK])
                recurrences(e)
                with ExitStack() as inner:
                    oT = e.split(inner, "mixer_oT")
                    gate_outputs(e, oT)
                    e.xT = e.sb(inner, "xT", [P, KT, T])
                    reload_x(e)
                    project_add(e, d["ab_w_out"][0], None, oT)
                    save_x(e)
        e.xT = e.sb(top, "xT", [P, KT, T])
        reload_x(e)
        with ExitStack() as ctx:
            hT = e.split(ctx, "hT")
            rmsnorm(e, "ffn0", hT)
            ffn(e, d["ffn_w_gu"][0], d["ffn_w_down"][0], hT)
            rmsnorm(e, "c", hT)
            qkv_projection(e, hT)
            v_projection(e, hT)
        bias_rows(e)
        with ExitStack() as ctx:
            oT = e.sb(ctx, "attention_oT", [P, KT, T])
            attention(e, oT)
            project_add(e, d["c_w_out"][0], oT, e.split(ctx, "oT_parts"))
        with ExitStack() as ctx:
            hT = e.split(ctx, "hT")
            rmsnorm(e, "ffn1", hT)
            ffn(e, d["ffn_w_gu"][1], d["ffn_w_down"][1], hT)
        yT = e.sb(top, "yT", [P, KT, T])
        rmsnorm(e, "final", yT)
        write_y(e, yT)


def kernel(**inputs):
    import numpy as _np
    import concourse.bacc as _bacc
    from concourse import mybir as _mybir
    from concourse.bass_utils import run_bass_kernel_spmd as _run

    nc = _bacc.Bacc("TRN2", target_bir_lowering=False, num_devices=1)
    const_f, const_u, where = shape_constants()
    inputs["const_f"], inputs["const_u"] = const_f, const_u
    inputs["bias_falling"] = _np.ascontiguousarray(_np.asarray(inputs["c_rel_bias"])[:, :, ::-1])
    arrays, d = {}, {}
    for name in NAMES:
        a = _np.ascontiguousarray(inputs[name])
        arrays[f"in_{name}_dram"] = a
        d[name] = nc.dram_tensor(f"in_{name}_dram", a.shape, _mybir.dt.from_np(a.dtype), kind="ExternalInput").ap()
    for i, (name, shape) in enumerate(OUTS):
        d[name] = nc.dram_tensor(f"out_{i}_dram", shape, F32, kind="ExternalOutput").ap()
    build_program(nc, d, where, (const_f.shape[1], const_u.shape[1]))
    r = _run(nc, [arrays], core_ids=[0])
    return tuple(r.results[0][f"out_{i}_dram"] for i in range(len(OUTS)))
```
